# Optimizing a Trainium2 kernel written in Bass

```python
import math
import jax
import jax.numpy as jnp
from jax import lax
import numpy as np

D_MODEL = 1024
BATCH = 1
SEQ = 256
DEPTH = 1

HEAD_DIM = 64
MOBA_HEADS = 6
RWKV_HEADS = 6
MEM_HEADS = 4
MOBA_W = MOBA_HEADS * HEAD_DIM
RWKV_W = RWKV_HEADS * HEAD_DIM
MEM_W = MEM_HEADS * HEAD_DIM
MIX_W = MOBA_W + RWKV_W + MEM_W
MOBA_BLOCK = 256
MOBA_TOPK = 3
MOBA_QCHUNK = 64
N_BUCKETS = 32
MAX_DISTANCE = 128
DECAY_LORA = 64
AAA_LORA = 64
GATE_LORA = 128
RWKV_COLS = 3 * RWKV_W + DECAY_LORA + AAA_LORA + GATE_LORA
RWKV_GN_EPS = 64e-5
N_MEM = 256
IN_COLS = 3 * MOBA_W + RWKV_COLS + MEM_W
N_EXPERTS = 32
TOP_K = 4
D_EXPERT = D_MODEL
SWIGLU_ALPHA = 1.702
SWIGLU_LIMIT = 7.0
MOE_BLOCK = 128
RMS_EPS = 1e-5

kernel_name = 'hymba_moba_rwkv7_memxattn_moe'

def rmsnorm(x, g):
    xf = x.astype(jnp.float32)
    y = xf * lax.rsqrt(jnp.mean(xf * xf, axis=-1, keepdims=True) + RMS_EPS)
    return (y * g.astype(jnp.float32)).astype(x.dtype)

def t5_bucket(dist):
    n = jnp.maximum(dist, 0)
    max_exact = N_BUCKETS // 2
    nf = jnp.maximum(n, 1).astype(jnp.float32)
    large = max_exact + (jnp.log(nf / max_exact) / math.log(MAX_DISTANCE / max_exact)
                         * (N_BUCKETS - max_exact)).astype(jnp.int32)
    large = jnp.minimum(large, N_BUCKETS - 1)
    return jnp.where(n < max_exact, n, large)

def moba_attention(q, k, v, rel_bias):
    B, S, H, dh = q.shape
    nb = -(-S // MOBA_BLOCK)
    topk = min(MOBA_TOPK, nb)
    nc = S // MOBA_QCHUNK
    scale = dh ** -0.5

    def blocks(t):
        t = jnp.pad(t, ((0, 0), (0, nb * MOBA_BLOCK - S), (0, 0), (0, 0)))
        return t.transpose(0, 2, 1, 3).reshape(B, H, nb, MOBA_BLOCK, dh)

    kb, vb = blocks(k), blocks(v)
    qh = q.transpose(0, 2, 1, 3)
    k_mean = jnp.mean(kb, axis=3)
    q_blk = jnp.arange(S) // MOBA_BLOCK
    past = jnp.arange(nb)[None, :] < q_blk[:, None]
    gate = jnp.einsum('bhsd,bhnd->bhsn', qh, k_mean).astype(jnp.float32)
    gate = jnp.where(past, gate, -jnp.inf)
    _, sel = lax.top_k(gate, topk)
    valid = sel < q_blk[:, None]
    bias_h = rel_bias.astype(jnp.float32).T
    b_idx = jnp.arange(B)[:, None, None, None]
    h_idx = jnp.arange(H)[None, :, None, None]
    offs = jnp.arange(MOBA_BLOCK)

    def chunks(t):
        t = t.reshape(t.shape[:2] + (nc, MOBA_QCHUNK) + t.shape[3:])
        return jnp.moveaxis(t, 2, 0)

    def attend_chunk(args):
        qc, selc, validc, ci = args
        q_pos = ci * MOBA_QCHUNK + jnp.arange(MOBA_QCHUNK)
        own = (ci * MOBA_QCHUNK) // MOBA_BLOCK
        kg = kb[b_idx, h_idx, selc]
        vg = vb[b_idx, h_idx, selc]
        kpos_g = selc[..., None] * MOBA_BLOCK + offs
        bias_g = bias_h[h_idx[..., None], t5_bucket(q_pos[:, None, None] - kpos_g)]
        s_g = jnp.einsum('bhqd,bhqkjd->bhqkj', qc, kg).astype(jnp.float32) * scale + bias_g
        s_g = jnp.where(validc[..., None], s_g, -jnp.inf)
        k_own = lax.dynamic_index_in_dim(kb, own, axis=2, keepdims=False)
        v_own = lax.dynamic_index_in_dim(vb, own, axis=2, keepdims=False)
        kpos_own = own * MOBA_BLOCK + offs
        bias_own = bias_h[:, t5_bucket(q_pos[:, None] - kpos_own[None, :])]
        s_own = jnp.einsum('bhqd,bhjd->bhqj', qc, k_own).astype(jnp.float32) * scale + bias_own
        s_own = jnp.where(kpos_own[None, :] <= q_pos[:, None], s_own, -jnp.inf)
        logits = jnp.concatenate([s_g.reshape(B, H, MOBA_QCHUNK, topk * MOBA_BLOCK), s_own], axis=-1)
        p = jax.nn.softmax(logits, axis=-1).astype(vb.dtype)
        p_g = p[..., :topk * MOBA_BLOCK].reshape(B, H, MOBA_QCHUNK, topk, MOBA_BLOCK)
        p_own = p[..., topk * MOBA_BLOCK:]
        return (jnp.einsum('bhqkj,bhqkjd->bhqd', p_g, vg)
                + jnp.einsum('bhqj,bhjd->bhqd', p_own, v_own))

    out = lax.map(attend_chunk, (chunks(qh), chunks(sel), chunks(valid), jnp.arange(nc)))
    out = jnp.moveaxis(out, 0, 2).reshape(B, H, S, dh)
    return out.transpose(0, 2, 1, 3).reshape(B, S, H * dh)

def token_shift(p):
    return jnp.pad(p, ((0, 0), (1, 0), (0, 0)))[:, :-1]

def rwkv7_time_mix(p, mu, w0, w_up, a0, a_up, g_up, k_k, k_a, r_k, gn_g, gn_b):
    B, S, _ = p.shape
    H, N = RWKV_HEADS, HEAD_DIM
    f32 = jnp.float32
    p = p + (token_shift(p) - p) * mu
    r, k, v, xw, xa, xg = jnp.split(
        p, [RWKV_W, 2 * RWKV_W, 3 * RWKV_W, 3 * RWKV_W + DECAY_LORA,
            3 * RWKV_W + DECAY_LORA + AAA_LORA], axis=-1)
    w = -jax.nn.softplus(-(w0 + jnp.tanh(xw) @ w_up)) - 0.5
    decay = jnp.exp(-jnp.exp(w.astype(f32)))
    a = jax.nn.sigmoid(a0 + xa @ a_up)
    g = jax.nn.sigmoid(xg) @ g_up
    heads = lambda t: t.astype(f32).reshape(B, S, H, N)
    kk = heads(k * k_k)
    kk = kk / jnp.maximum(jnp.sqrt(jnp.sum(kk * kk, axis=-1, keepdims=True)), 1e-12)
    k = k * (1.0 + (a - 1.0) * k_a)
    r, k, v, decay, a = heads(r), heads(k), heads(v), heads(decay), heads(a)

    def step(state, inp):
        r_t, w_t, k_t, v_t, a_t, b_t = inp
        sa = jnp.einsum('bhij,bhj->bhi', state, a_t)
        state = (state * w_t[:, :, None, :] + sa[..., None] * b_t[:, :, None, :]
                 + v_t[..., None] * k_t[:, :, None, :])
        return state, jnp.einsum('bhij,bhj->bhi', state, r_t)

    seq_first = lambda t: jnp.moveaxis(t, 1, 0)
    xs = tuple(seq_first(t) for t in (r, decay, k, v, -kk, kk * a))
    _, o = lax.scan(step, jnp.zeros((B, H, N, N), f32), xs)
    o = seq_first(o)
    mean = jnp.mean(o, axis=-1, keepdims=True)
    var = jnp.mean(jnp.square(o - mean), axis=-1, keepdims=True)
    o = (o - mean) * lax.rsqrt(var + RWKV_GN_EPS)
    o = o.reshape(B, S, H * N) * gn_g.astype(f32) + gn_b.astype(f32)
    o = o + (jnp.sum(r * k * r_k.astype(f32), axis=-1, keepdims=True) * v).reshape(B, S, H * N)
    return (o * g.astype(f32)).astype(p.dtype)

def memory_attention(q, mk, mv):
    scale = q.shape[-1] ** -0.5
    s = jnp.einsum('bshd,bmhd->bhsm', q, mk).astype(jnp.float32) * scale
    p = jax.nn.softmax(s, axis=-1).astype(mv.dtype)
    o = jnp.einsum('bhsm,bmhd->bshd', p, mv)
    return o.reshape(q.shape[0], q.shape[1], -1)

def moe_ffn(h, w_router, b_router, w_gate_up, b_gate_up, w_down, b_down):
    B, S, D = h.shape
    T = B * S
    A = T * TOP_K
    xt = h.reshape(T, D)
    logits = (xt @ w_router + b_router).astype(jnp.float32)
    top_val, top_idx = lax.top_k(logits, TOP_K)
    top_w = jax.nn.softmax(top_val, axis=-1)
    e_flat = top_idx.reshape(A).astype(jnp.int32)
    tok_flat = jnp.arange(A, dtype=jnp.int32) // TOP_K
    w_flat = top_w.reshape(A)
    e_sorted, order = lax.sort((e_flat, jnp.arange(A, dtype=jnp.int32)), num_keys=1, is_stable=True)
    counts = jnp.bincount(e_flat, length=N_EXPERTS)
    starts = jnp.cumsum(counts) - counts
    padded = (counts + MOE_BLOCK - 1) // MOE_BLOCK * MOE_BLOCK
    pad_ends = jnp.cumsum(padded)
    pad_starts = pad_ends - padded
    dest = pad_starts[e_sorted] + (jnp.arange(A, dtype=jnp.int32) - starts[e_sorted])
    n_blocks = -(-A // MOE_BLOCK) + N_EXPERTS
    P = n_blocks * MOE_BLOCK
    row_tok = jnp.zeros((P,), jnp.int32).at[dest].set(tok_flat[order])
    row_w = jnp.zeros((P,), jnp.float32).at[dest].set(w_flat[order])
    blk_start = jnp.arange(n_blocks, dtype=jnp.int32) * MOE_BLOCK
    blk_expert = jnp.minimum(jnp.searchsorted(pad_ends, blk_start, side='right'), N_EXPERTS - 1)
    xs = xt[row_tok].reshape(n_blocks, MOE_BLOCK, D)

    def expert_block(args):
        xb, e = args
        gu = xb @ w_gate_up[e] + b_gate_up[e]
        gate, up = gu[:, ::2], gu[:, 1::2]
        gate = jnp.minimum(gate, SWIGLU_LIMIT)
        up = jnp.clip(up, -SWIGLU_LIMIT, SWIGLU_LIMIT)
        glu = gate * jax.nn.sigmoid(gate * SWIGLU_ALPHA)
        return ((up + 1.0) * glu) @ w_down[e] + b_down[e]

    ys = lax.map(expert_block, (xs, blk_expert)).reshape(P, D)
    out = jax.ops.segment_sum(ys * row_w[:, None].astype(ys.dtype), row_tok, num_segments=T)
    return out.reshape(B, S, D)

def setup_inputs(seed: int = 0) -> dict:
    key = jax.random.key(seed)
    ks = jax.random.split(key, 32)
    f32 = jnp.float32
    L = DEPTH

    def nrm(k, shape, s):
        return jax.random.normal(k, shape, f32) * s

    return {
        'x': nrm(ks[0], (BATCH, SEQ, D_MODEL), 1.0),
        'mem': nrm(ks[1], (BATCH, N_MEM, D_MODEL), 1.0),
        'w_in': nrm(ks[2], (L, D_MODEL, IN_COLS), D_MODEL ** -0.5),
        'w_out': nrm(ks[3], (L, MIX_W, D_MODEL), MIX_W ** -0.5),
        'w_mem_kv': nrm(ks[4], (L, D_MODEL, 2 * MEM_W), D_MODEL ** -0.5),
        'g_mix': 1.0 + nrm(ks[5], (L, D_MODEL), 0.02),
        'g_mem': 1.0 + nrm(ks[6], (L, D_MODEL), 0.02),
        'g_ffn': 1.0 + nrm(ks[7], (L, D_MODEL), 0.02),
        'g_final': 1.0 + nrm(ks[8], (D_MODEL,), 0.02),
        'rel_bias': nrm(ks[9], (N_BUCKETS, MOBA_HEADS), 0.3),
        'rwkv_mu': jax.random.uniform(ks[10], (L, RWKV_COLS), f32),
        'rwkv_w0': jax.random.uniform(ks[11], (L, RWKV_W), f32, -6.0, 0.0),
        'rwkv_w_up': nrm(ks[12], (L, DECAY_LORA, RWKV_W), 0.1 * DECAY_LORA ** -0.5),
        'rwkv_a0': nrm(ks[13], (L, RWKV_W), 0.1),
        'rwkv_a_up': nrm(ks[14], (L, AAA_LORA, RWKV_W), 0.5 * AAA_LORA ** -0.5),
        'rwkv_g_up': nrm(ks[15], (L, GATE_LORA, RWKV_W), GATE_LORA ** -0.5),
        'rwkv_k_k': 0.85 + nrm(ks[16], (L, RWKV_W), 0.02),
        'rwkv_k_a': 1.0 + nrm(ks[17], (L, RWKV_W), 0.02),
        'rwkv_r_k': nrm(ks[18], (L, RWKV_HEADS, HEAD_DIM), 0.1),
        'rwkv_gn_g': 1.0 + nrm(ks[19], (L, RWKV_W), 0.02),
        'rwkv_gn_b': nrm(ks[20], (L, RWKV_W), 0.02),
        'w_router': nrm(ks[21], (L, D_MODEL, N_EXPERTS), D_MODEL ** -0.5),
        'b_router': nrm(ks[22], (L, N_EXPERTS), 0.01),
        'w_gate_up': nrm(ks[23], (L, N_EXPERTS, D_MODEL, 2 * D_EXPERT), D_MODEL ** -0.5),
        'b_gate_up': nrm(ks[24], (L, N_EXPERTS, 2 * D_EXPERT), 0.01),
        'w_down': nrm(ks[25], (L, N_EXPERTS, D_EXPERT, D_MODEL), D_EXPERT ** -0.5),
        'b_down': nrm(ks[26], (L, N_EXPERTS, D_MODEL), 0.01),
    }

def reference(x, mem, w_in, w_out, w_mem_kv, g_mix, g_mem, g_ffn, g_final, rel_bias,
              rwkv_mu, rwkv_w0, rwkv_w_up, rwkv_a0, rwkv_a_up, rwkv_g_up, rwkv_k_k, rwkv_k_a,
              rwkv_r_k, rwkv_gn_g, rwkv_gn_b, w_router, b_router, w_gate_up, b_gate_up,
              w_down, b_down):
    B, S, _ = x.shape
    M = mem.shape[1]
    for l in range(DEPTH):
        h = rmsnorm(x, g_mix[l])
        p = h @ w_in[l]
        pq, pk, pv, p_rwkv, p_mq = jnp.split(
            p, [MOBA_W, 2 * MOBA_W, 3 * MOBA_W, 3 * MOBA_W + RWKV_COLS], axis=-1)
        y_moba = moba_attention(pq.reshape(B, S, MOBA_HEADS, HEAD_DIM),
                                pk.reshape(B, S, MOBA_HEADS, HEAD_DIM),
                                pv.reshape(B, S, MOBA_HEADS, HEAD_DIM), rel_bias)
        y_rwkv = rwkv7_time_mix(p_rwkv, rwkv_mu[l], rwkv_w0[l], rwkv_w_up[l], rwkv_a0[l],
                                rwkv_a_up[l], rwkv_g_up[l], rwkv_k_k[l], rwkv_k_a[l],
                                rwkv_r_k[l], rwkv_gn_g[l], rwkv_gn_b[l])
        mkv = rmsnorm(mem, g_mem[l]) @ w_mem_kv[l]
        mk, mv = jnp.split(mkv, 2, axis=-1)
        y_mem = memory_attention(p_mq.reshape(B, S, MEM_HEADS, HEAD_DIM),
                                 mk.reshape(B, M, MEM_HEADS, HEAD_DIM),
                                 mv.reshape(B, M, MEM_HEADS, HEAD_DIM))
        x = x + jnp.concatenate([y_moba, y_rwkv, y_mem], axis=-1) @ w_out[l]
        x = x + moe_ffn(rmsnorm(x, g_ffn[l]), w_router[l], b_router[l], w_gate_up[l],
                        b_gate_up[l], w_down[l], b_down[l])
    return rmsnorm(x, g_final)


_drawn_inputs = setup_inputs


def setup_inputs(seed=0):
    import zlib

    import numpy as np

    out = dict(_drawn_inputs(seed))
    spreads = {}
    factors = {'g_mem': 3.8,
     'g_final': 8.995,
     'rwkv_w_up': 8.0,
     'rwkv_k_k': 15.755,
     'rwkv_k_a': 3.033,
     'b_gate_up': 8.0,
     'b_down': 8.0,
     'rwkv_gn_g': 3.403,
     'rwkv_gn_b': 3.609,
     'b_router': 3.831}
    for name, (base, spread) in spreads.items():
        noise = np.random.default_rng([zlib.crc32(name.encode()), seed]).standard_normal(out[name].shape)
        drawn = base * np.exp(spread * noise) if base else spread * noise
        out[name] = jnp.asarray(drawn.astype(out[name].dtype))
    for name, factor in factors.items():
        out[name] = (out[name] * factor).astype(out[name].dtype)
    return out
```

```python
from contextlib import ExitStack

import concourse.bass as bass
from concourse import mybir

P = 128
T = 256
D = 1024
KT = D // P
TT = T // P
HD = 64
NMOBA, NRWKV, NMEM = 6, 6, 4
NCT = 3
E = 32
TOPK = 4
CAP = 64
CH = 128
NM = NRWKV * T // CH
SLOT = 2048
NSLOT = 12
NG = 11
EPS = 1e-5
GN_EPS = 64e-5
DECAY = 0.6065306597126334
ALPHA, LIMIT = 1.702, 7.0
NEG = -1.0e30
NO_SLOT = 4096.0

F32 = mybir.dt.float32
I32 = mybir.dt.int32
U32 = mybir.dt.uint32
ALU = mybir.AluOpType
ACT = mybir.ActivationFunctionType
AX = mybir.AxisListType.X

C_ID, C_MASK, C_LVL, C_BLK, C_ONE, C_BLK64, C_IOTA, C_IOTAE, C_ANTI, C_END = (
    0, 128, 384, 1280, 1408, 1536, 1664, 1728, 1760, 1888)
P_GMIX, P_GMEM, P_GFFN, P_MU, P_W0, P_A0, P_KK, P_KA, P_RK, P_GNG, P_GNB, P_END = (
    0, 8, 16, 24, 35, 38, 41, 44, 47, 50, 53, 56)


class Chain:

    def __init__(self, eng, sem, base=None):
        self.eng, self.sem, self.base, self.n = eng, sem, base, 0

    def __call__(self, ins):
        self.n += 1
        ins.then_inc(self.sem, 1)
        self.eng.wait_ge(self.sem, self.n if self.base is None else self.base + self.n)


def layer_kernel(nc, xT, x, memT, win, wmem, wout, params, consts, wlora, gup, relb, onehot,
                 wr, brouter, bgu, bdown, gfin, wgu, wdn, out, dbg=None, part=9):
    ctx = ExitStack()
    with ctx:
        def sb(name, cols, dt=F32, rows=P):
            return ctx.enter_context(nc.sbuf_tensor(name, [rows, cols], dt))

        def sem(name):
            return ctx.enter_context(nc.semaphore(name))

        bank = [ctx.enter_context(nc.psum_tensor(f"bank{i}", [P, 512], F32)) for i in range(8)]
        bias_dram = nc.dram_tensor("bias_rows", [NMOBA, 512], F32).ap()

        ring = sb("ring", NSLOT * SLOT)
        spare = sb("spare", 8192)
        cst = sb("cst", C_END)
        par = sb("par", P_END)
        bgu_s = sb("bgu_s", E * 16)
        bdn_s = sb("bdn_s", D, rows=E)
        gfin_s = sb("gfin_s", D)
        lora_s = sb("lora_s", 384)
        gup_s = sb("gup_s", 384)
        relb_s = sb("relb_s", 8, rows=E)
        wr_s = sb("wr_s", KT * E)
        br_s = sb("br_s", E, rows=1)
        xT_s = sb("xT_s", KT * T)
        qm_s = sb("qm_s", 8 * T)
        vn_s = sb("vn_s", TT * 384)
        mk_s = sb("mk_s", 2 * T)
        mv_s = sb("mv_s", TT * 256)
        toep = sb("toep", NMOBA * 256)
        raw = sb("raw", 11 * 257)
        mix = sb("mix", 11 * 256)
        stat = sb("stat", 160)
        npass_i = sb("npass_i", 4, I32)

        def slot(k, n=1):
            return ring[:, k * SLOT:(k + n) * SLOT]

        def c_(col, n=128):
            return cst[:, col:col + n]

        def pc(col, n=1):
            return par[:, col:col + n]

        def r3(ap, a):
            return ap.rearrange("p (a n) -> p a n", a=a)

        ident = c_(C_ID)
        ones = c_(C_ONE)
        blk = c_(C_BLK)
        hT = r3(xT_s[:, :], KT)
        wmem_s = r3(spare[:, 0:4096], KT)
        hmT = r3(spare[:, 4096:6144], KT)
        sq = spare[:, 6144:8192]
        rstd = mix[:, 0:256]
        ohot_s = mix[0:E, 512:1024]
        brow_s = mix[0:NMOBA, 1024:1536]
        win_s = [r3(slot(g), KT) for g in range(NG)]
        wout_s = ring[:, 0:4 * SLOT].rearrange("p (k n) -> p k n", k=KT)
        qk = r3(qm_s[:, 0:6 * T], 6)
        mq = r3(qm_s[:, 6 * T:8 * T], 2)
        vn = r3(vn_s[:, :], TT)
        mk = r3(mk_s[:, :], 2)
        mv = r3(mv_s[:, :], TT)
        toe = r3(toep[:, :], NMOBA)
        rw = r3(raw[:, :], 11)
        mx = r3(mix[:, :], 11)
        W3 = 3 * T
        RA = spare[:, 0:1536].rearrange("p (a c r n) -> p a c r n", a=NCT, c=2, r=2)
        kt = r3(spare[:, 1536:1536 + W3], NCT)
        bt = r3(spare[:, 2304:2304 + W3], NCT)
        sig_a = r3(spare[:, 3072:3072 + W3], NCT)
        gate = r3(spare[:, 3840:3840 + W3], NCT)
        kk_ = r3(spare[:, 4608:4608 + W3], NCT)
        bonus = r3(spare[:, 5376:5376 + W3], NCT)
        tmp = r3(spare[:, 6144:6144 + W3], NCT)
        tmp2 = r3(spare[:, 6912:6912 + W3], NCT)
        sw = r3(raw[:, 0:W3], NCT)
        cum = raw[:, 768:768 + 6 * 129].rearrange("p (a c n) -> p a c n", a=NCT, c=2)
        epos = raw[:, 1542:1542 + 6 * 129].rearrange("p (a c n) -> p a c n", a=NCT, c=2)
        eneg = r3(raw[:, 0:W3], NCT)
        rr = mx[:, 5:8, :]
        vv = mx[:, 8:11, :]
        kv = mx[:, 2:5, :]
        R0 = 6 * SLOT
        AT = ring[:, R0:R0 + 6144].rearrange("p (m n) -> p m n", m=NM)
        Tm = ring[:, R0 + 6144:R0 + 7680].rearrange("p (m n) -> p m n", m=NM)
        Em = ring[:, R0 + 7680:R0 + 9216].rearrange("p (m n) -> p m n", m=NM)
        Wm = ring[:, R0 + 9216:R0 + 10752].rearrange("p (m n) -> p m n", m=NM)
        Cm = ring[:, R0 + 10752:R0 + 12288].rearrange("p (m n) -> p m n", m=NM)
        Vn = xT_s[:, 0:768].rearrange("p (c n) -> p c n", c=2)
        Kn = xT_s[:, 768:1152]
        Bn = xT_s[:, 1152:1536]
        G_s = xT_s[:, 1536:1920]
        U_s = mix[:, 0:384]
        X1 = mix[:, 384:576].rearrange("p (a n) -> p a n", a=NCT)
        osb = r3(spare[:, 0:W3], NCT)
        yT_s = mix[:, 768:2816]
        yT = r3(yT_s, KT)
        prob = [ring[:, 4 * SLOT + 512 * i:4 * SLOT + 512 * i + 512] for i in range(2)]
        pT = [ring[:, 4 * SLOT + 1024 + 512 * i:4 * SLOT + 1536 + 512 * i] for i in range(2)]
        x2 = r3(spare[:, 0:2048], TT)
        hn = r3(spare[:, 2048:4096], TT)
        h2T = r3(spare[:, 4096:6144], KT)
        sqx = spare[:, 6144:7168]
        xn = r3(qm_s[:, :], TT)
        lg = r3(raw[:, 0:64], 2)
        v8 = raw[:, 64:80]
        i8 = raw[:, 80:96].bitcast(U32)
        i8f = raw[:, 96:112]
        e4 = raw[:, 112:120]
        MK = r3(raw[:, 128:192], 2)
        MW = r3(raw[:, 192:256], 2)
        RKs = r3(raw[:, 256:320], 2)
        ttmp = raw[:, 320:352]
        MWT = raw[0:E, 352:608]
        s4 = raw[:, 608:616]
        ctr = raw[:, 616:624]
        sel = raw[:, 640:896].rearrange("p (t s) -> p t s", t=TT)
        selw = raw[:, 896:1152].rearrange("p (t s) -> p t s", t=TT)
        selT = raw[:, 1152:1408]
        XTs = r3(xT_s[:, 0:1024], KT)
        Hs = [r3(xT_s[:, 1024 + 512 * j:1536 + 512 * j], KT) for j in range(2)]
        yTs = r3(yT_s[:, 0:1024], KT)
        yN = yT_s[:, 1024:2048]
        g1 = qm_s[:, 0:512]
        u1 = qm_s[:, 512:1024]
        sg = qm_s[:, 1024:1536]
        tu = qm_s[:, 1536:2048]

        s_mem, s_wmem, s_cst, s_x, s_par, s_small = (sem("s_mem"), sem("s_wmem"), sem("s_cst"),
                                                     sem("s_x"), sem("s_par"), sem("s_small"))
        s_win = [sem(f"s_win{g}") for g in range(NG)]
        s_ohot, s_browd, s_toep, s_flip, s_flipe = (sem("s_ohot"), sem("s_browd"), sem("s_toep"),
                                                    sem("s_flip"), sem("s_flipe"))
        s_wout, s_xn = sem("s_wout"), sem("s_xn")
        s_slot = [sem(f"s_slot{k}") for k in range(NSLOT)]
        s_out = sem("s_out")
        s_sq, s_ss, s_ms, s_rt, s_h = (sem("s_sq"), sem("s_ss"), sem("s_ms"), sem("s_rt"), sem("s_h"))
        s_bps, s_brow = sem("s_bps"), sem("s_brow")
        s_proj, s_pev = sem("s_proj"), sem("s_pev")
        s_pad, s_mix, s_tanh, s_lora, s_lsig, s_lg = (sem("s_pad"), sem("s_mix"), sem("s_tanh"),
                                                      sem("s_lora"), sem("s_lsig"), sem("s_lg"))
        s_kksq, s_kkn, s_kkms, s_kkrt = sem("s_kksq"), sem("s_kkn"), sem("s_kkms"), sem("s_kkrt")
        s_cum, s_exp = sem("s_cum"), sem("s_exp")
        s_rkp, s_rks, s_rwp = sem("s_rkp"), sem("s_rks"), sem("s_rwp")
        s_tp, s_tpe = sem("s_tp"), sem("s_tpe")
        s_A, s_Ae = sem("s_A"), sem("s_Ae")
        s_C, s_T1, s_TE = sem("s_C"), sem("s_T1"), sem("s_TE")
        s_W, s_We, s_Y = sem("s_W"), sem("s_We"), sem("s_Y")
        s_sol, s_sole = sem("s_sol"), sem("s_sole")
        s_ops, s_osb, s_gm, s_gc, s_gv, s_gvm, s_grt, s_yr = (
            sem("s_ops"), sem("s_osb"), sem("s_gm"), sem("s_gc"), sem("s_gv"), sem("s_gvm"),
            sem("s_grt"), sem("s_yr"))
        s_S, s_Ssb, s_Pe, s_Pn, s_PT, s_PTe, s_O, s_Oe = (
            sem("s_S"), sem("s_Ssb"), sem("s_Pe"), sem("s_Pn"), sem("s_PT"), sem("s_PTe"),
            sem("s_O"), sem("s_Oe"))
        s_op, s_x2, s_sqx, s_m2, s_r2, s_hn = (sem("s_op"), sem("s_x2"), sem("s_sqx"), sem("s_m2"),
                                               sem("s_r2"), sem("s_hn"))
        s_hT2, s_hT2e, s_lgp, s_top, s_tope, s_mk, s_rank, s_np = (
            sem("s_hT2"), sem("s_hT2e"), sem("s_lgp"), sem("s_top"), sem("s_tope"), sem("s_mk"),
            sem("s_rank"), sem("s_np"))
        s_mwt, s_mwte, s_bd, s_bde = sem("s_mwt"), sem("s_mwte"), sem("s_bd"), sem("s_bde")
        m_used, m_sel, m_x, m_xe, m_gu, m_act, m_sig, m_h, m_y, m_ye = (
            sem("m_used"), sem("m_sel"), sem("m_x"), sem("m_xe"), sem("m_gu"), sem("m_act"),
            sem("m_sig"), sem("m_h"), sem("m_y"), sem("m_ye"))
        m_t, m_te, m_sc, m_acc, m_rk = sem("m_t"), sem("m_te"), sem("m_sc"), sem("m_acc"), sem("m_rk")
        s_dve, s_act, s_dvl, s_f = sem("s_dve"), sem("s_act"), sem("s_dvl"), sem("s_f")
        f_sq, f_ms, f_rt, f_o = sem("f_sq"), sem("f_ms"), sem("f_rt"), sem("f_o")
        s_pool = sem("s_pool")
        s_dbg = sem("s_dbg")

        jobs = [("moba", h) for h in range(NMOBA)] + [("mem", h) for h in range(NMEM)]
        NJ = len(jobs)

        def job(j):
            kind, h = jobs[j]
            b = HD * (h % 2)
            if kind == "moba":
                return (qk[b:b + HD, h // 2, :], qk[b:b + HD, 3 + h // 2, :], b, 128,
                        h // 2, lambda m: vn[:, m, h * HD:(h + 1) * HD])
            return (mq[b:b + HD, h // 2, :], mk[b:b + HD, h // 2, :], b, 256,
                    6 + h // 2, lambda m: mv[:, m, h * HD:(h + 1) * HD])

        block = ctx.enter_context(nc.Block())

        @block.sync
        def _(sp):
            sp.dma_start(hmT, memT).then_inc(s_mem, 16)
            sp.dma_start(cst[:, :], consts).then_inc(s_cst, 16)
            sp.dma_start(par[:, :], params).then_inc(s_par, 16)
            sp.dma_start(wmem_s, wmem).then_inc(s_wmem, 16)
            sp.dma_start(hT, xT).then_inc(s_x, 16)
            for g in range(NG):
                sp.dma_start(win_s[g], win[g]).then_inc(s_win[g], 16)
            sp.wait_ge(s_brow, 2)
            sp.dma_start(bias_dram, brow_s).then_inc(s_browd, 16)
            sp.wait_ge(s_browd, 16)
            src = bass.AP(tensor=bias_dram.tensor, offset=0,
                          ap=[[1, P], [512, NMOBA], [1, 256]])
            sp.dma_start(toe, src).then_inc(s_toep, 16)
            sp.wait_ge(s_proj, 6)
            sp.dma_start(wout_s, wout.rearrange("(k p) n -> p k n", p=P)).then_inc(s_wout, 16)
            if part < 3:
                return
            sp.wait_ge(s_Oe, NJ)
            sp.dma_start(xn, x.rearrange("(t p) d -> p t d", p=P)).then_inc(s_xn, 16)
            if part < 5:
                return

            def load(e, k):
                if k < 8:
                    return sp.dma_start(slot(k), wgu[e, k * P:(k + 1) * P, :])
                return sp.dma_start(r3(slot(k), 2),
                                    wdn[e, (k - 8) * 256:(k - 7) * 256, :].rearrange(
                                        "(c p) n -> p c n", p=P))
            sp.wait_ge(s_Oe, NJ)
            for k in (4, 5):
                load(0, k).then_inc(s_slot[k], 16)
            sp.wait_ge(s_ops, 2)
            for k in range(6, NSLOT):
                load(0, k).then_inc(s_slot[k], 16)
            sp.wait_ge(s_op, 4)
            for k in range(4):
                load(0, k).then_inc(s_slot[k], 16)

            def wait_free(k, done):
                if k == 7:
                    sp.wait_ge(m_gu, done + 1)
                elif k == 11:
                    sp.wait_ge(m_y, done + 1)
                else:
                    sp.wait_ge(m_used, done * (NSLOT - 2) + (k + 1 if k < 7 else k))

            with sp.Fori(1, E) as e:
                for k in range(NSLOT):
                    wait_free(k, e - 1)
                    load(e, k).then_inc(s_slot[k], 16)
            sp.wait_ge(s_np, 1)
            npass = sp.value_load(npass_i[0:1, 0:1], min_val=1, max_val=T // CAP)
            with sp.If(npass > 1):
                with sp.Fori(1, npass) as c:
                    with sp.Fori(0, E) as e:
                        for k in range(NSLOT):
                            wait_free(k, c * E + e - 1)
                            load(e, k).then_inc(s_slot[k], 16)
            for t in range(TT):
                sp.wait_ge(f_o, t + 1)
                sp.dma_start(out.rearrange("(t p) d -> p t d", p=P)[:, t, :], hn[:, t, :]).then_inc(s_out, 16)
            sp.wait_ge(s_out, 16 * TT)

        @block.gpsimd
        def _(pool):
            if part < 2:
                return
            mask = lambda l: c_(C_LVL + 128 * (l - 1)).unsqueeze(1).to_broadcast([P, NM, P])
            for l in range(1, 8):
                pool.wait_ge(s_Ae, NM)
                if l == 2:
                    pool.wait_ge(s_TE, NCT)
                if l >= 3:
                    pool.wait_ge(s_W, NCT * (l - 2))
                pool.tensor_tensor(Cm, AT[:, :, 0:P], mask(l), ALU.mult).then_inc(s_C, 1)

        @block.scalar
        def _(act):
            link = Chain(act, s_act)
            act.dma_start(lora_s[:, :], wlora).then_inc(s_small, 16)
            act.dma_start(gup_s[:, :], gup).then_inc(s_small, 16)
            act.dma_start(relb_s[:, 0:NMOBA], relb).then_inc(s_ohot, 16)
            act.dma_start(ohot_s, onehot).then_inc(s_ohot, 16)
            act.dma_start(wr_s[:, :], wr).then_inc(s_small, 16)
            act.dma_start(br_s[:, :], brouter).then_inc(s_small, 16)
            act.dma_start(bgu_s[:, :], bgu).then_inc(s_small, 16)
            act.dma_start(bdn_s[:, :], bdown).then_inc(s_small, 16)
            act.dma_start(gfin_s[:, :], gfin.partition_broadcast(P)).then_inc(s_small, 16)
            for n, (src, s) in enumerate(((hmT, s_mem), (hT, s_x))):
                act.wait_ge(s, 16)
                if n:
                    act.wait_ge(s_ss, 1)
                act.activation(r3(sq, KT), src, ACT.Square).then_inc(s_sq, 1)
                act.wait_ge(s_ms, n + 1)
                act.activation(rstd, rstd, ACT.Sqrt).then_inc(s_rt, 1)
            for u in range(13):
                act.wait_ge(s_proj, u + 1)
                ps = bank[u % 3]
                g = u - 2
                if u == 0:
                    act.activation(mk_s[:, :], ps[:, :], ACT.Copy).then_inc(s_pev, 1)
                elif u == 1:
                    act.activation(mv_s[:, :], ps[:, :], ACT.Copy).then_inc(s_pev, 1)
                elif g < 5:
                    if g == 0:
                        act.wait_ge(s_pad, 1)
                    act.activation(rw[:, 2 * g:2 * g + 2, 1:257], r3(ps[:, :], 2), ACT.Copy).then_inc(s_pev, 1)
                elif g == 5:
                    act.activation(rw[:, 10, 1:257], ps[:, 0:256], ACT.Copy).then_inc(s_pev, 1)
                    act.activation(qk[:, 0, :], ps[:, 256:512], ACT.Copy).then_inc(s_pev, 1)
                elif g < 8:
                    act.activation(qk[:, 2 * g - 11:2 * g - 9, :], r3(ps[:, :], 2), ACT.Copy).then_inc(s_pev, 1)
                elif g == 8:
                    act.activation(qk[:, 5, :], ps[:, 0:256], ACT.Copy).then_inc(s_pev, 1)
                    act.activation(mq[:, 0, :], ps[:, 256:512], ACT.Copy).then_inc(s_pev, 1)
                elif g == 9:
                    act.activation(vn[:, :, 0:256], r3(ps[:, :], 2), ACT.Copy).then_inc(s_pev, 1)
                else:
                    act.activation(mq[:, 1, :], ps[:, 0:256], ACT.Copy).then_inc(s_pev, 1)
                    act.activation(vn[:, :, 256:384], r3(ps[:, 256:512], 2), ACT.Copy).then_inc(s_pev, 1)
                if g == 2:
                    act.wait_ge(s_mix, 1)
                    act.activation(mx[0:64, 0, :], mx[0:64, 0, :], ACT.Tanh).then_inc(s_tanh, 1)
                    act.activation(mx[:, 1, :], mx[:, 1, :], ACT.Sigmoid).then_inc(s_tanh, 1)
                if g == 7:
                    act.wait_ge(s_lora, 1)
                    act.wait_ge(s_mix, 6)
                    zw = [bank[3][:, 0:256], bank[3][:, 256:512], bank[4][:, 0:256]]
                    za = [bank[5][:, 0:256], bank[5][:, 256:512], bank[6][:, 0:256]]
                    for a in range(NCT):
                        act.activation(sw[:, a, :], zw[a], ACT.Sigmoid, bias=pc(P_W0 + a)).then_inc(s_lsig, 1)
                    for a in range(NCT):
                        act.activation(sig_a[:, a, :], za[a], ACT.Sigmoid, bias=pc(P_A0 + a)).then_inc(s_lsig, 1)
                    act.activation(gate[:, 0:2, :], r3(bank[7][:, :], 2), ACT.Copy).then_inc(s_lg, 1)
                    act.activation(gate[:, 2, :], bank[4][:, 256:512], ACT.Copy).then_inc(s_lg, 1)
            act.wait_ge(s_kkms, 1)
            act.activation(tmp2, tmp2, ACT.Sqrt).then_inc(s_kkrt, 1)
            act.wait_ge(s_cum, 1)
            for a in range(NCT):
                for c in range(2):
                    m = 2 * a + c
                    act.activation(epos[:, a, c, :], cum[:, a, c, :], ACT.Exp,
                                   bias=stat[:, m:m + 1], scale=-DECAY).then_inc(s_exp, 1)
                    act.activation(eneg[:, a, c * CH:(c + 1) * CH], cum[:, a, c, 1:129], ACT.Exp,
                                   bias=stat[:, 6 + m:7 + m], scale=DECAY).then_inc(s_exp, 1)
            if part < 2:
                return
            for n, dst in enumerate((Vn[:, 0, :], Vn[:, 1, :], Kn, Bn)):
                act.wait_ge(s_tp, n + 1)
                act.activation(dst, bank[n][:, 0:384], ACT.Copy).then_inc(s_tpe, 1)
            for l in range(2, 8):
                for g in range(NCT):
                    n = NCT * (l - 2) + g
                    act.wait_ge(s_W, n + 1)
                    act.activation(Wm[:, 4 * g:4 * g + 4, :], r3(bank[n % 2][:, :], 4), ACT.Copy).then_inc(s_We, 1)
            act.wait_ge(s_gvm, 1)
            act.activation(tmp, tmp, ACT.Sqrt).then_inc(s_grt, 1)
            if part < 3:
                return
            for j in range(NJ):
                w0 = job(j)[3]
                act.wait_ge(s_Ssb, j + 1)
                pr = prob[j % 2]
                st = 16 * (j % 2)
                for q, (lo, hi) in enumerate(((0, w0), (w0, w0 + 256))):
                    act.activation(pr[:, lo:hi], pr[:, lo:hi], ACT.Exp, bias=stat[:, 32 + st + q:33 + st + q],
                                   accum_out=stat[:, 36 + st + q:37 + st + q]).then_inc(s_Pe, 1)
                act.wait_ge(s_PT, j + 1)
                w = w0 + 256
                act.activation(pT[j % 2][:, 0:w], bank[2 + j % 2][:, 0:w], ACT.Copy).then_inc(s_PTe, 1)
                act.wait_ge(s_O, j + 1)
                b, ot = job(j)[2], job(j)[4]
                act.activation(yT[b:b + HD, ot, :], bank[4 + j % 2][b:b + HD, 0:256], ACT.Copy).then_inc(s_Oe, 1)
            if part < 4:
                return
            act.wait_ge(s_x2, 4)
            for t in range(TT):
                act.activation(sqx, x2[:, t, :], ACT.Square, accum_out=stat[:, 64 + t:65 + t]).then_inc(s_sqx, 1)
                act.wait_ge(s_sqx, t + 1)
            act.wait_ge(s_m2, 1)
            act.activation(stat[:, 66:68], stat[:, 66:68], ACT.Sqrt).then_inc(s_r2, 1)
            for t in range(TT):
                act.wait_ge(s_top, t + 1)
                act.activation(e4[:, 4 * t:4 * t + 4], v8[:, 8 * t:8 * t + 4], ACT.Exp,
                               bias=s4[:, t:t + 1], accum_out=s4[:, 2 + t:3 + t]).then_inc(s_tope, 1)
            if part < 5:
                return
            act.wait_ge(s_np, 1)
            npass = act.value_load(npass_i[0:1, 0:1], min_val=1, max_val=T // CAP)
            with act.Fori(0, npass) as c:
                with act.Fori(0, E // 2) as i:
                    n = c * (E // 2) + i
                    for j in range(2):
                        act.wait_ge(m_act, n * 2 + (j + 1))
                        act.activation(sg, g1, ACT.Sigmoid, scale=ALPHA).then_inc(m_sig, 1)
                        act.wait_ge(m_y, n * 2 + (j + 1))
                        act.activation(yTs[:, :, j * CAP:(j + 1) * CAP], r3(bank[4][:, :], KT), ACT.Copy).then_inc(m_ye, 1)
                    for b in range(2):
                        act.wait_ge(m_t, n * 3 + (2 + b))
                        act.activation(yN[:, 512 * b:512 * b + 512], bank[6 + b][:, :], ACT.Copy).then_inc(m_te, 1)
            act.wait_ge(f_sq, 1)
            for t in range(TT):
                act.activation(sqx, x2[:, t, :], ACT.Square, accum_out=stat[:, 80 + t:81 + t]).then_inc(f_ms, 1)
                act.wait_ge(f_ms, t + 1)
            act.wait_ge(f_sq, 2)
            act.activation(stat[:, 82:84], stat[:, 82:84], ACT.Sqrt).then_inc(f_rt, 1)

        @block.vector
        def _(dve):
            link = Chain(dve, s_dve)
            dve.memset(rw[:, :, 0:1], 0.0).then_inc(s_pad, 1)
            dve.wait_ge(s_bps, 1)
            dve.tensor_copy(brow_s[:, 0:256], bank[3][0:NMOBA, 0:256]).then_inc(s_brow, 1)
            dve.memset(brow_s[:, 256:512], NEG).then_inc(s_brow, 1)
            for n, (h, g) in enumerate(((hmT, P_GMEM), (hT, P_GMIX))):
                dve.wait_ge(s_ss, n + 1)
                dve.tensor_scalar(rstd, bank[7][:, 0:256], 1.0 / D, EPS, ALU.mult, ALU.add).then_inc(s_ms, 1)
                dve.wait_ge(s_rt, n + 1)
                dve.wait_ge(s_par, 16)
                link(dve.reciprocal(rstd, rstd))
                for k in range(KT):
                    ins = dve.scalar_tensor_tensor(out=h[:, k, :], in0=h[:, k, :], scalar=pc(g + k), in1=rstd,
                                                   op0=ALU.mult, op1=ALU.mult)
                    ins.then_inc(s_h, 1)
                dve.wait_ge(s_h, KT * (n + 1))
            dve.wait_ge(s_pad, 1)
            dve.wait_ge(s_browd, 16)
            for u in range(6):
                lo, hi = 2 * u, min(2 * u + 2, 11)
                if u == 3:
                    dve.wait_ge(s_flip, 1)
                    for b in range(3):
                        dve.tensor_copy(toep[:, b * 512:(b + 1) * 512], bank[4 + b][:, :]).then_inc(s_flipe, 1)
                dve.wait_ge(s_pev, u + 3)
                link(dve.tensor_tensor(mx[:, lo:hi, :], rw[:, lo:hi, 0:256], rw[:, lo:hi, 1:257], ALU.subtract))
                for i in range(lo, hi):
                    ins = dve.scalar_tensor_tensor(out=mx[:, i, :], in0=mx[:, i, :], scalar=pc(P_MU + i),
                                                   in1=rw[:, i, 1:257], op0=ALU.mult, op1=ALU.add)
                    if i < hi - 1:
                        link(ins)
                    else:
                        ins.then_inc(s_mix, 1)
            dve.wait_ge(s_mix, 6)
            dve.wait_ge(s_proj, 2)
            for a in range(NCT):
                link(dve.tensor_scalar(kk_[:, a, :], kv[:, a, :], pc(P_KK + a), None, ALU.mult))
            dve.tensor_tensor(tmp, kk_, kk_, ALU.mult).then_inc(s_kksq, 1)
            dve.wait_ge(s_lsig, 3)
            link(dve.memset(cum[:, :, :, 0:1], 0.0))
            for a in range(NCT):
                for c in range(2):
                    link(dve.tensor_tensor_scan(cum[:, a, c, 1:129], c_(C_ONE), sw[:, a, c * CH:(c + 1) * CH],
                                                0.0, ALU.mult, ALU.add))
            cmid = raw[:, 768:768 + 6 * 129].rearrange("p (m n) -> p m n", m=6)[:, :, 64]
            link(dve.tensor_scalar(stat[:, 0:6], cmid, DECAY, None, ALU.mult))
            dve.tensor_scalar(stat[:, 6:12], cmid, -DECAY, None, ALU.mult).then_inc(s_cum, 1)
            dve.wait_ge(s_kkn, 1)
            link(dve.tensor_copy(tmp2[:, 0:2, :], r3(bank[3][:, :], 2)))
            dve.tensor_copy(tmp2[:, 2, :], bank[4][:, 0:256]).then_inc(s_kkms, 1)
            dve.wait_ge(s_kkrt, 1)
            link(dve.tensor_scalar(tmp2, tmp2, 1e-12, None, ALU.max))
            link(dve.reciprocal(tmp2, tmp2))
            link(dve.tensor_tensor(kk_, kk_, tmp2, ALU.mult))
            dve.wait_ge(s_lsig, 6)
            for a in range(NCT):
                link(dve.tensor_scalar(tmp[:, a, :], sig_a[:, a, :], 1.0, pc(P_KA + a), ALU.subtract, ALU.mult))
            link(dve.scalar_tensor_tensor(out=kv, in0=tmp, scalar=1.0, in1=kv, op0=ALU.add, op1=ALU.mult))
            for a in range(NCT):
                ins = dve.scalar_tensor_tensor(out=tmp2[:, a, :], in0=kv[:, a, :], scalar=pc(P_RK + a), in1=rr[:, a, :],
                                               op0=ALU.mult, op1=ALU.mult)
                ins.then_inc(s_rkp, 1)
            dve.wait_ge(s_rks, 1)
            link(dve.tensor_tensor(bonus[:, 0:2, :], r3(bank[5][:, :], 2), vv[:, 0:2, :], ALU.mult))
            link(dve.tensor_tensor(bonus[:, 2, :], bank[6][:, 0:256], vv[:, 2, :], ALU.mult))
            dve.wait_ge(s_exp, 12)
            link(dve.tensor_tensor(tmp, kk_, sig_a, ALU.mult))
            link(dve.tensor_tensor(bt, tmp, eneg, ALU.mult))
            link(dve.tensor_tensor(kt, kv, eneg, ALU.mult))
            for a in range(NCT):
                link(dve.tensor_tensor(RA[:, a, :, 1, :], r3(rr[:, a, :], 2), epos[:, a, :, 1:129], ALU.mult))
                link(dve.scalar_tensor_tensor(out=RA[:, a, :, 0, :], in0=r3(kk_[:, a, :], 2), scalar=-1.0,
                                              in1=epos[:, a, :, 0:128], op0=ALU.mult, op1=ALU.mult))
            link(dve.reciprocal(stat[:, 12:15], epos[:, :, 1, 0]))
            dve.tensor_tensor(stat[:, 12:15], stat[:, 12:15], epos[:, :, 0, 128], ALU.mult).then_inc(s_rwp, 1)
            if part < 2:
                return
            for m in range(NM):
                dve.wait_ge(s_A, m + 1)
                dve.tensor_tensor(AT[:, m, :].rearrange("p (a n) -> p a n", a=2),
                                  r3(bank[4 + m % 4][:, :], 2),
                                  c_(C_MASK, 256).unsqueeze(1).to_broadcast([P, 2, 256]), ALU.mult).then_inc(s_Ae, 1)
            dve.wait_ge(s_C, 1)
            dve.wait_ge(s_T1, NCT)
            idb = ident.unsqueeze(1).to_broadcast([P, 4, P])
            for g in range(NCT):
                m4 = slice(4 * g, 4 * g + 4)
                link(dve.tensor_tensor(Em[:, m4, :], Cm[:, m4, :], idb, ALU.add))
                dve.tensor_tensor(Tm[:, m4, :], r3(bank[4 + g][:, :], 4), idb, ALU.add).then_inc(s_TE, 1)
            for l in range(2, 8):
                for g in range(NCT):
                    m4 = slice(4 * g, 4 * g + 4)
                    dve.wait_ge(s_Y, NCT * (l - 2) + g + 1)
                    dve.wait_ge(s_TE, NCT * (l - 2) + g + 1)
                    if l < 7:
                        link(dve.tensor_tensor(Tm[:, m4, :], r3(bank[2 + 2 * g][:, :], 4), Tm[:, m4, :], ALU.add))
                    dve.tensor_tensor(Em[:, m4, :], r3(bank[3 + 2 * g][:, :], 4), Em[:, m4, :], ALU.add).then_inc(s_TE, 1)
            for c in range(2):
                dve.wait_ge(s_sol, 3 * c + 1)
                Gv = G_s.rearrange("p (a h n) -> p a h n", a=NCT, h=2)
                link(dve.tensor_copy(Gv[:, :, 0, :], r3(bank[0][:, 0:192], NCT)))
                dve.tensor_copy(Gv[:, :, 1, :], r3(bank[3][:, 0:192], NCT)).then_inc(s_sole, 1)
                dve.wait_ge(s_sol, 3 * c + 2)
                if c:
                    dve.wait_ge(s_ops, 1)
                dve.tensor_copy(U_s, bank[1][:, 0:384]).then_inc(s_sole, 1)
                if c == 0:
                    dve.wait_ge(s_sol, 3)
                    for a in range(NCT):
                        for h in range(2):
                            b = HD * h
                            ins = dve.tensor_scalar(X1[b:b + HD, a, :], bank[2][b:b + HD, a * P + b:a * P + b + HD],
                                                    stat[b:b + HD, 12 + a:13 + a], None, ALU.mult)
                            if a < NCT - 1 or h == 0:
                                link(ins)
                            else:
                                ins.then_inc(s_sole, 1)
            dve.wait_ge(s_ops, 2)
            link(dve.tensor_copy(osb[:, 0:2, :], r3(bank[4][:, :], 2)))
            dve.tensor_copy(osb[:, 2, :], bank[5][:, 0:256]).then_inc(s_osb, 1)
            dve.wait_ge(s_gm, 1)
            dve.wait_ge(s_osb, 1)
            link(dve.tensor_tensor(osb[:, 0:2, :], osb[:, 0:2, :], r3(bank[6][:, :], 2), ALU.subtract))
            link(dve.tensor_tensor(osb[:, 2, :], osb[:, 2, :], bank[7][:, 0:256], ALU.subtract))
            dve.tensor_tensor(tmp, osb, osb, ALU.mult).then_inc(s_gc, 1)
            dve.wait_ge(s_gv, 1)
            link(dve.tensor_scalar(tmp[:, 0:2, :], r3(bank[6][:, :], 2), GN_EPS, None, ALU.add))
            dve.tensor_scalar(tmp[:, 2, :], bank[7][:, 0:256], GN_EPS, None, ALU.add).then_inc(s_gvm, 1)
            dve.wait_ge(s_grt, 1)
            link(dve.reciprocal(tmp, tmp))
            link(dve.tensor_tensor(osb, osb, tmp, ALU.mult))
            for a in range(NCT):
                link(dve.tensor_scalar(osb[:, a, :], osb[:, a, :], pc(P_GNG + a), pc(P_GNB + a), ALU.mult, ALU.add))
            link(dve.tensor_tensor(osb, osb, bonus, ALU.add))
            dve.wait_ge(s_lg, 2)
            for a in range(NCT):
                dve.tensor_tensor(yT[:, 3 + a, :], osb[:, a, :], gate[:, a, :], ALU.mult).then_inc(s_yr, 1)
            if part < 3:
                return
            dve.wait_ge(s_flipe, 3)
            for j in range(NJ):
                w0 = job(j)[3]
                w = w0 + 256
                pr = prob[j % 2]
                st = 16 * (j % 2)
                ps = bank[j % 2]
                dve.wait_ge(s_S, j + 1)
                if j >= 2:
                    dve.wait_ge(s_PT, j - 1)
                if j < NMOBA:
                    link(dve.scalar_tensor_tensor(out=pr[:, 0:128], in0=ps[:, 0:128], scalar=HD ** -0.5,
                                                  in1=toe[:, j, 128:256], op0=ALU.mult, op1=ALU.add))
                    link(dve.scalar_tensor_tensor(out=pr[:, 128:384], in0=ps[:, 128:384], scalar=HD ** -0.5,
                                                  in1=toe[:, j, :], op0=ALU.mult, op1=ALU.add))
                else:
                    link(dve.tensor_scalar(pr[:, 0:w], ps[:, 0:w], HD ** -0.5, None, ALU.mult))
                mxc = stat[:, 34 + st:36 + st]
                link(dve.tensor_reduce(mxc[:, 0:1], pr[:, 0:w0], AX, ALU.max))
                link(dve.tensor_reduce(mxc[:, 1:2], pr[:, w0:w], AX, ALU.max))
                dve.tensor_scalar(stat[:, 32 + st:34 + st], mxc, -1.0, None, ALU.mult).then_inc(s_Ssb, 1)
                dve.wait_ge(s_Pe, 2 * j + 2)
                link(dve.reciprocal(stat[:, 38 + st:40 + st], stat[:, 36 + st:38 + st]))
                link(dve.tensor_scalar(pr[:, 0:w0], pr[:, 0:w0], stat[:, 38 + st:39 + st], None, ALU.mult))
                dve.tensor_scalar(pr[:, w0:w], pr[:, w0:w], stat[:, 39 + st:40 + st], None, ALU.mult).then_inc(s_Pn, 1)
            if part < 4:
                return
            dve.wait_ge(s_xn, 16)
            for n in range(4):
                t, h = n // 2, n % 2
                dve.wait_ge(s_op, n + 1)
                dve.tensor_tensor(x2[:, t, h * 512:h * 512 + 512], bank[n][:, :], xn[:, t, h * 512:h * 512 + 512],
                                  ALU.add).then_inc(s_x2, 1)
            dve.wait_ge(s_sqx, 2)
            dve.tensor_scalar(stat[:, 66:68], stat[:, 64:66], 1.0 / D, EPS, ALU.mult, ALU.add).then_inc(s_m2, 1)
            dve.wait_ge(s_r2, 1)
            link(dve.reciprocal(stat[:, 66:68], stat[:, 66:68]))
            for t in range(TT):
                dve.tensor_scalar(hn[:, t, :], x2[:, t, :], stat[:, 66 + t:67 + t], None, ALU.mult).then_inc(s_hn, 1)
            for b in range(4):
                dve.wait_ge(s_hT2, b + 1)
                dve.tensor_tensor(h2T[:, 2 * b:2 * b + 2, :], r3(bank[4 + b][:, :], 2),
                                  pc(P_GFFN + 2 * b, 2).unsqueeze(2).to_broadcast([P, 2, 256]),
                                  ALU.mult).then_inc(s_hT2e, 1)
            dve.wait_ge(s_lgp, 1)
            link(dve.tensor_copy(lg, r3(bank[0][:, 0:64], 2)))
            link(dve.memset(MK, 0.0))
            link(dve.memset(MW, 0.0))
            for t in range(TT):
                link(dve.max(v8[:, 8 * t:8 * t + 8], lg[:, t, :]))
                link(dve.max_index(i8[:, 8 * t:8 * t + 8], v8[:, 8 * t:8 * t + 8], lg[:, t, :]))
                link(dve.tensor_copy(i8f[:, 8 * t:8 * t + 8], i8[:, 8 * t:8 * t + 8]))
                dve.tensor_scalar(s4[:, t:t + 1], v8[:, 8 * t:8 * t + 1], -1.0, None, ALU.mult).then_inc(s_top, 1)
            iota_e = c_(C_IOTAE, E)
            for t in range(TT):
                for k in range(TOPK):
                    ins = dve.scalar_tensor_tensor(out=MK[:, t, :], in0=iota_e, scalar=i8f[:, 8 * t + k:8 * t + k + 1],
                                                   in1=MK[:, t, :], op0=ALU.is_equal, op1=ALU.add)
                    if k < TOPK - 1:
                        link(ins)
                    else:
                        ins.then_inc(s_mk, 1)
            dve.wait_ge(s_tope, 2)
            link(dve.reciprocal(s4[:, 2:4], s4[:, 2:4]))
            for t in range(TT):
                link(dve.tensor_scalar(e4[:, 4 * t:4 * t + 4], e4[:, 4 * t:4 * t + 4], s4[:, 2 + t:3 + t], None, ALU.mult))
                for k in range(TOPK):
                    link(dve.tensor_scalar(ttmp, iota_e, i8f[:, 8 * t + k:8 * t + k + 1],
                                           e4[:, 4 * t + k:4 * t + k + 1], ALU.is_equal, ALU.mult))
                    link(dve.tensor_tensor(MW[:, t, :], MW[:, t, :], ttmp, ALU.add))
            dve.wait_ge(s_rank, 1)
            dve.wait_ge(s_mk, 2)
            link(dve.scalar_tensor_tensor(out=RKs, in0=r3(bank[1][:, 0:64], 2), scalar=NO_SLOT, in1=MK,
                                          op0=ALU.add, op1=ALU.mult))
            link(dve.tensor_scalar(RKs, RKs, -NO_SLOT, None, ALU.add))
            link(dve.tensor_reduce(ctr[0:1, 0:1], bank[2][0:1, 0:E], AX, ALU.max))
            link(dve.tensor_scalar(ctr[0:1, 1:2], ctr[0:1, 0:1], CAP + 0.5, 1.0, ALU.is_gt, ALU.add))
            for k in range(2, T // CAP):
                link(dve.scalar_tensor_tensor(out=ctr[0:1, 1:2], in0=ctr[0:1, 0:1], scalar=k * CAP + 0.5,
                                              in1=ctr[0:1, 1:2], op0=ALU.is_gt, op1=ALU.add))
            dve.tensor_copy(npass_i[0:1, 0:1], ctr[0:1, 1:2]).then_inc(s_np, 1)
            dve.wait_ge(s_mwt, 1)
            dve.tensor_copy(MWT, bank[3][0:E, 0:256]).then_inc(s_mwte, 1)
            for n in range(4):
                t, h = n // 2, n % 2
                dve.wait_ge(s_bd, n + 1)
                ins = dve.tensor_tensor(x2[:, t, h * 512:h * 512 + 512], bank[4 + n][:, :],
                                        x2[:, t, h * 512:h * 512 + 512], ALU.add)
                if n < 3:
                    link(ins)
                else:
                    ins.then_inc(s_dvl, 1)
            if part < 5:
                return
            dve.wait_ge(s_np, 1)
            npass = dve.value_load(npass_i[0:1, 0:1], min_val=1, max_val=T // CAP)
            iota = c_(C_IOTA, CAP)
            NB = 18
            with dve.Fori(0, npass) as c:
                with dve.Fori(0, E // 2) as i:
                    n = c * (E // 2) + i
                    lk = Chain(dve, s_dvl, base=n * NB + c + 1)
                    for j in range(2):
                        for t in range(TT):
                            rk = RKs[:, t, :][:, bass.ds(i * 2 + j, 1)]
                            mw = MW[:, t, :][:, bass.ds(i * 2 + j, 1)]
                            lk(dve.tensor_scalar(selw[:, t, j * CAP:(j + 1) * CAP], iota, rk, mw,
                                                 ALU.is_equal, ALU.mult))
                            ins = dve.tensor_scalar(sel[:, t, j * CAP:(j + 1) * CAP], iota, rk, None, ALU.is_equal)
                            ins.then_inc(m_sel, 1)
                    for b in range(2):
                        dve.wait_ge(m_x, n * 2 + (b + 1))
                        dve.tensor_tensor(XTs[:, 4 * b:4 * b + 4, :], r3(bank[b][:, :], 4),
                                          pc(P_GFFN + 4 * b, 4).unsqueeze(2).to_broadcast([P, 4, 128]),
                                          ALU.mult).then_inc(m_xe, 1)
                    for j in range(2):
                        dve.wait_ge(m_gu, n * 2 + (j + 1))
                        bg = bgu_s[:, bass.ds(i * 32 + j * 16, 8)].unsqueeze(2).to_broadcast([P, 8, CAP])
                        bu = bgu_s[:, bass.ds(i * 32 + j * 16 + 8, 8)].unsqueeze(2).to_broadcast([P, 8, CAP])
                        lk(dve.tensor_tensor(r3(g1, 8), r3(bank[2][:, :], 8), bg, ALU.add))
                        dve.tensor_scalar(g1, g1, LIMIT, None, ALU.min).then_inc(m_act, 1)
                        lk(dve.tensor_tensor(r3(u1, 8), r3(bank[3][:, :], 8), bu, ALU.add))
                        lk(dve.tensor_scalar(u1, u1, LIMIT, -LIMIT, ALU.min, ALU.max))
                        dve.wait_ge(m_act, n * 2 + (j + 1))
                        lk(dve.scalar_tensor_tensor(out=tu, in0=u1, scalar=1.0, in1=g1, op0=ALU.add, op1=ALU.mult))
                        dve.wait_ge(m_sig, n * 2 + (j + 1))
                        dve.tensor_tensor(Hs[j].rearrange("p a n -> p (a n)"), tu, sg, ALU.mult).then_inc(m_h, 1)
                    dve.wait_ge(m_t, n * 3 + 1)
                    lk(dve.tensor_copy(selT, bank[5][:, 0:256]))
                    for q in range(4):
                        t, h = q // 2, q % 2
                        dve.wait_ge(m_sc, n * 4 + (q + 1))
                        lk(dve.tensor_tensor(x2[:, t, h * 512:h * 512 + 512], bank[(0, 1, 5, 4)[q]][:, :],
                                             x2[:, t, h * 512:h * 512 + 512], ALU.add))
                    assert lk.n == NB - 1, lk.n
                    lk(dve.memset(stat[:, 100:101], 0.0))
                lk = Chain(dve, s_dvl, base=(c + 1) * (E // 2 * NB) + c + 1)
                lk(dve.tensor_scalar(RKs, RKs, -float(CAP), None, ALU.add))
            lf = Chain(dve, s_f)
            dve.memset(stat[:, 101:102], 0.0).then_inc(f_sq, 1)
            dve.wait_ge(f_ms, 2)
            dve.tensor_scalar(stat[:, 82:84], stat[:, 80:82], 1.0 / D, EPS, ALU.mult, ALU.add).then_inc(f_sq, 1)
            dve.wait_ge(f_rt, 1)
            lf(dve.reciprocal(stat[:, 82:84], stat[:, 82:84]))
            for t in range(TT):
                dve.scalar_tensor_tensor(out=hn[:, t, :], in0=x2[:, t, :], scalar=stat[:, 82 + t:83 + t],
                                         in1=gfin_s[:, :], op0=ALU.mult, op1=ALU.mult).then_inc(f_o, 1)

        @block.tensor
        def _(pe):
            mm = pe.matmul
            pe.wait_ge(s_ohot, 32)
            mm(bank[3][0:NMOBA, 0:512], relb_s[:, 0:NMOBA], ohot_s, start=True, stop=True).then_inc(s_bps, 1)
            pe.wait_ge(s_cst, 16)

            def norm_sum(n):
                pe.wait_ge(s_sq, n + 1)
                if n:
                    pe.wait_ge(s_ms, n)
                for k in range(KT):
                    i = mm(bank[7][:, 0:256], ones, r3(sq, KT)[:, k, :], start=k == 0, stop=k == KT - 1)
                i.then_inc(s_ss, 1)

            def unit_start(u):
                if u >= 3:
                    pe.wait_ge(s_pev, u - 2 + (u - 3 >= 7) + (u - 3 >= 10))

            def channels(out_ap, w, h, last=None):
                for k in range(KT):
                    i = mm(out_ap, w[:, k, :], h[:, k, :], start=k == 0, stop=k == KT - 1)
                return i

            def tokens(ps, col, ncol, w, h, lo):
                for t in range(TT):
                    for k in range(KT):
                        i = mm(ps[:, col + t * ncol:col + (t + 1) * ncol], h[:, k, t * P:(t + 1) * P],
                               w[:, k, lo:lo + ncol], start=k == 0, stop=k == KT - 1)
                return i

            norm_sum(0)
            pe.wait_ge(s_wmem, 16)
            pe.wait_ge(s_h, KT)
            for a in range(2):
                i = channels(bank[0][:, a * 256:(a + 1) * 256], wmem_s[:, :, a * P:(a + 1) * P], hmT)
            i.then_inc(s_proj, 1)
            tokens(bank[1], 0, 256, wmem_s, hmT, 256).then_inc(s_proj, 1)
            norm_sum(1)
            pe.wait_ge(s_h, 2 * KT)
            for g in range(NG):
                u = g + 2
                if g == 2:
                    pe.wait_ge(s_toep, 16)
                    for b in range(3):
                        i = mm(bank[4 + b][:, :], c_(C_ANTI), toep[:, b * 512:(b + 1) * 512], start=True, stop=True)
                    i.then_inc(s_flip, 1)
                unit_start(u)
                pe.wait_ge(s_win[g], 16)
                ps = bank[u % 3]
                if g == 9:
                    i = tokens(ps, 0, 256, win_s[g], hT, 0)
                else:
                    i = channels(ps[:, 0:256], win_s[g][:, :, 0:P], hT)
                    if g == 10:
                        i = tokens(ps, 256, 128, win_s[g], hT, 128)
                    else:
                        i = channels(ps[:, 256:512], win_s[g][:, :, P:2 * P], hT)
                i.then_inc(s_proj, 1)
                if g == 6:
                    pe.wait_ge(s_tanh, 2)
                    pe.wait_ge(s_small, 7 * 16)
                    pe.wait_ge(s_brow, 1)
                    pe.wait_ge(s_flipe, 3)
                    zw = [bank[3][:, 0:256], bank[3][:, 256:512], bank[4][:, 0:256]]
                    za = [bank[5][:, 0:256], bank[5][:, 256:512], bank[6][:, 0:256]]
                    zg = [bank[7][:, 0:256], bank[7][:, 256:512], bank[4][:, 256:512]]
                    for a in range(NCT):
                        cs = slice(a * P, (a + 1) * P)
                        mm(zw[a], lora_s[0:64, cs], mx[0:64, 0, :], start=True, stop=True)
                        mm(za[a], lora_s[64:128, cs], mx[64:128, 0, :], start=True, stop=True)
                        i = mm(zg[a], gup_s[:, cs], mx[:, 1, :], start=True, stop=True)
                    i.then_inc(s_lora, 1)
            pe.wait_ge(s_kksq, 1)
            pe.wait_ge(s_lsig, 6)
            pe.wait_ge(s_lg, 2)
            three = lambda b: [bank[b][:, 0:256], bank[b][:, 256:512], bank[b + 1][:, 0:256]]
            for a in range(NCT):
                i = mm(three(3)[a], blk, tmp[:, a, :], start=True, stop=True)
            i.then_inc(s_kkn, 1)
            pe.wait_ge(s_rkp, 3)
            pe.wait_ge(s_lg, 2)
            for a in range(NCT):
                i = mm(three(5)[a], blk, tmp2[:, a, :], start=True, stop=True)
            i.then_inc(s_rks, 1)
            if part < 2:
                return
            pe.wait_ge(s_pev, 16)
            pe.wait_ge(s_rwp, 1)
            for n in range(4):
                for a in range(NCT):
                    src = (vv[:, a, 0:128], vv[:, a, 128:256], kt[:, a, 0:128], bt[:, a, 0:128])[n]
                    i = pe.transpose(bank[n][:, a * P:(a + 1) * P], src, ident)
                i.then_inc(s_tp, 1)
            for m in range(NM):
                a, c, h = m // 4, m // 2 % 2, m % 2
                b = HD * h
                if m >= 4:
                    pe.wait_ge(s_Ae, m - 3)
                rhs = RA[b:b + HD, a, c, :, :].rearrange("p r n -> p (r n)")
                mm(bank[4 + m % 4][:, 0:256], bt[b:b + HD, a, c * CH:(c + 1) * CH], rhs, start=True, stop=True)
                mm(bank[4 + m % 4][:, 256:512], kt[b:b + HD, a, c * CH:(c + 1) * CH], rhs,
                   start=True, stop=True).then_inc(s_A, 1)
            pe.wait_ge(s_Ae, NM)
            pe.wait_ge(s_C, 1)
            for g in range(NCT):
                for q in range(4):
                    i = pe.transpose(bank[4 + g][:, q * P:(q + 1) * P], Cm[:, 4 * g + q, :], ident)
                i.then_inc(s_T1, 1)
            pe.wait_ge(s_tpe, 4)
            for l in range(2, 8):
                def w_step(g):
                    n = NCT * (l - 2) + g
                    pe.wait_ge(s_TE, n + 1)
                    if n >= 2:
                        pe.wait_ge(s_We, n - 1)
                    for q in range(4):
                        i = mm(bank[n % 2][:, q * P:(q + 1) * P], Cm[:, 4 * g + q, :], Tm[:, 4 * g + q, :],
                               start=True, stop=True)
                    i.then_inc(s_W, 1)

                def y_step(g):
                    n = NCT * (l - 2) + g
                    pe.wait_ge(s_We, n + 1)
                    if l == 2:
                        pe.wait_ge(s_TE, NCT)
                    for q in range(4):
                        m = 4 * g + q
                        if l < 7:
                            mm(bank[2 + 2 * g][:, q * P:(q + 1) * P], Em[:, m, :], Wm[:, m, :], start=True, stop=True)
                        i = mm(bank[3 + 2 * g][:, q * P:(q + 1) * P], Wm[:, m, :], Em[:, m, :], start=True, stop=True)
                    i.then_inc(s_Y, 1)

                pe.wait_ge(s_C, l)
                w_step(0)
                w_step(1)
                y_step(0)
                w_step(2)
                y_step(1)
                y_step(2)
            pe.wait_ge(s_TE, NCT * 7)
            for c in range(2):
                for a in range(NCT):
                    for h in range(2):
                        m, b = a * 4 + c * 2 + h, HD * h
                        o = bank[3 * h][:, a * HD:(a + 1) * HD]
                        if c:
                            mm(o, RA[b:b + HD, a, 1, 0, :], X1[b:b + HD, a, :], start=True, stop=False)
                        i = mm(o, AT[:, m, 256:384], Vn[:, c, a * P + b:a * P + b + HD], start=c == 0, stop=True)
                i.then_inc(s_sol, 1)
                pe.wait_ge(s_sole, 3 * c + 1)
                for a in range(NCT):
                    for h in range(2):
                        m, b = a * 4 + c * 2 + h, HD * h
                        i = mm(bank[1][:, a * P + b:a * P + b + HD], Em[:, m, :], G_s[:, a * P + b:a * P + b + HD],
                               start=True, stop=True)
                i.then_inc(s_sol, 1)
                pe.wait_ge(s_sole, 3 * c + 2)
                if c == 0:
                    for a in range(NCT):
                        cs = slice(a * P, (a + 1) * P)
                        mm(bank[2][:, cs], Bn[:, cs], U_s[:, cs], start=True, stop=False)
                        i = mm(bank[2][:, cs], Kn[:, cs], Vn[:, 0, cs], start=False, stop=True)
                    i.then_inc(s_sol, 1)
                for a in range(NCT):
                    for h in range(2):
                        m, b = a * 4 + c * 2 + h, HD * h
                        o = bank[4 + a // 2][b:b + HD, (a % 2) * 256 + c * CH:(a % 2) * 256 + (c + 1) * CH]
                        vs = slice(a * P + b, a * P + b + HD)
                        mm(o, U_s[:, vs], AT[:, m, 128:256], start=True, stop=False)
                        i = mm(o, Vn[:, c, vs], AT[:, m, 384:512], start=False, stop=c == 0)
                        if c:
                            i = mm(o, X1[b:b + HD, a, :], RA[b:b + HD, a, 1, 1, :], start=False, stop=True)
                i.then_inc(s_ops, 1)
                if c == 0:
                    pe.wait_ge(s_sole, 3)
            pe.wait_ge(s_osb, 1)
            for a in range(NCT):
                i = mm(three(6)[a], c_(C_BLK64), osb[:, a, :], start=True, stop=True)
            i.then_inc(s_gm, 1)
            pe.wait_ge(s_gc, 1)
            for a in range(NCT):
                i = mm(three(6)[a], c_(C_BLK64), tmp[:, a, :], start=True, stop=True)
            i.then_inc(s_gv, 1)
            if part < 3:
                return
            for j in range(NJ):
                q_, k_, b, w0, ot, vals = job(j)
                S = bank[j % 2]
                if j >= 2:
                    pe.wait_ge(s_Ssb, j - 1)
                mm(S[:, 0:w0], q_[:, 0:128], k_[:, 0:w0], start=True, stop=True)
                mm(S[:, w0:w0 + 256], q_[:, 128:256], k_, start=True, stop=True).then_inc(s_S, 1)
                pe.wait_ge(s_Pn, j + 1)
                pr = prob[j % 2]
                pb = bank[2 + j % 2]
                if j >= 2:
                    pe.wait_ge(s_PTe, j - 1)
                pe.transpose(pb[:, 0:128], pr[:, 0:128], ident)
                if w0 == 256:
                    pe.transpose(pb[:, 256:384], pr[:, 128:256], ident)
                pe.transpose(pb[:, 128:256], pr[:, w0:w0 + 128], ident)
                pe.transpose(pb[:, w0 + 128:w0 + 256], pr[:, w0 + 128:w0 + 256], ident).then_inc(s_PT, 1)
                pe.wait_ge(s_PTe, j + 1)
                if j >= 2:
                    pe.wait_ge(s_Oe, j - 1)
                ob = bank[4 + j % 2]
                pt = pT[j % 2]
                lo = 256 - w0
                if lo:
                    mm(ob[b:b + HD, 0:lo], vals(0), pt[:, 0:lo], start=True, stop=True)
                mm(ob[b:b + HD, lo:256], vals(0), pt[:, lo:256], start=True, stop=False)
                mm(ob[b:b + HD, lo:256], vals(1), pt[:, 256:256 + w0], start=False, stop=True).then_inc(s_O, 1)
            if part < 4:
                return
            pe.wait_ge(s_wout, 16)
            pe.wait_ge(s_Oe, NJ)
            pe.wait_ge(s_yr, NCT)
            for n in range(4):
                t, h = n // 2, n % 2
                for k in range(KT):
                    i = mm(bank[n][:, :], yT[:, k, t * P:(t + 1) * P], wout_s[:, k, h * 512:(h + 1) * 512],
                           start=k == 0, stop=k == KT - 1)
                i.then_inc(s_op, 1)
            pe.wait_ge(s_hn, TT)
            for b in range(4):
                for k in range(2):
                    for t in range(TT):
                        i = pe.transpose(bank[4 + b][:, k * 256 + t * P:k * 256 + (t + 1) * P],
                                         hn[:, t, (2 * b + k) * P:(2 * b + k + 1) * P], ident)
                i.then_inc(s_hT2, 1)
            pe.wait_ge(s_hT2e, 4)
            pe.wait_ge(s_x2, 4)
            for t in range(TT):
                o = bank[0][:, t * E:(t + 1) * E]
                for k in range(KT):
                    mm(o, h2T[:, k, t * P:(t + 1) * P], wr_s[:, k * E:(k + 1) * E], start=k == 0, stop=False)
                i = mm(o, c_(C_ONE)[0:1, :], br_s[0:1, :], start=False, stop=True)
            i.then_inc(s_lgp, 1)
            pe.wait_ge(s_mk, 2)
            strict = c_(C_MASK)
            mm(bank[1][:, 0:E], strict, MK[:, 0, :], start=True, stop=True)
            mm(bank[1][:, E:2 * E], strict, MK[:, 1, :], start=True, stop=False)
            mm(bank[1][:, E:2 * E], ones, MK[:, 0, :], start=False, stop=True)
            mm(bank[2][0:1, 0:E], ones[:, 0:1], MK[:, 0, :], start=True, stop=False)
            mm(bank[2][0:1, 0:E], ones[:, 0:1], MK[:, 1, :], start=False, stop=True).then_inc(s_rank, 1)
            pe.wait_ge(s_np, 1)
            for t in range(TT):
                i = pe.transpose(bank[3][0:E, t * P:(t + 1) * P], MW[:, t, :], ident)
            i.then_inc(s_mwt, 1)
            pe.wait_ge(s_mwte, 1)
            for n in range(4):
                t, h = n // 2, n % 2
                mm(bank[4 + n][:, :], MWT[:, t * P:(t + 1) * P], bdn_s[:, h * 512:(h + 1) * 512],
                   start=True, stop=True).then_inc(s_bd, 1)
            if part < 5:
                return
            npass = pe.value_load(npass_i[0:1, 0:1], min_val=1, max_val=T // CAP)
            with pe.Fori(0, npass) as c:
                with pe.Fori(0, E // 2) as i:
                    n = c * (E // 2) + i
                    dvl = n * 18 + c + 1
                    pe.wait_ge(m_sel, n * 4 + 4)
                    pe.wait_ge(s_dvl, dvl)
                    for k in range(KT):
                        for t in range(TT):
                            x_ = mm(bank[k // 4][:, (k % 4) * P:(k % 4 + 1) * P], hn[:, t, k * P:(k + 1) * P],
                                    sel[:, t, :], start=t == 0, stop=t == 1)
                        if k % 4 == 3:
                            x_.then_inc(m_x, 1)
                    pe.wait_ge(m_xe, n * 2 + 2)
                    for j in range(2):
                        for k in range(KT):
                            pe.wait_ge(s_slot[k], n * 32 + 16 * (j + 1))
                            w = slot(k).rearrange("p (f g) -> p g f", g=2)
                            for g in range(2):
                                for f in range(8):
                                    x_ = mm(bank[2 + g][:, f * CAP:(f + 1) * CAP], w[:, g, f * P:(f + 1) * P],
                                            XTs[:, k, j * CAP:(j + 1) * CAP], start=(k == 0 and f == 0),
                                            stop=(k == KT - 1), skip_group_check=True)
                            if k < KT - 1:
                                x_.then_inc(m_used, 1)
                            else:
                                x_.then_inc(m_gu, 1)
                        if j == 0:
                            for t in range(TT):
                                x_ = pe.transpose(bank[5][:, t * P:(t + 1) * P], selw[:, t, :], ident)
                            x_.then_inc(m_t, 1)
                        pe.wait_ge(m_h, n * 2 + (j + 1))
                        if j:
                            pe.wait_ge(m_ye, n * 2 + 1)
                        for k in range(KT):
                            w = r3(slot(8 + k // 2), 2)[:, k % 2, :]
                            if k % 2 == 0:
                                pe.wait_ge(s_slot[8 + k // 2], n * 32 + 16 * (j + 1))
                            for d in range(KT):
                                x_ = mm(bank[4][:, d * CAP:(d + 1) * CAP], w[:, d * P:(d + 1) * P], Hs[j][:, k, :],
                                        start=(k == 0 and d == 0), stop=(k == KT - 1), skip_group_check=True)
                            if k % 2 and k < KT - 1:
                                x_.then_inc(m_used, 1)
                        x_.then_inc(m_y, 1)
                    pe.wait_ge(m_ye, n * 2 + 2)
                    for d in range(KT):
                        x_ = pe.transpose(bank[6 + d // 4][:, (d % 4) * P:(d % 4 + 1) * P], yTs[:, d, :], ident)
                        if d % 4 == 3:
                            x_.then_inc(m_t, 1)
                    for q in range(4):
                        t, h = q // 2, q % 2
                        pe.wait_ge(m_te, n * 2 + (1 + h))
                        if q == 0:
                            pe.wait_ge(s_dvl, dvl + 13)
                        mm(bank[(0, 1, 5, 4)[q]][:, :], selT[:, t * P:(t + 1) * P], yN[:, h * 512:(h + 1) * 512],
                           start=True, stop=True).then_inc(m_sc, 1)


def _bucket_onehot():
    import math
    import numpy as np
    n = np.maximum(255 - np.arange(256), 0)
    nf = np.maximum(n, 1).astype(np.float32)
    large = 16 + (np.log(nf / np.float32(16)) / np.float32(math.log(8.0)) * np.float32(16)).astype(np.int32)
    b = np.where(n < 16, n, np.minimum(large, 31))
    oh = np.zeros((32, 512), np.float32)
    oh[b, np.arange(256)] = 1.0
    return oh


def _constants():
    import numpy as np
    c = np.zeros((P, C_END), np.float32)
    s, t = np.meshgrid(np.arange(P), np.arange(P), indexing="ij")
    c[:, C_ID:C_ID + P] = s == t
    c[:, C_MASK:C_MASK + P] = s < t
    c[:, C_MASK + P:C_MASK + 2 * P] = s <= t
    for l in range(1, 8):
        b = 2 ** l
        c[:, C_LVL + P * (l - 1):C_LVL + P * l] = (s // b == t // b) & (s % b < b // 2) & (t % b >= b // 2)
    c[:, C_BLK:C_BLK + P] = s // HD == t // HD
    c[:, C_ONE:C_ONE + P] = 1.0
    c[:, C_BLK64:C_BLK64 + P] = (s // HD == t // HD) / HD
    c[:, C_ANTI:C_ANTI + P] = s + t == P - 1
    c[:, C_IOTA:C_IOTA + CAP] = np.arange(CAP)
    c[:, C_IOTAE:C_IOTAE + E] = np.arange(E)
    return c


def kernel(**inputs):
    import numpy as np
    import concourse.bacc as bacc
    from concourse import mybir as mb
    from concourse.bass_utils import run_bass_kernel_spmd

    A = {k: np.asarray(v) for k, v in inputs.items()}
    order = [18, 19, 12, 13, 14, 9, 10, 11, 15, 16, 17, 0, 1, 2, 3, 4, 5, 20, 6, 7, 21, 8]
    w = A["w_in"][0].reshape(KT, P, 22, P)[:, :, order, :]
    col = lambda v: v.reshape(-1, P).T
    mu = A["rwkv_mu"][0].reshape(11, P)[[9, 10, 3, 4, 5, 0, 1, 2, 6, 7, 8]].T
    tr = lambda v: v.reshape(T, KT, P).transpose(2, 1, 0)
    arrays = {
        "xT": tr(A["x"][0]), "x": A["x"][0], "memT": tr(A["mem"][0]),
        "win": w.reshape(KT, P, NG, 256).transpose(2, 1, 0, 3),
        "wmem": A["w_mem_kv"][0].reshape(KT, P, 512).transpose(1, 0, 2),
        "wout": A["w_out"][0],
        "params": np.concatenate([col(A["g_mix"][0]), col(A["g_mem"][0]), col(A["g_ffn"][0]), mu] + [
            col(A[n][0]) for n in ("rwkv_w0", "rwkv_a0", "rwkv_k_k", "rwkv_k_a", "rwkv_r_k",
                                   "rwkv_gn_g", "rwkv_gn_b")], axis=1),
        "consts": _constants(),
        "wlora": np.concatenate([A["rwkv_w_up"][0], A["rwkv_a_up"][0]], axis=0),
        "gup": A["rwkv_g_up"][0], "relb": A["rel_bias"], "onehot": _bucket_onehot(),
        "wr": A["w_router"][0].reshape(KT, P, E).transpose(1, 0, 2).reshape(P, KT * E),
        "brouter": A["b_router"],
        "bgu": A["b_gate_up"][0].reshape(E, 8, P, 2).transpose(2, 0, 3, 1).reshape(P, E * 16),
        "bdown": A["b_down"][0], "gfin": A["g_final"],
        "wgu": A["w_gate_up"][0], "wdn": A["w_down"][0],
    }
    arrays = {k: np.ascontiguousarray(v) for k, v in arrays.items()}
    nc = bacc.Bacc("TRN2", target_bir_lowering=False, num_devices=1)
    args = [nc.dram_tensor(k, v.shape, mb.dt.from_np(v.dtype), kind="ExternalInput").ap()
            for k, v in arrays.items()]
    out = nc.dram_tensor("out", (T, D), mb.dt.float32, kind="ExternalOutput").ap()
    layer_kernel(nc, *args, out)
    r = run_bass_kernel_spmd(nc, [arrays], core_ids=[0])
    return r.results[0]["out"].reshape(1, T, D)
```

```python
from contextlib import ExitStack

import concourse.bass as bass
from concourse import mybir

P = 128
T = 256
D = 1024
KT = D // P
TT = T // P
HD = 64
NMOBA, NRWKV, NMEM = 6, 6, 4
NCT = 3
E = 32
TOPK = 4
CAP = 64
CH = 128
NM = NRWKV * T // CH
SLOT = 2048
NSLOT = 12
NG = 11
EPS = 1e-5
GN_EPS = 64e-5
DECAY = 0.6065306597126334
ALPHA, LIMIT = 1.702, 7.0
NEG = -1.0e30
NO_SLOT = 4096.0

F32 = mybir.dt.float32
I32 = mybir.dt.int32
U32 = mybir.dt.uint32
ALU = mybir.AluOpType
ACT = mybir.ActivationFunctionType
AX = mybir.AxisListType.X

C_ID, C_MASK, C_LVL, C_BLK, C_ONE, C_BLK64, C_IOTA, C_IOTAE, C_ANTI, C_EHOT, C_END = (
    0, 128, 384, 1280, 1408, 1536, 1664, 1728, 1760, 1888, 1921)
P_GMIX, P_GMEM, P_GFFN, P_MU, P_W0, P_A0, P_KK, P_KA, P_RK, P_GNG, P_GNB, P_END = (
    0, 8, 16, 24, 35, 38, 41, 44, 47, 50, 53, 56)


class Chain:

    def __init__(self, eng, sem, base=None):
        self.eng, self.sem, self.base, self.n = eng, sem, base, 0

    def __call__(self, ins):
        self.n += 1
        ins.then_inc(self.sem, 1)
        self.eng.wait_ge(self.sem, self.n if self.base is None else self.base + self.n)


def layer_kernel(nc, xT, x, memT, win, wmem, wout, params, consts, wlora, gup, relb, onehot,
                 wr, brouter, bgu, bdown, gffn, gfin, wgu, wdn, out, dbg=None, part=9):
    ctx = ExitStack()
    with ctx:
        def sb(name, cols, dt=F32, rows=P):
            return ctx.enter_context(nc.sbuf_tensor(name, [rows, cols], dt))

        def sem(name):
            return ctx.enter_context(nc.semaphore(name))

        bank = [ctx.enter_context(nc.psum_tensor(f"bank{i}", [P, 512], F32)) for i in range(8)]
        bias_dram = nc.dram_tensor("bias_rows", [NMOBA, 512], F32).ap()

        ring = sb("ring", NSLOT * SLOT)
        spare = sb("spare", 8192)
        cst = sb("cst", C_END)
        par = sb("par", P_END)
        bgu_s = sb("bgu_s", 2 * D)
        bdn_s = sb("bdn_s", D, rows=E)
        lora_s = sb("lora_s", 384)
        gup_s = sb("gup_s", 384)
        relb_s = sb("relb_s", 8, rows=E)
        wr_s = sb("wr_s", KT * E)
        br_s = sb("br_s", E, rows=1)
        xT_s = sb("xT_s", KT * T)
        qm_s = sb("qm_s", 8 * T)
        vn_s = sb("vn_s", TT * 384)
        mk_s = sb("mk_s", 2 * T)
        mv_s = sb("mv_s", TT * 256)
        toep = sb("toep", NMOBA * 256)
        raw = sb("raw", 11 * 257)
        mix = sb("mix", 11 * 256)
        stat = sb("stat", 160)
        npass_i = sb("npass_i", 4, I32)

        def slot(k, n=1):
            return ring[:, k * SLOT:(k + n) * SLOT]

        def c_(col, n=128):
            return cst[:, col:col + n]

        def pc(col, n=1):
            return par[:, col:col + n]

        def r3(ap, a):
            return ap.rearrange("p (a n) -> p a n", a=a)

        ident = c_(C_ID)
        ones = c_(C_ONE)
        blk = c_(C_BLK)
        hT = r3(xT_s[:, :], KT)
        wmem_s = r3(spare[:, 0:4096], KT)
        hmT = r3(spare[:, 4096:6144], KT)
        sq = spare[:, 6144:8192]
        rstd = mix[:, 0:256]
        ohot_s = mix[0:E, 512:1024]
        brow_s = mix[0:NMOBA, 1024:1536]
        win_s = [r3(slot(g), KT) for g in range(NG)]
        wout_s = ring[:, 0:4 * SLOT].rearrange("p (k n) -> p k n", k=KT)
        qk = r3(qm_s[:, 0:6 * T], 6)
        mq = r3(qm_s[:, 6 * T:8 * T], 2)
        vn = r3(vn_s[:, :], TT)
        mk = r3(mk_s[:, :], 2)
        mv = r3(mv_s[:, :], TT)
        toe = r3(toep[:, :], NMOBA)
        rw = r3(raw[:, :], 11)
        mx = r3(mix[:, :], 11)
        W3 = 3 * T
        RA = spare[:, 0:1536].rearrange("p (a c r n) -> p a c r n", a=NCT, c=2, r=2)
        kt = r3(spare[:, 1536:1536 + W3], NCT)
        bt = r3(spare[:, 2304:2304 + W3], NCT)
        sig_a = r3(spare[:, 3072:3072 + W3], NCT)
        gate = r3(spare[:, 3840:3840 + W3], NCT)
        kk_ = r3(spare[:, 4608:4608 + W3], NCT)
        bonus = r3(spare[:, 5376:5376 + W3], NCT)
        tmp = r3(spare[:, 6144:6144 + W3], NCT)
        tmp2 = r3(spare[:, 6912:6912 + W3], NCT)
        sw = r3(raw[:, 0:W3], NCT)
        cum = raw[:, 768:768 + 6 * 129].rearrange("p (a c n) -> p a c n", a=NCT, c=2)
        epos = raw[:, 1542:1542 + 6 * 129].rearrange("p (a c n) -> p a c n", a=NCT, c=2)
        eneg = r3(raw[:, 0:W3], NCT)
        rr = mx[:, 5:8, :]
        vv = mx[:, 8:11, :]
        kv = mx[:, 2:5, :]
        R0 = 6 * SLOT
        AT = ring[:, R0:R0 + 6144].rearrange("p (m n) -> p m n", m=NM)
        Tm = ring[:, R0 + 6144:R0 + 7680].rearrange("p (m n) -> p m n", m=NM)
        Em = ring[:, R0 + 7680:R0 + 9216].rearrange("p (m n) -> p m n", m=NM)
        Wm = ring[:, R0 + 9216:R0 + 10752].rearrange("p (m n) -> p m n", m=NM)
        Cm = ring[:, R0 + 10752:R0 + 12288].rearrange("p (m n) -> p m n", m=NM)
        Vn = xT_s[:, 0:768].rearrange("p (c n) -> p c n", c=2)
        Kn = xT_s[:, 768:1152]
        Bn = xT_s[:, 1152:1536]
        G_s = xT_s[:, 1536:1920]
        U_s = mix[:, 0:384]
        X1 = mix[:, 384:576].rearrange("p (a n) -> p a n", a=NCT)
        osb = r3(spare[:, 0:W3], NCT)
        yT_s = mix[:, 768:2816]
        yT = r3(yT_s, KT)
        prob = [ring[:, 4 * SLOT + 512 * i:4 * SLOT + 512 * i + 512] for i in range(2)]
        pT = [ring[:, 4 * SLOT + 1024 + 512 * i:4 * SLOT + 1536 + 512 * i] for i in range(2)]
        x2 = r3(spare[:, 0:2048], TT)
        hn = r3(spare[:, 2048:4096], TT)
        h2T = r3(spare[:, 4096:6144], KT)
        sqx = spare[:, 6144:7168]
        xn = r3(qm_s[:, :], TT)
        gffn_s = toep[:, 0:D]
        gfin_s = spare[:, 4096:5120]
        lg = r3(raw[:, 0:64], 2)
        v8 = raw[:, 64:80]
        i8 = raw[:, 80:96].bitcast(U32)
        i8f = raw[:, 96:112]
        e4 = raw[:, 112:120]
        MK = r3(raw[:, 128:192], 2)
        MW = r3(raw[:, 192:256], 2)
        RKs = r3(raw[:, 256:322], 2)
        ttmp = raw[:, 324:356]
        MWT = raw[0:E, 356:612]
        s4 = raw[:, 612:620]
        ctr = raw[:, 620:624]
        sel = raw[:, 640:768].rearrange("p (t s) -> p t s", t=TT)
        selw = raw[:, 768:1024].rearrange("p (t a s) -> p t a s", t=TT, a=2)
        selT = raw[:, 1024:1280]
        pick = raw[:, 1280:1344]
        h_s = raw[:, 1344:1856]
        xg_s = raw[:, 1856:2368]
        XTs = xT_s[:, 0:512]
        hTs = xT_s[:, 512:1024]
        y_s = xT_s[:, 1024:1536]
        g1 = qm_s[:, 0:512]
        u1 = qm_s[:, 512:1024]
        sg = qm_s[:, 1024:1536]
        tu = qm_s[:, 1536:2048]

        def kcol(ap, k):
            return ap[:, (k % 4) * P + (k // 4) * CAP:(k % 4) * P + (k // 4 + 1) * CAP]

        s_mem, s_wmem, s_cst, s_x, s_par, s_small = (sem("s_mem"), sem("s_wmem"), sem("s_cst"),
                                                     sem("s_x"), sem("s_par"), sem("s_small"))
        s_win = [sem(f"s_win{g}") for g in range(NG)]
        s_ohot, s_browd, s_toep, s_flip, s_flipe = (sem("s_ohot"), sem("s_browd"), sem("s_toep"),
                                                    sem("s_flip"), sem("s_flipe"))
        s_wout, s_xn, s_gffn, s_gfin = sem("s_wout"), sem("s_xn"), sem("s_gffn"), sem("s_gfin")
        s_slot = [sem(f"s_slot{k}") for k in range(NSLOT)]
        s_out = sem("s_out")
        s_sq, s_ss, s_ms, s_rt, s_h = (sem("s_sq"), sem("s_ss"), sem("s_ms"), sem("s_rt"), sem("s_h"))
        s_bps, s_brow = sem("s_bps"), sem("s_brow")
        s_proj, s_pev = sem("s_proj"), sem("s_pev")
        s_pad, s_mix, s_tanh, s_lora, s_lsig, s_lg = (sem("s_pad"), sem("s_mix"), sem("s_tanh"),
                                                      sem("s_lora"), sem("s_lsig"), sem("s_lg"))
        s_kksq, s_kkn, s_kkms, s_kkrt = sem("s_kksq"), sem("s_kkn"), sem("s_kkms"), sem("s_kkrt")
        s_cum, s_exp = sem("s_cum"), sem("s_exp")
        s_rkp, s_rks, s_rwp = sem("s_rkp"), sem("s_rks"), sem("s_rwp")
        s_tp, s_tpe = sem("s_tp"), sem("s_tpe")
        s_A, s_Ae = sem("s_A"), sem("s_Ae")
        s_C, s_T1, s_TE = sem("s_C"), sem("s_T1"), sem("s_TE")
        s_W, s_We, s_Y = sem("s_W"), sem("s_We"), sem("s_Y")
        s_sol, s_sole = sem("s_sol"), sem("s_sole")
        s_ops, s_osb, s_gm, s_gc, s_gv, s_gvm, s_grt, s_yr = (
            sem("s_ops"), sem("s_osb"), sem("s_gm"), sem("s_gc"), sem("s_gv"), sem("s_gvm"),
            sem("s_grt"), sem("s_yr"))
        s_S, s_Ssb, s_Pe, s_Pn, s_PT, s_PTe, s_O, s_Oe = (
            sem("s_S"), sem("s_Ssb"), sem("s_Pe"), sem("s_Pn"), sem("s_PT"), sem("s_PTe"),
            sem("s_O"), sem("s_Oe"))
        s_op, s_x2, s_sqx, s_m2, s_r2, s_hn = (sem("s_op"), sem("s_x2"), sem("s_sqx"), sem("s_m2"),
                                               sem("s_r2"), sem("s_hn"))
        s_hT2, s_hT2e, s_lgp, s_top, s_tope, s_mk, s_rank, s_np = (
            sem("s_hT2"), sem("s_hT2e"), sem("s_lgp"), sem("s_top"), sem("s_tope"), sem("s_mk"),
            sem("s_rank"), sem("s_np"))
        s_mwt, s_mwte, s_bd, s_bde = sem("s_mwt"), sem("s_mwte"), sem("s_bd"), sem("s_bde")
        m_used, m_sel, m_xg, m_xgs, m_xt, m_xts, m_pick, m_gu, m_g, m_sig, m_h = (
            sem("m_used"), sem("m_sel"), sem("m_xg"), sem("m_xgs"), sem("m_xt"), sem("m_xts"),
            sem("m_pick"), sem("m_gu"), sem("m_g"), sem("m_sig"), sem("m_h"))
        m_selw, m_st, m_sts, m_ht, m_hts, m_y, m_ys, m_sc, m_acc = (
            sem("m_selw"), sem("m_st"), sem("m_sts"), sem("m_ht"), sem("m_hts"), sem("m_y"),
            sem("m_ys"), sem("m_sc"), sem("m_acc"))
        s_dve, s_act, s_dvl, s_f = sem("s_dve"), sem("s_act"), sem("s_dvl"), sem("s_f")
        f_sc, f_sq, f_ms, f_rt, f_o = sem("f_sc"), sem("f_sq"), sem("f_ms"), sem("f_rt"), sem("f_o")
        s_pool = sem("s_pool")
        s_dbg = sem("s_dbg")

        jobs = [("moba", h) for h in range(NMOBA)] + [("mem", h) for h in range(NMEM)]
        NJ = len(jobs)

        def job(j):
            kind, h = jobs[j]
            b = HD * (h % 2)
            if kind == "moba":
                return (qk[b:b + HD, h // 2, :], qk[b:b + HD, 3 + h // 2, :], b, 128,
                        h // 2, lambda m: vn[:, m, h * HD:(h + 1) * HD])
            return (mq[b:b + HD, h // 2, :], mk[b:b + HD, h // 2, :], b, 256,
                    6 + h // 2, lambda m: mv[:, m, h * HD:(h + 1) * HD])

        block = ctx.enter_context(nc.Block())

        @block.sync
        def _(sp):
            sp.dma_start(hmT, memT).then_inc(s_mem, 16)
            sp.dma_start(cst[:, :], consts).then_inc(s_cst, 16)
            sp.dma_start(par[:, :], params).then_inc(s_par, 16)
            sp.dma_start(wmem_s, wmem).then_inc(s_wmem, 16)
            sp.dma_start(hT, xT).then_inc(s_x, 16)
            for g in range(NG):
                sp.dma_start(win_s[g], win[g]).then_inc(s_win[g], 16)
            sp.wait_ge(s_brow, 2)
            sp.dma_start(bias_dram, brow_s).then_inc(s_browd, 16)
            sp.wait_ge(s_browd, 16)
            src = bass.AP(tensor=bias_dram.tensor, offset=0,
                          ap=[[1, P], [512, NMOBA], [1, 256]])
            sp.dma_start(toe, src).then_inc(s_toep, 16)
            sp.wait_ge(s_proj, 6)
            sp.dma_start(wout_s, wout.rearrange("(k p) n -> p k n", p=P)).then_inc(s_wout, 16)
            if part < 3:
                return
            sp.wait_ge(s_Oe, NJ)
            sp.dma_start(xn, x.rearrange("(t p) d -> p t d", p=P)).then_inc(s_xn, 16)
            sp.dma_start(gffn_s, gffn.partition_broadcast(P)).then_inc(s_gffn, 16)
            if part < 5:
                return

            def load(e, k):
                if k < 8:
                    return sp.dma_start(slot(k), wgu[e, k * P:(k + 1) * P, :])
                return sp.dma_start(r3(slot(k), 2),
                                    wdn[e, (k - 8) * 256:(k - 7) * 256, :].rearrange(
                                        "(c p) n -> p c n", p=P))
            sp.wait_ge(s_Oe, NJ)
            for k in (4, 5):
                load(0, k).then_inc(s_slot[k], 16)
            sp.wait_ge(s_ops, 2)
            for k in range(6, NSLOT):
                load(0, k).then_inc(s_slot[k], 16)
            sp.wait_ge(s_op, 4)
            for k in range(4):
                load(0, k).then_inc(s_slot[k], 16)

            def wait_free(k, done):
                if k == 7:
                    sp.wait_ge(m_gu, done + 1)
                elif k == 11:
                    sp.wait_ge(m_y, done + 1)
                else:
                    sp.wait_ge(m_used, done * (NSLOT - 2) + (k + 1 if k < 7 else k))

            with sp.Fori(1, E) as e:
                for k in range(NSLOT):
                    wait_free(k, e - 1)
                    load(e, k).then_inc(s_slot[k], 16)
            sp.wait_ge(s_np, 1)
            npass = sp.value_load(npass_i[0:1, 0:1], min_val=1, max_val=T // CAP)
            with sp.If(npass > 1):
                with sp.Fori(1, npass) as c:
                    with sp.Fori(0, E) as e:
                        for k in range(NSLOT):
                            wait_free(k, c * E + e - 1)
                            load(e, k).then_inc(s_slot[k], 16)
            sp.dma_start(gfin_s, gfin.partition_broadcast(P)).then_inc(s_gfin, 16)
            for t in range(TT):
                sp.wait_ge(f_o, t + 1)
                sp.dma_start(out.rearrange("(t p) d -> p t d", p=P)[:, t, :], hn[:, t, :]).then_inc(s_out, 16)
            sp.wait_ge(s_out, 16 * TT)

        @block.gpsimd
        def _(pool):
            if part < 2:
                return
            mask = lambda l: c_(C_LVL + 128 * (l - 1)).unsqueeze(1).to_broadcast([P, NM, P])
            for l in range(1, 8):
                pool.wait_ge(s_Ae, NM)
                if l == 2:
                    pool.wait_ge(s_TE, NCT)
                if l >= 3:
                    pool.wait_ge(s_W, NCT * (l - 2))
                pool.tensor_tensor(Cm, AT[:, :, 0:P], mask(l), ALU.mult).then_inc(s_C, 1)

        @block.scalar
        def _(act):
            link = Chain(act, s_act)
            act.dma_start(lora_s[:, :], wlora).then_inc(s_small, 16)
            act.dma_start(gup_s[:, :], gup).then_inc(s_small, 16)
            act.dma_start(relb_s[:, 0:NMOBA], relb).then_inc(s_ohot, 16)
            act.dma_start(ohot_s, onehot).then_inc(s_ohot, 16)
            act.dma_start(wr_s[:, :], wr).then_inc(s_small, 16)
            act.dma_start(br_s[:, :], brouter).then_inc(s_small, 16)
            act.wait_ge(s_pad, 2)
            act.dma_start(bgu_s[0:E, :], bgu).then_inc(s_small, 16)
            act.dma_start(bdn_s[:, :], bdown).then_inc(s_small, 16)
            for n, (src, s) in enumerate(((hmT, s_mem), (hT, s_x))):
                act.wait_ge(s, 16)
                if n:
                    act.wait_ge(s_ss, 1)
                act.activation(r3(sq, KT), src, ACT.Square).then_inc(s_sq, 1)
                act.wait_ge(s_ms, n + 1)
                act.activation(rstd, rstd, ACT.Sqrt).then_inc(s_rt, 1)
            for u in range(13):
                act.wait_ge(s_proj, u + 1)
                ps = bank[u % 3]
                g = u - 2
                if u == 0:
                    act.activation(mk_s[:, :], ps[:, :], ACT.Copy).then_inc(s_pev, 1)
                elif u == 1:
                    act.activation(mv_s[:, :], ps[:, :], ACT.Copy).then_inc(s_pev, 1)
                elif g < 5:
                    if g == 0:
                        act.wait_ge(s_pad, 2)
                    act.activation(rw[:, 2 * g:2 * g + 2, 1:257], r3(ps[:, :], 2), ACT.Copy).then_inc(s_pev, 1)
                elif g == 5:
                    act.activation(rw[:, 10, 1:257], ps[:, 0:256], ACT.Copy).then_inc(s_pev, 1)
                    act.activation(qk[:, 0, :], ps[:, 256:512], ACT.Copy).then_inc(s_pev, 1)
                elif g < 8:
                    act.activation(qk[:, 2 * g - 11:2 * g - 9, :], r3(ps[:, :], 2), ACT.Copy).then_inc(s_pev, 1)
                elif g == 8:
                    act.activation(qk[:, 5, :], ps[:, 0:256], ACT.Copy).then_inc(s_pev, 1)
                    act.activation(mq[:, 0, :], ps[:, 256:512], ACT.Copy).then_inc(s_pev, 1)
                elif g == 9:
                    act.activation(vn[:, :, 0:256], r3(ps[:, :], 2), ACT.Copy).then_inc(s_pev, 1)
                else:
                    act.activation(mq[:, 1, :], ps[:, 0:256], ACT.Copy).then_inc(s_pev, 1)
                    act.activation(vn[:, :, 256:384], r3(ps[:, 256:512], 2), ACT.Copy).then_inc(s_pev, 1)
                if g == 2:
                    act.wait_ge(s_mix, 1)
                    act.activation(mx[0:64, 0, :], mx[0:64, 0, :], ACT.Tanh).then_inc(s_tanh, 1)
                    act.activation(mx[:, 1, :], mx[:, 1, :], ACT.Sigmoid).then_inc(s_tanh, 1)
                if g == 7:
                    act.wait_ge(s_lora, 1)
                    act.wait_ge(s_mix, 6)
                    zw = [bank[3][:, 0:256], bank[3][:, 256:512], bank[4][:, 0:256]]
                    za = [bank[5][:, 0:256], bank[5][:, 256:512], bank[6][:, 0:256]]
                    for a in range(NCT):
                        act.activation(sw[:, a, :], zw[a], ACT.Sigmoid, bias=pc(P_W0 + a)).then_inc(s_lsig, 1)
                    for a in range(NCT):
                        act.activation(sig_a[:, a, :], za[a], ACT.Sigmoid, bias=pc(P_A0 + a)).then_inc(s_lsig, 1)
                    act.activation(gate[:, 0:2, :], r3(bank[7][:, :], 2), ACT.Copy).then_inc(s_lg, 1)
                    act.activation(gate[:, 2, :], bank[4][:, 256:512], ACT.Copy).then_inc(s_lg, 1)
            act.wait_ge(s_kkms, 1)
            act.activation(tmp2, tmp2, ACT.Sqrt).then_inc(s_kkrt, 1)
            act.wait_ge(s_cum, 1)
            for a in range(NCT):
                for c in range(2):
                    m = 2 * a + c
                    act.activation(epos[:, a, c, :], cum[:, a, c, :], ACT.Exp,
                                   bias=stat[:, m:m + 1], scale=-DECAY).then_inc(s_exp, 1)
                    act.activation(eneg[:, a, c * CH:(c + 1) * CH], cum[:, a, c, 1:129], ACT.Exp,
                                   bias=stat[:, 6 + m:7 + m], scale=DECAY).then_inc(s_exp, 1)
            if part < 2:
                return
            for n, dst in enumerate((Vn[:, 0, :], Vn[:, 1, :], Kn, Bn)):
                act.wait_ge(s_tp, n + 1)
                act.activation(dst, bank[n][:, 0:384], ACT.Copy).then_inc(s_tpe, 1)
            for l in range(2, 8):
                for g in range(NCT):
                    n = NCT * (l - 2) + g
                    act.wait_ge(s_W, n + 1)
                    act.activation(Wm[:, 4 * g:4 * g + 4, :], r3(bank[n % 2][:, :], 4), ACT.Copy).then_inc(s_We, 1)
            act.wait_ge(s_gvm, 1)
            act.activation(tmp, tmp, ACT.Sqrt).then_inc(s_grt, 1)
            if part < 3:
                return
            for j in range(NJ):
                w0 = job(j)[3]
                act.wait_ge(s_Ssb, j + 1)
                pr = prob[j % 2]
                st = 16 * (j % 2)
                for q, (lo, hi) in enumerate(((0, w0), (w0, w0 + 256))):
                    act.activation(pr[:, lo:hi], pr[:, lo:hi], ACT.Exp, bias=stat[:, 32 + st + q:33 + st + q],
                                   accum_out=stat[:, 36 + st + q:37 + st + q]).then_inc(s_Pe, 1)
                act.wait_ge(s_PT, j + 1)
                w = w0 + 256
                act.activation(pT[j % 2][:, 0:w], bank[2 + j % 2][:, 0:w], ACT.Copy).then_inc(s_PTe, 1)
                act.wait_ge(s_O, j + 1)
                b, ot = job(j)[2], job(j)[4]
                act.activation(yT[b:b + HD, ot, :], bank[4 + j % 2][b:b + HD, 0:256], ACT.Copy).then_inc(s_Oe, 1)
            if part < 4:
                return
            act.wait_ge(s_x2, 4)
            for t in range(TT):
                act.activation(sqx, x2[:, t, :], ACT.Square, accum_out=stat[:, 64 + t:65 + t]).then_inc(s_sqx, 1)
                act.wait_ge(s_sqx, t + 1)
            act.wait_ge(s_m2, 1)
            act.activation(stat[:, 66:68], stat[:, 66:68], ACT.Sqrt).then_inc(s_r2, 1)
            for t in range(TT):
                act.wait_ge(s_top, t + 1)
                act.activation(e4[:, 4 * t:4 * t + 4], v8[:, 8 * t:8 * t + 4], ACT.Exp,
                               bias=s4[:, t:t + 1], accum_out=s4[:, 2 + t:3 + t]).then_inc(s_tope, 1)
            if part < 5:
                return

            def gathered(n):
                act.wait_ge(m_xg, n + 1)
                act.activation(xg_s, bank[6][:, :], ACT.Copy).then_inc(m_xgs, 1)

            def transposed(n):
                act.wait_ge(m_xt, n + 1)
                act.activation(XTs, bank[6][:, :], ACT.Copy).then_inc(m_xts, 1)

            gathered(0)
            transposed(0)
            act.wait_ge(s_np, 1)
            npass = act.value_load(npass_i[0:1, 0:1], min_val=1, max_val=T // CAP)
            with act.Fori(0, npass) as c:
                with act.Fori(0, E) as e:
                    n = c * E + e
                    act.wait_ge(m_g, n + 1)
                    act.activation(sg, g1, ACT.Sigmoid, scale=ALPHA).then_inc(m_sig, 1)
                    gathered(n + 1)
                    act.wait_ge(m_st, n + 1)
                    act.activation(selT, bank[7][:, 0:256], ACT.Copy).then_inc(m_sts, 1)
                    transposed(n + 1)
                    act.wait_ge(m_ht, n + 1)
                    act.activation(hTs, bank[7][:, :], ACT.Copy).then_inc(m_hts, 1)
                    act.wait_ge(m_y, n + 1)
                    act.activation(y_s, bank[2][:, :], ACT.Copy).then_inc(m_ys, 1)
            act.wait_ge(f_sq, 4)
            for t in range(TT):
                act.activation(sqx, x2[:, t, :], ACT.Square, accum_out=stat[:, 80 + t:81 + t]).then_inc(f_ms, 1)
                act.wait_ge(f_ms, t + 1)
            act.wait_ge(f_sq, 5)
            act.activation(stat[:, 82:84], stat[:, 82:84], ACT.Sqrt).then_inc(f_rt, 1)

        @block.vector
        def _(dve):
            link = Chain(dve, s_dve)
            dve.memset(rw[:, :, 0:1], 0.0).then_inc(s_pad, 1)
            dve.memset(bgu_s[:, :], 0.0).then_inc(s_pad, 1)
            dve.wait_ge(s_bps, 1)
            dve.tensor_copy(brow_s[:, 0:256], bank[3][0:NMOBA, 0:256]).then_inc(s_brow, 1)
            dve.memset(brow_s[:, 256:512], NEG).then_inc(s_brow, 1)
            for n, (h, g) in enumerate(((hmT, P_GMEM), (hT, P_GMIX))):
                dve.wait_ge(s_ss, n + 1)
                dve.tensor_scalar(rstd, bank[7][:, 0:256], 1.0 / D, EPS, ALU.mult, ALU.add).then_inc(s_ms, 1)
                dve.wait_ge(s_rt, n + 1)
                dve.wait_ge(s_par, 16)
                link(dve.reciprocal(rstd, rstd))
                for k in range(KT):
                    ins = dve.scalar_tensor_tensor(out=h[:, k, :], in0=h[:, k, :], scalar=pc(g + k), in1=rstd,
                                                   op0=ALU.mult, op1=ALU.mult)
                    ins.then_inc(s_h, 1)
                dve.wait_ge(s_h, KT * (n + 1))
            dve.wait_ge(s_pad, 2)
            dve.wait_ge(s_browd, 16)
            for u in range(6):
                lo, hi = 2 * u, min(2 * u + 2, 11)
                if u == 3:
                    dve.wait_ge(s_flip, 1)
                    for b in range(3):
                        dve.tensor_copy(toep[:, b * 512:(b + 1) * 512], bank[4 + b][:, :]).then_inc(s_flipe, 1)
                dve.wait_ge(s_pev, u + 3)
                link(dve.tensor_tensor(mx[:, lo:hi, :], rw[:, lo:hi, 0:256], rw[:, lo:hi, 1:257], ALU.subtract))
                for i in range(lo, hi):
                    ins = dve.scalar_tensor_tensor(out=mx[:, i, :], in0=mx[:, i, :], scalar=pc(P_MU + i),
                                                   in1=rw[:, i, 1:257], op0=ALU.mult, op1=ALU.add)
                    if i < hi - 1:
                        link(ins)
                    else:
                        ins.then_inc(s_mix, 1)
            dve.wait_ge(s_mix, 6)
            dve.wait_ge(s_proj, 2)
            for a in range(NCT):
                link(dve.tensor_scalar(kk_[:, a, :], kv[:, a, :], pc(P_KK + a), None, ALU.mult))
            dve.tensor_tensor(tmp, kk_, kk_, ALU.mult).then_inc(s_kksq, 1)
            dve.wait_ge(s_lsig, 3)
            link(dve.memset(cum[:, :, :, 0:1], 0.0))
            for a in range(NCT):
                for c in range(2):
                    link(dve.tensor_tensor_scan(cum[:, a, c, 1:129], c_(C_ONE), sw[:, a, c * CH:(c + 1) * CH],
                                                0.0, ALU.mult, ALU.add))
            cmid = raw[:, 768:768 + 6 * 129].rearrange("p (m n) -> p m n", m=6)[:, :, 64]
            link(dve.tensor_scalar(stat[:, 0:6], cmid, DECAY, None, ALU.mult))
            dve.tensor_scalar(stat[:, 6:12], cmid, -DECAY, None, ALU.mult).then_inc(s_cum, 1)
            dve.wait_ge(s_kkn, 1)
            link(dve.tensor_copy(tmp2[:, 0:2, :], r3(bank[3][:, :], 2)))
            dve.tensor_copy(tmp2[:, 2, :], bank[4][:, 0:256]).then_inc(s_kkms, 1)
            dve.wait_ge(s_kkrt, 1)
            link(dve.tensor_scalar(tmp2, tmp2, 1e-12, None, ALU.max))
            link(dve.reciprocal(tmp2, tmp2))
            link(dve.tensor_tensor(kk_, kk_, tmp2, ALU.mult))
            dve.wait_ge(s_lsig, 6)
            for a in range(NCT):
                link(dve.tensor_scalar(tmp[:, a, :], sig_a[:, a, :], 1.0, pc(P_KA + a), ALU.subtract, ALU.mult))
            link(dve.scalar_tensor_tensor(out=kv, in0=tmp, scalar=1.0, in1=kv, op0=ALU.add, op1=ALU.mult))
            for a in range(NCT):
                ins = dve.scalar_tensor_tensor(out=tmp2[:, a, :], in0=kv[:, a, :], scalar=pc(P_RK + a), in1=rr[:, a, :],
                                               op0=ALU.mult, op1=ALU.mult)
                ins.then_inc(s_rkp, 1)
            dve.wait_ge(s_rks, 1)
            link(dve.tensor_tensor(bonus[:, 0:2, :], r3(bank[5][:, :], 2), vv[:, 0:2, :], ALU.mult))
            link(dve.tensor_tensor(bonus[:, 2, :], bank[6][:, 0:256], vv[:, 2, :], ALU.mult))
            dve.wait_ge(s_exp, 12)
            link(dve.tensor_tensor(tmp, kk_, sig_a, ALU.mult))
            link(dve.tensor_tensor(bt, tmp, eneg, ALU.mult))
            link(dve.tensor_tensor(kt, kv, eneg, ALU.mult))
            for a in range(NCT):
                link(dve.tensor_tensor(RA[:, a, :, 1, :], r3(rr[:, a, :], 2), epos[:, a, :, 1:129], ALU.mult))
                link(dve.scalar_tensor_tensor(out=RA[:, a, :, 0, :], in0=r3(kk_[:, a, :], 2), scalar=-1.0,
                                              in1=epos[:, a, :, 0:128], op0=ALU.mult, op1=ALU.mult))
            link(dve.reciprocal(stat[:, 12:15], epos[:, :, 1, 0]))
            dve.tensor_tensor(stat[:, 12:15], stat[:, 12:15], epos[:, :, 0, 128], ALU.mult).then_inc(s_rwp, 1)
            if part < 2:
                return
            for m in range(NM):
                dve.wait_ge(s_A, m + 1)
                dve.tensor_tensor(AT[:, m, :].rearrange("p (a n) -> p a n", a=2),
                                  r3(bank[4 + m % 4][:, :], 2),
                                  c_(C_MASK, 256).unsqueeze(1).to_broadcast([P, 2, 256]), ALU.mult).then_inc(s_Ae, 1)
            dve.wait_ge(s_C, 1)
            dve.wait_ge(s_T1, NCT)
            idb = ident.unsqueeze(1).to_broadcast([P, 4, P])
            for g in range(NCT):
                m4 = slice(4 * g, 4 * g + 4)
                link(dve.tensor_tensor(Em[:, m4, :], Cm[:, m4, :], idb, ALU.add))
                dve.tensor_tensor(Tm[:, m4, :], r3(bank[4 + g][:, :], 4), idb, ALU.add).then_inc(s_TE, 1)
            for l in range(2, 8):
                for g in range(NCT):
                    m4 = slice(4 * g, 4 * g + 4)
                    dve.wait_ge(s_Y, NCT * (l - 2) + g + 1)
                    dve.wait_ge(s_TE, NCT * (l - 2) + g + 1)
                    if l < 7:
                        link(dve.tensor_tensor(Tm[:, m4, :], r3(bank[2 + 2 * g][:, :], 4), Tm[:, m4, :], ALU.add))
                    dve.tensor_tensor(Em[:, m4, :], r3(bank[3 + 2 * g][:, :], 4), Em[:, m4, :], ALU.add).then_inc(s_TE, 1)
            for c in range(2):
                dve.wait_ge(s_sol, 3 * c + 1)
                Gv = G_s.rearrange("p (a h n) -> p a h n", a=NCT, h=2)
                link(dve.tensor_copy(Gv[:, :, 0, :], r3(bank[0][:, 0:192], NCT)))
                dve.tensor_copy(Gv[:, :, 1, :], r3(bank[3][:, 0:192], NCT)).then_inc(s_sole, 1)
                dve.wait_ge(s_sol, 3 * c + 2)
                if c:
                    dve.wait_ge(s_ops, 1)
                dve.tensor_copy(U_s, bank[1][:, 0:384]).then_inc(s_sole, 1)
                if c == 0:
                    dve.wait_ge(s_sol, 3)
                    for a in range(NCT):
                        for h in range(2):
                            b = HD * h
                            ins = dve.tensor_scalar(X1[b:b + HD, a, :], bank[2][b:b + HD, a * P + b:a * P + b + HD],
                                                    stat[b:b + HD, 12 + a:13 + a], None, ALU.mult)
                            if a < NCT - 1 or h == 0:
                                link(ins)
                            else:
                                ins.then_inc(s_sole, 1)
            dve.wait_ge(s_ops, 2)
            link(dve.tensor_copy(osb[:, 0:2, :], r3(bank[4][:, :], 2)))
            dve.tensor_copy(osb[:, 2, :], bank[5][:, 0:256]).then_inc(s_osb, 1)
            dve.wait_ge(s_gm, 1)
            dve.wait_ge(s_osb, 1)
            link(dve.tensor_tensor(osb[:, 0:2, :], osb[:, 0:2, :], r3(bank[6][:, :], 2), ALU.subtract))
            link(dve.tensor_tensor(osb[:, 2, :], osb[:, 2, :], bank[7][:, 0:256], ALU.subtract))
            dve.tensor_tensor(tmp, osb, osb, ALU.mult).then_inc(s_gc, 1)
            dve.wait_ge(s_gv, 1)
            link(dve.tensor_scalar(tmp[:, 0:2, :], r3(bank[6][:, :], 2), GN_EPS, None, ALU.add))
            dve.tensor_scalar(tmp[:, 2, :], bank[7][:, 0:256], GN_EPS, None, ALU.add).then_inc(s_gvm, 1)
            dve.wait_ge(s_grt, 1)
            link(dve.reciprocal(tmp, tmp))
            link(dve.tensor_tensor(osb, osb, tmp, ALU.mult))
            for a in range(NCT):
                link(dve.tensor_scalar(osb[:, a, :], osb[:, a, :], pc(P_GNG + a), pc(P_GNB + a), ALU.mult, ALU.add))
            link(dve.tensor_tensor(osb, osb, bonus, ALU.add))
            dve.wait_ge(s_lg, 2)
            for a in range(NCT):
                dve.tensor_tensor(yT[:, 3 + a, :], osb[:, a, :], gate[:, a, :], ALU.mult).then_inc(s_yr, 1)
            if part < 3:
                return
            dve.wait_ge(s_flipe, 3)
            for j in range(NJ):
                w0 = job(j)[3]
                w = w0 + 256
                pr = prob[j % 2]
                st = 16 * (j % 2)
                ps = bank[j % 2]
                dve.wait_ge(s_S, j + 1)
                if j >= 2:
                    dve.wait_ge(s_PT, j - 1)
                if j < NMOBA:
                    link(dve.scalar_tensor_tensor(out=pr[:, 0:128], in0=ps[:, 0:128], scalar=HD ** -0.5,
                                                  in1=toe[:, j, 128:256], op0=ALU.mult, op1=ALU.add))
                    link(dve.scalar_tensor_tensor(out=pr[:, 128:384], in0=ps[:, 128:384], scalar=HD ** -0.5,
                                                  in1=toe[:, j, :], op0=ALU.mult, op1=ALU.add))
                else:
                    link(dve.tensor_scalar(pr[:, 0:w], ps[:, 0:w], HD ** -0.5, None, ALU.mult))
                mxc = stat[:, 34 + st:36 + st]
                link(dve.tensor_reduce(mxc[:, 0:1], pr[:, 0:w0], AX, ALU.max))
                link(dve.tensor_reduce(mxc[:, 1:2], pr[:, w0:w], AX, ALU.max))
                dve.tensor_scalar(stat[:, 32 + st:34 + st], mxc, -1.0, None, ALU.mult).then_inc(s_Ssb, 1)
                dve.wait_ge(s_Pe, 2 * j + 2)
                link(dve.reciprocal(stat[:, 38 + st:40 + st], stat[:, 36 + st:38 + st]))
                link(dve.tensor_scalar(pr[:, 0:w0], pr[:, 0:w0], stat[:, 38 + st:39 + st], None, ALU.mult))
                dve.tensor_scalar(pr[:, w0:w], pr[:, w0:w], stat[:, 39 + st:40 + st], None, ALU.mult).then_inc(s_Pn, 1)
            if part < 4:
                return
            dve.wait_ge(s_xn, 16)
            for n in range(4):
                t, h = n // 2, n % 2
                dve.wait_ge(s_op, n + 1)
                dve.tensor_tensor(x2[:, t, h * 512:h * 512 + 512], bank[n][:, :], xn[:, t, h * 512:h * 512 + 512],
                                  ALU.add).then_inc(s_x2, 1)
            dve.wait_ge(s_sqx, 2)
            dve.tensor_scalar(stat[:, 66:68], stat[:, 64:66], 1.0 / D, EPS, ALU.mult, ALU.add).then_inc(s_m2, 1)
            dve.wait_ge(s_r2, 1)
            link(dve.reciprocal(stat[:, 66:68], stat[:, 66:68]))
            dve.wait_ge(s_gffn, 16)
            for t in range(TT):
                dve.scalar_tensor_tensor(out=hn[:, t, :], in0=x2[:, t, :], scalar=stat[:, 66 + t:67 + t],
                                         in1=gffn_s, op0=ALU.mult, op1=ALU.mult).then_inc(s_hn, 1)
            for b in range(4):
                dve.wait_ge(s_hT2, b + 1)
                dve.tensor_copy(h2T[:, 2 * b:2 * b + 2, :], r3(bank[4 + b][:, :], 2)).then_inc(s_hT2e, 1)
            dve.wait_ge(s_lgp, 1)
            link(dve.tensor_copy(lg, r3(bank[0][:, 0:64], 2)))
            link(dve.memset(MK, 0.0))
            link(dve.memset(MW, 0.0))
            for t in range(TT):
                link(dve.max(v8[:, 8 * t:8 * t + 8], lg[:, t, :]))
                link(dve.max_index(i8[:, 8 * t:8 * t + 8], v8[:, 8 * t:8 * t + 8], lg[:, t, :]))
                link(dve.tensor_copy(i8f[:, 8 * t:8 * t + 8], i8[:, 8 * t:8 * t + 8]))
                dve.tensor_scalar(s4[:, t:t + 1], v8[:, 8 * t:8 * t + 1], -1.0, None, ALU.mult).then_inc(s_top, 1)
            iota_e = c_(C_IOTAE, E)
            for t in range(TT):
                for k in range(TOPK):
                    ins = dve.scalar_tensor_tensor(out=MK[:, t, :], in0=iota_e, scalar=i8f[:, 8 * t + k:8 * t + k + 1],
                                                   in1=MK[:, t, :], op0=ALU.is_equal, op1=ALU.add)
                    if k < TOPK - 1:
                        link(ins)
                    else:
                        ins.then_inc(s_mk, 1)
            dve.wait_ge(s_tope, 2)
            link(dve.reciprocal(s4[:, 2:4], s4[:, 2:4]))
            for t in range(TT):
                link(dve.tensor_scalar(e4[:, 4 * t:4 * t + 4], e4[:, 4 * t:4 * t + 4], s4[:, 2 + t:3 + t], None, ALU.mult))
                for k in range(TOPK):
                    link(dve.tensor_scalar(ttmp, iota_e, i8f[:, 8 * t + k:8 * t + k + 1],
                                           e4[:, 4 * t + k:4 * t + k + 1], ALU.is_equal, ALU.mult))
                    link(dve.tensor_tensor(MW[:, t, :], MW[:, t, :], ttmp, ALU.add))
            dve.wait_ge(s_rank, 1)
            dve.wait_ge(s_mk, 2)
            link(dve.scalar_tensor_tensor(out=RKs[:, :, 0:E], in0=r3(bank[1][:, 0:64], 2), scalar=NO_SLOT, in1=MK,
                                          op0=ALU.add, op1=ALU.mult))
            link(dve.tensor_scalar(RKs[:, :, 0:E], RKs[:, :, 0:E], -NO_SLOT, None, ALU.add))
            link(dve.tensor_scalar(RKs[:, :, E:E + 1], RKs[:, :, 0:1], -float(CAP), None, ALU.add))
            link(dve.tensor_reduce(ctr[0:1, 0:1], bank[2][0:1, 0:E], AX, ALU.max))
            link(dve.tensor_scalar(ctr[0:1, 1:2], ctr[0:1, 0:1], CAP + 0.5, 1.0, ALU.is_gt, ALU.add))
            for k in range(2, T // CAP):
                link(dve.scalar_tensor_tensor(out=ctr[0:1, 1:2], in0=ctr[0:1, 0:1], scalar=k * CAP + 0.5,
                                              in1=ctr[0:1, 1:2], op0=ALU.is_gt, op1=ALU.add))
            dve.tensor_copy(npass_i[0:1, 0:1], ctr[0:1, 1:2]).then_inc(s_np, 1)
            dve.wait_ge(s_mwt, 1)
            dve.tensor_copy(MWT, bank[3][0:E, 0:256]).then_inc(s_mwte, 1)
            for n in range(4):
                t, h = n // 2, n % 2
                dve.wait_ge(s_bd, n + 1)
                dve.tensor_tensor(x2[:, t, h * 512:h * 512 + 512], bank[2 + n][:, :],
                                  x2[:, t, h * 512:h * 512 + 512], ALU.add).then_inc(m_acc, 1)
            if part < 5:
                return
            link(dve.memset(xT_s[:, 512:1536], 0.0))
            dve.memset(y_s, 0.0).then_inc(m_ys, 1)
            dve.memset(selT, 0.0).then_inc(m_sts, 1)
            dve.wait_ge(m_ys, 1)
            dve.wait_ge(m_sts, 1)
            iota = c_(C_IOTA, CAP)

            def pick_expert(e):
                col = cst[:, bass.ds(e + C_EHOT, 1)]
                dve.tensor_copy(pick, col.to_broadcast([P, CAP])).then_inc(m_pick, 1)

            def select(e):
                for t in range(TT):
                    ins = dve.tensor_scalar(sel[:, t, :], iota, RKs[:, t, :][:, bass.ds(e, 1)], None, ALU.is_equal)
                    ins.then_inc(m_sel, 1)

            select(0)
            pick_expert(0)
            dve.wait_ge(s_np, 1)
            dve.wait_ge(m_sel, 2)
            npass = dve.value_load(npass_i[0:1, 0:1], min_val=1, max_val=T // CAP)
            NB = 4
            with dve.Fori(0, npass) as c:
                with dve.Fori(0, E) as e:
                    n = c * E + e
                    lk = Chain(dve, s_dvl, base=n * NB + c)
                    dve.wait_ge(m_xg, n + 1)
                    for t in range(TT):
                        dve.tensor_scalar(selw[:, t, :, :], iota.unsqueeze(1).to_broadcast([P, 2, CAP]),
                                          RKs[:, t, :][:, bass.ds(e, 1)], MW[:, t, :][:, bass.ds(e, 1)],
                                          ALU.is_equal, ALU.mult).then_inc(m_selw, 1)
                    select(e + 1)
                    dve.wait_ge(m_gu, n + 1)
                    pair = [bank[b][:, :].rearrange("p (f g) -> p g f", g=2) for b in range(2)]
                    for b in range(2):
                        ins = dve.tensor_scalar(g1[:, b * 256:(b + 1) * 256], pair[b][:, 0, :], LIMIT, None, ALU.min)
                        if b:
                            ins.then_inc(m_g, 1)
                    for b in range(2):
                        ins = dve.tensor_scalar(u1[:, b * 256:(b + 1) * 256], pair[b][:, 1, :], LIMIT, -LIMIT,
                                                ALU.min, ALU.max)
                        if b:
                            lk(ins)
                    pick_expert(e + 1)
                    dve.wait_ge(m_g, n + 1)
                    lk(dve.scalar_tensor_tensor(out=tu, in0=u1, scalar=1.0, in1=g1, op0=ALU.add, op1=ALU.mult))
                    dve.wait_ge(m_sig, n + 1)
                    dve.tensor_tensor(h_s, tu, sg, ALU.mult).then_inc(m_h, 1)
                    for q in range(4):
                        t, h = q // 2, q % 2
                        dve.wait_ge(m_sc, n * 4 + (q + 1))
                        dve.tensor_tensor(x2[:, t, h * 512:h * 512 + 512], bank[2 + q][:, :],
                                          x2[:, t, h * 512:h * 512 + 512], ALU.add).then_inc(m_acc, 1)
                    dve.wait_ge(m_acc, n * 4 + 8)
                    lk(dve.memset(stat[:, 100:101], 0.0))
                    lk(dve.memset(stat[:, 102:103], 0.0))
                    assert lk.n == NB, lk.n
                lk = Chain(dve, s_dvl, base=(c + 1) * (E * NB) + c)
                lk(dve.tensor_scalar(RKs, RKs, -float(CAP), None, ALU.add))
            for q in range(4):
                t, h = q // 2, q % 2
                dve.wait_ge(f_sc, q + 1)
                dve.tensor_tensor(x2[:, t, h * 512:h * 512 + 512], bank[2 + q][:, :],
                                  x2[:, t, h * 512:h * 512 + 512], ALU.add).then_inc(f_sq, 1)
            lf = Chain(dve, s_f)
            dve.wait_ge(f_ms, 2)
            dve.tensor_scalar(stat[:, 82:84], stat[:, 80:82], 1.0 / D, EPS, ALU.mult, ALU.add).then_inc(f_sq, 1)
            dve.wait_ge(f_rt, 1)
            lf(dve.reciprocal(stat[:, 82:84], stat[:, 82:84]))
            dve.wait_ge(s_gfin, 16)
            for t in range(TT):
                dve.scalar_tensor_tensor(out=hn[:, t, :], in0=x2[:, t, :], scalar=stat[:, 82 + t:83 + t],
                                         in1=gfin_s, op0=ALU.mult, op1=ALU.mult).then_inc(f_o, 1)

        @block.tensor
        def _(pe):
            mm = pe.matmul
            pe.wait_ge(s_ohot, 32)
            mm(bank[3][0:NMOBA, 0:512], relb_s[:, 0:NMOBA], ohot_s, start=True, stop=True).then_inc(s_bps, 1)
            pe.wait_ge(s_cst, 16)

            def norm_sum(n):
                pe.wait_ge(s_sq, n + 1)
                if n:
                    pe.wait_ge(s_ms, n)
                for k in range(KT):
                    i = mm(bank[7][:, 0:256], ones, r3(sq, KT)[:, k, :], start=k == 0, stop=k == KT - 1)
                i.then_inc(s_ss, 1)

            def unit_start(u):
                if u >= 3:
                    pe.wait_ge(s_pev, u - 2 + (u - 3 >= 7) + (u - 3 >= 10))

            def channels(out_ap, w, h, last=None):
                for k in range(KT):
                    i = mm(out_ap, w[:, k, :], h[:, k, :], start=k == 0, stop=k == KT - 1)
                return i

            def tokens(ps, col, ncol, w, h, lo):
                for t in range(TT):
                    for k in range(KT):
                        i = mm(ps[:, col + t * ncol:col + (t + 1) * ncol], h[:, k, t * P:(t + 1) * P],
                               w[:, k, lo:lo + ncol], start=k == 0, stop=k == KT - 1)
                return i

            norm_sum(0)
            pe.wait_ge(s_wmem, 16)
            pe.wait_ge(s_h, KT)
            for a in range(2):
                i = channels(bank[0][:, a * 256:(a + 1) * 256], wmem_s[:, :, a * P:(a + 1) * P], hmT)
            i.then_inc(s_proj, 1)
            tokens(bank[1], 0, 256, wmem_s, hmT, 256).then_inc(s_proj, 1)
            norm_sum(1)
            pe.wait_ge(s_h, 2 * KT)
            for g in range(NG):
                u = g + 2
                if g == 2:
                    pe.wait_ge(s_toep, 16)
                    for b in range(3):
                        i = mm(bank[4 + b][:, :], c_(C_ANTI), toep[:, b * 512:(b + 1) * 512], start=True, stop=True)
                    i.then_inc(s_flip, 1)
                unit_start(u)
                pe.wait_ge(s_win[g], 16)
                ps = bank[u % 3]
                if g == 9:
                    i = tokens(ps, 0, 256, win_s[g], hT, 0)
                else:
                    i = channels(ps[:, 0:256], win_s[g][:, :, 0:P], hT)
                    if g == 10:
                        i = tokens(ps, 256, 128, win_s[g], hT, 128)
                    else:
                        i = channels(ps[:, 256:512], win_s[g][:, :, P:2 * P], hT)
                i.then_inc(s_proj, 1)
                if g == 6:
                    pe.wait_ge(s_tanh, 2)
                    pe.wait_ge(s_small, 6 * 16)
                    pe.wait_ge(s_brow, 1)
                    pe.wait_ge(s_flipe, 3)
                    zw = [bank[3][:, 0:256], bank[3][:, 256:512], bank[4][:, 0:256]]
                    za = [bank[5][:, 0:256], bank[5][:, 256:512], bank[6][:, 0:256]]
                    zg = [bank[7][:, 0:256], bank[7][:, 256:512], bank[4][:, 256:512]]
                    for a in range(NCT):
                        cs = slice(a * P, (a + 1) * P)
                        mm(zw[a], lora_s[0:64, cs], mx[0:64, 0, :], start=True, stop=True)
                        mm(za[a], lora_s[64:128, cs], mx[64:128, 0, :], start=True, stop=True)
                        i = mm(zg[a], gup_s[:, cs], mx[:, 1, :], start=True, stop=True)
                    i.then_inc(s_lora, 1)
            pe.wait_ge(s_kksq, 1)
            pe.wait_ge(s_lsig, 6)
            pe.wait_ge(s_lg, 2)
            three = lambda b: [bank[b][:, 0:256], bank[b][:, 256:512], bank[b + 1][:, 0:256]]
            for a in range(NCT):
                i = mm(three(3)[a], blk, tmp[:, a, :], start=True, stop=True)
            i.then_inc(s_kkn, 1)
            pe.wait_ge(s_rkp, 3)
            pe.wait_ge(s_lg, 2)
            for a in range(NCT):
                i = mm(three(5)[a], blk, tmp2[:, a, :], start=True, stop=True)
            i.then_inc(s_rks, 1)
            if part < 2:
                return
            pe.wait_ge(s_pev, 16)
            pe.wait_ge(s_rwp, 1)
            for n in range(4):
                for a in range(NCT):
                    src = (vv[:, a, 0:128], vv[:, a, 128:256], kt[:, a, 0:128], bt[:, a, 0:128])[n]
                    i = pe.transpose(bank[n][:, a * P:(a + 1) * P], src, ident)
                i.then_inc(s_tp, 1)
            for m in range(NM):
                a, c, h = m // 4, m // 2 % 2, m % 2
                b = HD * h
                if m >= 4:
                    pe.wait_ge(s_Ae, m - 3)
                rhs = RA[b:b + HD, a, c, :, :].rearrange("p r n -> p (r n)")
                mm(bank[4 + m % 4][:, 0:256], bt[b:b + HD, a, c * CH:(c + 1) * CH], rhs, start=True, stop=True)
                mm(bank[4 + m % 4][:, 256:512], kt[b:b + HD, a, c * CH:(c + 1) * CH], rhs,
                   start=True, stop=True).then_inc(s_A, 1)
            pe.wait_ge(s_Ae, NM)
            pe.wait_ge(s_C, 1)
            for g in range(NCT):
                for q in range(4):
                    i = pe.transpose(bank[4 + g][:, q * P:(q + 1) * P], Cm[:, 4 * g + q, :], ident)
                i.then_inc(s_T1, 1)
            pe.wait_ge(s_tpe, 4)
            for l in range(2, 8):
                def w_step(g):
                    n = NCT * (l - 2) + g
                    pe.wait_ge(s_TE, n + 1)
                    if n >= 2:
                        pe.wait_ge(s_We, n - 1)
                    for q in range(4):
                        i = mm(bank[n % 2][:, q * P:(q + 1) * P], Cm[:, 4 * g + q, :], Tm[:, 4 * g + q, :],
                               start=True, stop=True)
                    i.then_inc(s_W, 1)

                def y_step(g):
                    n = NCT * (l - 2) + g
                    pe.wait_ge(s_We, n + 1)
                    if l == 2:
                        pe.wait_ge(s_TE, NCT)
                    for q in range(4):
                        m = 4 * g + q
                        if l < 7:
                            mm(bank[2 + 2 * g][:, q * P:(q + 1) * P], Em[:, m, :], Wm[:, m, :], start=True, stop=True)
                        i = mm(bank[3 + 2 * g][:, q * P:(q + 1) * P], Wm[:, m, :], Em[:, m, :], start=True, stop=True)
                    i.then_inc(s_Y, 1)

                pe.wait_ge(s_C, l)
                w_step(0)
                w_step(1)
                y_step(0)
                w_step(2)
                y_step(1)
                y_step(2)
            pe.wait_ge(s_TE, NCT * 7)
            for c in range(2):
                for a in range(NCT):
                    for h in range(2):
                        m, b = a * 4 + c * 2 + h, HD * h
                        o = bank[3 * h][:, a * HD:(a + 1) * HD]
                        if c:
                            mm(o, RA[b:b + HD, a, 1, 0, :], X1[b:b + HD, a, :], start=True, stop=False)
                        i = mm(o, AT[:, m, 256:384], Vn[:, c, a * P + b:a * P + b + HD], start=c == 0, stop=True)
                i.then_inc(s_sol, 1)
                pe.wait_ge(s_sole, 3 * c + 1)
                for a in range(NCT):
                    for h in range(2):
                        m, b = a * 4 + c * 2 + h, HD * h
                        i = mm(bank[1][:, a * P + b:a * P + b + HD], Em[:, m, :], G_s[:, a * P + b:a * P + b + HD],
                               start=True, stop=True)
                i.then_inc(s_sol, 1)
                pe.wait_ge(s_sole, 3 * c + 2)
                if c == 0:
                    for a in range(NCT):
                        cs = slice(a * P, (a + 1) * P)
                        mm(bank[2][:, cs], Bn[:, cs], U_s[:, cs], start=True, stop=False)
                        i = mm(bank[2][:, cs], Kn[:, cs], Vn[:, 0, cs], start=False, stop=True)
                    i.then_inc(s_sol, 1)
                for a in range(NCT):
                    for h in range(2):
                        m, b = a * 4 + c * 2 + h, HD * h
                        o = bank[4 + a // 2][b:b + HD, (a % 2) * 256 + c * CH:(a % 2) * 256 + (c + 1) * CH]
                        vs = slice(a * P + b, a * P + b + HD)
                        mm(o, U_s[:, vs], AT[:, m, 128:256], start=True, stop=False)
                        i = mm(o, Vn[:, c, vs], AT[:, m, 384:512], start=False, stop=c == 0)
                        if c:
                            i = mm(o, X1[b:b + HD, a, :], RA[b:b + HD, a, 1, 1, :], start=False, stop=True)
                i.then_inc(s_ops, 1)
                if c == 0:
                    pe.wait_ge(s_sole, 3)
            pe.wait_ge(s_osb, 1)
            for a in range(NCT):
                i = mm(three(6)[a], c_(C_BLK64), osb[:, a, :], start=True, stop=True)
            i.then_inc(s_gm, 1)
            pe.wait_ge(s_gc, 1)
            for a in range(NCT):
                i = mm(three(6)[a], c_(C_BLK64), tmp[:, a, :], start=True, stop=True)
            i.then_inc(s_gv, 1)
            if part < 3:
                return
            for j in range(NJ):
                q_, k_, b, w0, ot, vals = job(j)
                S = bank[j % 2]
                if j >= 2:
                    pe.wait_ge(s_Ssb, j - 1)
                mm(S[:, 0:w0], q_[:, 0:128], k_[:, 0:w0], start=True, stop=True)
                mm(S[:, w0:w0 + 256], q_[:, 128:256], k_, start=True, stop=True).then_inc(s_S, 1)
                pe.wait_ge(s_Pn, j + 1)
                pr = prob[j % 2]
                pb = bank[2 + j % 2]
                if j >= 2:
                    pe.wait_ge(s_PTe, j - 1)
                pe.transpose(pb[:, 0:128], pr[:, 0:128], ident)
                if w0 == 256:
                    pe.transpose(pb[:, 256:384], pr[:, 128:256], ident)
                pe.transpose(pb[:, 128:256], pr[:, w0:w0 + 128], ident)
                pe.transpose(pb[:, w0 + 128:w0 + 256], pr[:, w0 + 128:w0 + 256], ident).then_inc(s_PT, 1)
                pe.wait_ge(s_PTe, j + 1)
                if j >= 2:
                    pe.wait_ge(s_Oe, j - 1)
                ob = bank[4 + j % 2]
                pt = pT[j % 2]
                lo = 256 - w0
                if lo:
                    mm(ob[b:b + HD, 0:lo], vals(0), pt[:, 0:lo], start=True, stop=True)
                mm(ob[b:b + HD, lo:256], vals(0), pt[:, lo:256], start=True, stop=False)
                mm(ob[b:b + HD, lo:256], vals(1), pt[:, 256:256 + w0], start=False, stop=True).then_inc(s_O, 1)
            if part < 4:
                return
            pe.wait_ge(s_wout, 16)
            pe.wait_ge(s_Oe, NJ)
            pe.wait_ge(s_yr, NCT)
            for n in range(4):
                t, h = n // 2, n % 2
                for k in range(KT):
                    i = mm(bank[n][:, :], yT[:, k, t * P:(t + 1) * P], wout_s[:, k, h * 512:(h + 1) * 512],
                           start=k == 0, stop=k == KT - 1)
                i.then_inc(s_op, 1)
            pe.wait_ge(s_hn, TT)
            for b in range(4):
                for k in range(2):
                    for t in range(TT):
                        i = pe.transpose(bank[4 + b][:, k * 256 + t * P:k * 256 + (t + 1) * P],
                                         hn[:, t, (2 * b + k) * P:(2 * b + k + 1) * P], ident)
                i.then_inc(s_hT2, 1)
            pe.wait_ge(s_hT2e, 4)
            pe.wait_ge(s_x2, 4)
            for t in range(TT):
                o = bank[0][:, t * E:(t + 1) * E]
                for k in range(KT):
                    mm(o, h2T[:, k, t * P:(t + 1) * P], wr_s[:, k * E:(k + 1) * E], start=k == 0, stop=False)
                i = mm(o, c_(C_ONE)[0:1, :], br_s[0:1, :], start=False, stop=True)
            i.then_inc(s_lgp, 1)
            pe.wait_ge(s_mk, 2)
            strict = c_(C_MASK)
            mm(bank[1][:, 0:E], strict, MK[:, 0, :], start=True, stop=True)
            mm(bank[1][:, E:2 * E], strict, MK[:, 1, :], start=True, stop=False)
            mm(bank[1][:, E:2 * E], ones, MK[:, 0, :], start=False, stop=True)
            mm(bank[2][0:1, 0:E], ones[:, 0:1], MK[:, 0, :], start=True, stop=False)
            mm(bank[2][0:1, 0:E], ones[:, 0:1], MK[:, 1, :], start=False, stop=True).then_inc(s_rank, 1)
            pe.wait_ge(s_np, 1)
            for t in range(TT):
                i = pe.transpose(bank[3][0:E, t * P:(t + 1) * P], MW[:, t, :], ident)
            i.then_inc(s_mwt, 1)
            pe.wait_ge(s_mwte, 1)
            for n in range(4):
                t, h = n // 2, n % 2
                mm(bank[2 + n][:, :], MWT[:, t * P:(t + 1) * P], bdn_s[:, h * 512:(h + 1) * 512],
                   start=True, stop=True).then_inc(s_bd, 1)
            if part < 5:
                return

            def gather(n):
                pe.wait_ge(m_sel, n * 2 + 2)
                for t in range(TT):
                    for h in range(2):
                        i = mm(bank[6][h * CAP:(h + 1) * CAP, :], sel[:, t, :], hn[:, t, h * 512:(h + 1) * 512],
                               start=t == 0, stop=t == 1)
                i.then_inc(m_xg, 1)

            def turn(n):
                pe.wait_ge(m_xgs, n + 1)
                for b in range(4):
                    i = pe.transpose(bank[6][:, b * P:(b + 1) * P], xg_s[:, b * P:(b + 1) * P], ident)
                i.then_inc(m_xt, 1)

            def scatter(done):
                for q in range(4):
                    t, h = q // 2, q % 2
                    hs = slice(h * CAP, (h + 1) * CAP)
                    mm(bank[2 + q][:, :], selT[hs, t * P:(t + 1) * P], y_s[hs, :],
                       start=True, stop=True).then_inc(done, 1)

            gather(0)
            turn(0)
            npass = pe.value_load(npass_i[0:1, 0:1], min_val=1, max_val=T // CAP)
            with pe.Fori(0, npass) as c:
                with pe.Fori(0, E) as e:
                    n = c * E + e
                    pe.wait_ge(m_pick, n + 1)
                    pe.wait_ge(m_xts, n + 1)

                    def gate_up(lhs, w, first, last):
                        for b in range(2):
                            for h in range(2):
                                i = mm(bank[b][h * CAP:(h + 1) * CAP, :], lhs,
                                       w[:, h * 1024 + b * 512:h * 1024 + (b + 1) * 512], start=first, stop=last)
                        return i

                    gate_up(pick, bgu_s[:, :], True, False)
                    for k in range(KT):
                        pe.wait_ge(s_slot[k], n * 16 + 16)
                        gate_up(kcol(XTs, k), slot(k), False, k == KT - 1).then_inc(
                            m_gu if k == KT - 1 else m_used, 1)
                    pe.wait_ge(m_ys, n + 1)
                    pe.wait_ge(m_sts, n + 1)
                    pe.wait_ge(m_acc, n * 4 + 4)
                    scatter(m_sc)
                    pe.wait_ge(m_selw, n * 2 + 2)
                    for t in range(TT):
                        i = pe.transpose(bank[7][:, t * P:(t + 1) * P],
                                         selw[:, t, :, :].rearrange("p a s -> p (a s)"), ident)
                    i.then_inc(m_st, 1)
                    gather(n + 1)
                    turn(n + 1)
                    pe.wait_ge(m_sts, n + 2)
                    pe.wait_ge(m_h, n + 1)
                    for b in range(4):
                        i = pe.transpose(bank[7][:, b * P:(b + 1) * P], h_s[:, b * P:(b + 1) * P], ident)
                    i.then_inc(m_ht, 1)
                    pe.wait_ge(m_hts, n + 1)
                    pe.wait_ge(m_acc, n * 4 + 5)
                    for k in range(KT):
                        if k % 2 == 0:
                            pe.wait_ge(s_slot[8 + k // 2], n * 16 + 16)
                        w = r3(slot(8 + k // 2), 2)[:, k % 2, :]
                        for h in range(2):
                            i = mm(bank[2][h * CAP:(h + 1) * CAP, :], kcol(hTs, k), w[:, h * 512:(h + 1) * 512],
                                   start=k == 0, stop=k == KT - 1)
                        if k % 2:
                            i.then_inc(m_y if k == KT - 1 else m_used, 1)
            pe.wait_ge(m_acc, npass * (4 * E) + 4)
            pe.wait_ge(m_ys, npass * E + 1)
            scatter(f_sc)


def _bucket_onehot():
    import math
    import numpy as np
    n = np.maximum(255 - np.arange(256), 0)
    nf = np.maximum(n, 1).astype(np.float32)
    large = 16 + (np.log(nf / np.float32(16)) / np.float32(math.log(8.0)) * np.float32(16)).astype(np.int32)
    b = np.where(n < 16, n, np.minimum(large, 31))
    oh = np.zeros((32, 512), np.float32)
    oh[b, np.arange(256)] = 1.0
    return oh


def _constants():
    import numpy as np
    c = np.zeros((P, C_END), np.float32)
    s, t = np.meshgrid(np.arange(P), np.arange(P), indexing="ij")
    c[:, C_ID:C_ID + P] = s == t
    c[:, C_MASK:C_MASK + P] = s < t
    c[:, C_MASK + P:C_MASK + 2 * P] = s <= t
    for l in range(1, 8):
        b = 2 ** l
        c[:, C_LVL + P * (l - 1):C_LVL + P * l] = (s // b == t // b) & (s % b < b // 2) & (t % b >= b // 2)
    c[:, C_BLK:C_BLK + P] = s // HD == t // HD
    c[:, C_ONE:C_ONE + P] = 1.0
    c[:, C_BLK64:C_BLK64 + P] = (s // HD == t // HD) / HD
    c[:, C_ANTI:C_ANTI + P] = s + t == P - 1
    c[:, C_EHOT:C_EHOT + E + 1] = np.arange(P)[:, None] == np.arange(E + 1)[None, :] % E
    c[:, C_IOTA:C_IOTA + CAP] = np.arange(CAP)
    c[:, C_IOTAE:C_IOTAE + E] = np.arange(E)
    return c


def kernel(**inputs):
    import numpy as np
    import concourse.bacc as bacc
    from concourse import mybir as mb
    from concourse.bass_utils import run_bass_kernel_spmd

    A = {k: np.asarray(v) for k, v in inputs.items()}
    order = [18, 19, 12, 13, 14, 9, 10, 11, 15, 16, 17, 0, 1, 2, 3, 4, 5, 20, 6, 7, 21, 8]
    w = A["w_in"][0].reshape(KT, P, 22, P)[:, :, order, :]
    col = lambda v: v.reshape(-1, P).T
    mu = A["rwkv_mu"][0].reshape(11, P)[[9, 10, 3, 4, 5, 0, 1, 2, 6, 7, 8]].T
    tr = lambda v: v.reshape(T, KT, P).transpose(2, 1, 0)
    arrays = {
        "xT": tr(A["x"][0]), "x": A["x"][0], "memT": tr(A["mem"][0]),
        "win": w.reshape(KT, P, NG, 256).transpose(2, 1, 0, 3),
        "wmem": A["w_mem_kv"][0].reshape(KT, P, 512).transpose(1, 0, 2),
        "wout": A["w_out"][0],
        "params": np.concatenate([col(A["g_mix"][0]), col(A["g_mem"][0]), col(A["g_ffn"][0]), mu] + [
            col(A[n][0]) for n in ("rwkv_w0", "rwkv_a0", "rwkv_k_k", "rwkv_k_a", "rwkv_r_k",
                                   "rwkv_gn_g", "rwkv_gn_b")], axis=1),
        "consts": _constants(),
        "wlora": np.concatenate([A["rwkv_w_up"][0], A["rwkv_a_up"][0]], axis=0),
        "gup": A["rwkv_g_up"][0], "relb": A["rel_bias"], "onehot": _bucket_onehot(),
        "wr": A["w_router"][0].reshape(KT, P, E).transpose(1, 0, 2).reshape(P, KT * E),
        "brouter": A["b_router"],
        "bgu": A["b_gate_up"][0],
        "bdown": A["b_down"][0], "gffn": A["g_ffn"][0], "gfin": A["g_final"],
        "wgu": A["w_gate_up"][0], "wdn": A["w_down"][0],
    }
    arrays = {k: np.ascontiguousarray(v) for k, v in arrays.items()}
    nc = bacc.Bacc("TRN2", target_bir_lowering=False, num_devices=1)
    args = [nc.dram_tensor(k, v.shape, mb.dt.from_np(v.dtype), kind="ExternalInput").ap()
            for k, v in arrays.items()]
    out = nc.dram_tensor("out", (T, D), mb.dt.float32, kind="ExternalOutput").ap()
    layer_kernel(nc, *args, out)
    r = run_bass_kernel_spmd(nc, [arrays], core_ids=[0])
    return r.results[0]["out"].reshape(1, T, D)
```

```python
from contextlib import ExitStack

import concourse.bass as bass
from concourse import mybir

P = 128
T = 256
D = 1024
KT = D // P
TT = T // P
HD = 64
NMOBA, NRWKV, NMEM = 6, 6, 4
NCT = 3
E = 32
TOPK = 4
CAP = 64
CH = 128
NM = NRWKV * T // CH
SLOT = 2048
NSLOT = 12
NG = 11
EPS = 1e-5
GN_EPS = 64e-5
DECAY = 0.6065306597126334
ALPHA, LIMIT = 1.702, 7.0
NEG = -1.0e30
NO_SLOT = 4096.0

F32 = mybir.dt.float32
I32 = mybir.dt.int32
U32 = mybir.dt.uint32
ALU = mybir.AluOpType
ACT = mybir.ActivationFunctionType
AX = mybir.AxisListType.X

P_GMIX, P_GMEM, P_MU, P_W0, P_A0, P_KK, P_KA, P_RK, P_GNG, P_GNB, P_BR, P_END = (
    0, 8, 16, 27, 30, 33, 36, 39, 42, 45, 48, 49)
C_ONE, C_EPS, C_PAR, C_ID, C_MASK, C_LVL, C_BLK, C_BLK64, C_IOTA, C_IOTAE, C_ANTI, C_EHOT, C_STK, C_END = (
    0, 128, 130, 179, 307, 563, 1459, 1587, 1715, 1779, 1811, 1939, 1972, 2004)

UNITS = [0, 1, "mk", "mv"] + list(range(2, NG))


def copies(n):
    return sum(2 if u in (5, 8, 10) else 1 for u in UNITS[2:n])


class Chain:

    def __init__(self, eng, sem, base=None):
        self.eng, self.sem, self.base, self.n = eng, sem, base, 0

    def __call__(self, ins):
        self.n += 1
        ins.then_inc(self.sem, 1)
        self.eng.wait_ge(self.sem, self.n if self.base is None else self.base + self.n)


def layer_kernel(nc, xT, x, memT, win, wmem, wout, consts, wlora, gup, relb, onehot,
                 wr, bgu, bdown, gffn, gfin, wgu, wdn, out):
    ctx = ExitStack()
    with ctx:
        def sb(name, cols, dt=F32, rows=P):
            return ctx.enter_context(nc.sbuf_tensor(name, [rows, cols], dt))

        def sem(name):
            return ctx.enter_context(nc.semaphore(name))

        bank = [ctx.enter_context(nc.psum_tensor(f"bank{i}", [P, 512], F32)) for i in range(8)]
        bias_dram = nc.dram_tensor("bias_rows", [NMOBA, 512], F32).ap()

        ring = sb("ring", NSLOT * SLOT)
        spare = sb("spare", 8192)
        cst = sb("cst", C_END)
        bgu_s = sb("bgu_s", 2 * D, rows=E)
        bdn_s = sb("bdn_s", D, rows=E)
        relb_s = sb("relb_s", 8, rows=E)
        wr_s = sb("wr_s", KT * E)
        xT_s = sb("xT_s", KT * T)
        qm_s = sb("qm_s", 8 * T)
        work = sb("work", 2 * SLOT)
        vn_s, mk_s, mv_s = work[:, 0:768], work[:, 768:1280], work[:, 1280:1792]
        toep = work[:, 1792:3328]
        lora_s, gup_s = work[:, 3328:3712], work[:, 3712:4096]
        raw = sb("raw", 11 * 257)
        mix = sb("mix", 11 * 256)
        stat = sb("stat", 160)
        npass_i = sb("npass_i", 4, I32)

        def slot(k, n=1):
            return ring[:, k * SLOT:(k + n) * SLOT]

        OBANK = (4, 5, 2, 3)
        even = [work[:, 0:SLOT], work[:, SLOT:2 * SLOT],
                spare[:, 2 * SLOT:3 * SLOT], spare[:, 3 * SLOT:4 * SLOT]]

        order = ((4, 5, 6, 7, 0, 1, 2, 3), (0, 1, 2, 3, 4, 5, 6, 7))

        def gu_chunk(k, parity):
            return even[k] if k < 4 and parity == 0 else slot(k)

        def c_(col, n=128):
            return cst[:, col:col + n]

        def pc(col, n=1):
            return cst[:, C_PAR + col:C_PAR + col + n]

        def r3(ap, a):
            return ap.rearrange("p (a n) -> p a n", a=a)

        ident = c_(C_ID)
        ones = c_(C_ONE)
        blk = c_(C_BLK)
        hT = r3(xT_s[:, :], KT)
        wmem_s = r3(spare[:, 0:4096], KT)
        hmT = r3(spare[:, 4096:6144], KT)
        xg = r3(slot(11), KT)
        sq = [r3(qm_s[:, :], KT), r3(spare[:, 6144:8192], KT)]
        rstd = [vn_s[:, 0:256], vn_s[:, 256:512]]
        sums = vn_s[:, 512:768]
        ohot_s = toep[0:E, 512:1024]
        brow_s = toep[0:NMOBA, 0:512]
        win_s = [r3(slot(g), KT) for g in range(NG)]
        wout_s = ring[:, 0:4 * SLOT].rearrange("p (k n) -> p k n", k=KT)
        qk = r3(qm_s[:, 0:6 * T], 6)
        mq = r3(qm_s[:, 6 * T:8 * T], 2)
        vn = r3(vn_s[:, :], TT)
        mk = r3(mk_s[:, :], 2)
        mv = r3(mv_s[:, :], TT)
        toe = r3(toep[:, :], NMOBA)
        rw = r3(raw[:, :], 11)
        mx = r3(mix[:, :], 11)
        W3 = 3 * T
        RA = spare[:, 0:1536].rearrange("p (a c r n) -> p a c r n", a=NCT, c=2, r=2)
        kt = r3(spare[:, 1536:1536 + W3], NCT)
        bt = r3(spare[:, 2304:2304 + W3], NCT)
        sig_a = r3(spare[:, 3072:3072 + W3], NCT)
        gate = r3(spare[:, 3840:3840 + W3], NCT)
        kk_ = r3(spare[:, 4608:4608 + W3], NCT)
        bonus = r3(spare[:, 5376:5376 + W3], NCT)
        tmp = r3(spare[:, 6144:6144 + W3], NCT)
        tmp2 = r3(spare[:, 6912:6912 + W3], NCT)
        sw = r3(raw[:, 0:W3], NCT)
        cum = raw[:, 768:768 + 6 * 129].rearrange("p (a c n) -> p a c n", a=NCT, c=2)
        epos = raw[:, 1542:1542 + 6 * 129].rearrange("p (a c n) -> p a c n", a=NCT, c=2)
        eneg = r3(raw[:, 0:W3], NCT)
        rr = mx[:, 5:8, :]
        vv = mx[:, 8:11, :]
        kv = mx[:, 2:5, :]
        R0 = 6 * SLOT
        AT = ring[:, R0:R0 + 6144].rearrange("p (m n) -> p m n", m=NM)
        Tm = ring[:, R0 + 6144:R0 + 7680].rearrange("p (m n) -> p m n", m=NM)
        Em = ring[:, R0 + 7680:R0 + 9216].rearrange("p (m n) -> p m n", m=NM)
        Wm = ring[:, R0 + 9216:R0 + 10752].rearrange("p (m n) -> p m n", m=NM)
        Cm = [ring[:, o:o + 1536].rearrange("p (m n) -> p m n", m=NM)
              for o in (R0 + 10752, 4 * SLOT + 2048)]
        Vn = xT_s[:, 0:768].rearrange("p (c n) -> p c n", c=2)
        Kn = xT_s[:, 768:1152]
        Bn = xT_s[:, 1152:1536]
        G_s = xT_s[:, 1536:1920]
        U_s = mix[:, 0:384]
        X1 = mix[:, 384:576].rearrange("p (a n) -> p a n", a=NCT)
        osb = r3(spare[:, 0:W3], NCT)
        yT_s = mix[:, 768:2816]
        yT = r3(yT_s, KT)
        prob = [ring[:, 4 * SLOT + 512 * i:4 * SLOT + 512 * i + 512] for i in range(2)]
        pT = [ring[:, 4 * SLOT + 1024 + 512 * i:4 * SLOT + 1536 + 512 * i] for i in range(2)]
        x2 = r3(spare[:, 0:2048], TT)
        hn = r3(spare[:, 2048:4096], TT)
        h2T = yT
        sqx = xT_s[:, 0:1024]
        xn = r3(qm_s[:, :], TT)
        gffn_s = raw[:, 1344:2368]
        gfin_s = mix[:, 0:1024]
        lgT = raw[:, 2368:2624]
        lg = r3(raw[:, 0:64], 2)
        v8 = raw[:, 64:80]
        i8 = raw[:, 80:96].bitcast(U32)
        i8f = raw[:, 96:112]
        e4 = raw[:, 112:120]
        MK = r3(raw[:, 128:192], 2)
        MW = r3(raw[:, 192:256], 2)
        RKs = r3(raw[:, 256:322], 2)
        ttmp = raw[:, 324:356]
        s4 = raw[:, 612:620]
        ctr = raw[:, 620:624]
        sel = raw[:, 640:768].rearrange("p (t s) -> p t s", t=TT)
        selw = raw[:, 768:1024].rearrange("p (t e s) -> p t e s", t=TT, e=2)
        selT = raw[:, 1024:1280]
        pick_d = raw[0:E, 356:420]
        pick = raw[0:E, 1280:1344]
        h_s = raw[:, 1344:1856]
        xg_s = raw[:, 1856:2368]
        XTs = xT_s[:, 0:512]
        hTs = xT_s[:, 512:1024]
        y_s = xT_s[:, 1024:2048]
        g1 = qm_s[:, 0:512]
        u1 = qm_s[:, 512:1024]
        sg = qm_s[:, 1024:1536]
        tu = qm_s[:, 1536:2048]

        def kcol(ap, k):
            return ap[:, (k % 4) * P + (k // 4) * CAP:(k % 4) * P + (k // 4 + 1) * CAP]

        s_mem, s_wmem, s_cst, s_par, s_small = (sem("s_mem"), sem("s_wmem"), sem("s_cst"),
                                                sem("s_par"), sem("s_small"))
        s_sqh = sem("s_sqh")
        s_x = [sem("s_x0"), sem("s_x1")]
        s_win0 = [sem("s_win0a"), sem("s_win0b")]
        s_div = sem("s_div")
        s_xg, s_sqm = sem("s_xg"), sem("s_sqm")
        s_win = [sem(f"s_win{g}") for g in range(NG)]
        s_ohot, s_browd, s_toep, s_flip, s_flipe = (sem("s_ohot"), sem("s_browd"), sem("s_toep"),
                                                    sem("s_flip"), sem("s_flipe"))
        s_wout, s_xn, s_gffn, s_gfin = sem("s_wout"), sem("s_xn"), sem("s_gffn"), sem("s_gfin")
        s_slot = [sem(f"s_slot{k}") for k in range(NSLOT)]
        s_even = [sem(f"s_even{k}") for k in range(4)]
        s_out = sem("s_out")
        s_sq, s_ss, s_rt, s_h = sem("s_sq"), sem("s_ss"), sem("s_rt"), sem("s_h")
        s_bps, s_brow, s_lgT, s_lgTe = sem("s_bps"), sem("s_brow"), sem("s_lgT"), sem("s_lgTe")
        s_proj, s_pev = sem("s_proj"), sem("s_pev")
        s_pad, s_mix, s_tanh, s_lora, s_lsig, s_lg = (sem("s_pad"), sem("s_mix"), sem("s_tanh"),
                                                      sem("s_lora"), sem("s_lsig"), sem("s_lg"))
        s_kksq, s_kkn, s_kkrt = sem("s_kksq"), sem("s_kkn"), sem("s_kkrt")
        s_cum, s_exp = sem("s_cum"), sem("s_exp")
        s_rkp, s_rks, s_rwp, s_Sb, s_Sm, s_E = (sem("s_rkp"), sem("s_rks"), sem("s_rwp"), sem("s_Sb"),
                                                sem("s_Sm"), sem("s_E"))
        s_tp, s_tpe = sem("s_tp"), sem("s_tpe")
        s_A, s_Ae = sem("s_A"), sem("s_Ae")
        s_C, s_T1, s_TE = sem("s_C"), sem("s_T1"), sem("s_TE")
        s_W, s_We, s_Y = sem("s_W"), sem("s_We"), sem("s_Y")
        s_sol, s_sole = sem("s_sol"), sem("s_sole")
        s_ops, s_osb, s_gm, s_gc, s_gv, s_gvm, s_grt, s_yr = (
            sem("s_ops"), sem("s_osb"), sem("s_gm"), sem("s_gc"), sem("s_gv"), sem("s_gvm"),
            sem("s_grt"), sem("s_yr"))
        s_S, s_Ssb, s_Pe, s_Pn, s_PT, s_PTe, s_O, s_Oe = (
            sem("s_S"), sem("s_Ssb"), sem("s_Pe"), sem("s_Pn"), sem("s_PT"), sem("s_PTe"),
            sem("s_O"), sem("s_Oe"))
        s_op, s_x2, s_sqx, s_m2, s_r2, s_hn = (sem("s_op"), sem("s_x2"), sem("s_sqx"), sem("s_m2"),
                                               sem("s_r2"), sem("s_hn"))
        s_hT2, s_hT2e, s_lgp, s_top, s_tope, s_mk, s_rank, s_np = (
            sem("s_hT2"), sem("s_hT2e"), sem("s_lgp"), sem("s_top"), sem("s_tope"), sem("s_mk"),
            sem("s_rank"), sem("s_np"))
        s_v8, s_i8, s_cnt = sem("s_v8"), sem("s_i8"), sem("s_cnt")
        m_used, m_sel, m_xg, m_xgs, m_xt, m_xts, m_pick, m_gu, m_g, m_sig, m_h = (
            sem("m_used"), sem("m_sel"), sem("m_xg"), sem("m_xgs"), sem("m_xt"), sem("m_xts"),
            sem("m_pick"), sem("m_gu"), sem("m_g"), sem("m_sig"), sem("m_h"))
        m_pickd = sem("m_pickd")
        m_selw, m_st, m_sts, m_ht, m_hts, m_y, m_ys, m_sc, m_acc = (
            sem("m_selw"), sem("m_st"), sem("m_sts"), sem("m_ht"), sem("m_hts"), sem("m_y"),
            sem("m_ys"), sem("m_sc"), sem("m_acc"))
        s_dve, s_dvl, s_f = sem("s_dve"), sem("s_dvl"), sem("s_f")
        f_sum = sem("f_sum")
        f_sc, f_sq, f_ms, f_rt, f_o = sem("f_sc"), sem("f_sq"), sem("f_ms"), sem("f_rt"), sem("f_o")

        jobs = [("moba", h) for h in range(NMOBA)] + [("mem", h) for h in range(NMEM)]
        NPAIR = len(jobs) // 2

        def job(j):
            kind, h = jobs[j]
            b = HD * (h % 2)
            if kind == "moba":
                return (qk[b:b + HD, h // 2, :], qk[b:b + HD, 3 + h // 2, :], b, 128,
                        h // 2, lambda m: vn[:, m, h * HD:(h + 1) * HD])
            return (mq[b:b + HD, h // 2, :], mk[b:b + HD, h // 2, :], b, 256,
                    6 + h // 2, lambda m: mv[:, m, h * HD:(h + 1) * HD])

        block = ctx.enter_context(nc.Block())

        @block.sync
        def _(sp):
            sp.dma_start(cst[:, 0:C_ID], consts[:, 0:C_ID]).then_inc(s_par, 16)
            for h in range(2):
                hs = slice(4 * h, 4 * h + 4)
                sp.dma_start(hT[:, hs, :], xT[:, hs, :]).then_inc(s_x[h], 16)
                sp.dma_start(win_s[0][:, hs, :], win[0][:, hs, :]).then_inc(s_win0[h], 16)
            sp.dma_start(hmT, memT).then_inc(s_mem, 16)
            sp.dma_start(win_s[1], win[1]).then_inc(s_win[1], 16)
            sp.dma_start(wmem_s, wmem).then_inc(s_wmem, 16)
            sp.dma_start(cst[:, C_ID:C_END], consts[:, C_ID:C_END]).then_inc(s_cst, 16)
            for g in range(2, NG):
                sp.dma_start(win_s[g], win[g]).then_inc(s_win[g], 16)
            sp.wait_ge(s_brow, 2)
            sp.dma_start(bias_dram, brow_s).then_inc(s_browd, 16)
            sp.wait_ge(s_browd, 16)
            src = bass.AP(tensor=bias_dram.tensor, offset=0,
                          ap=[[1, P], [512, NMOBA], [1, 256]])
            sp.dma_start(toe, src).then_inc(s_toep, 16)
            sp.wait_ge(s_proj, 6)
            sp.dma_start(wout_s, wout.rearrange("(k p) n -> p k n", p=P)).then_inc(s_wout, 16)
            sp.wait_ge(s_Oe, NPAIR)
            sp.dma_start(xn, x.rearrange("(t p) d -> p t d", p=P)).then_inc(s_xn, 16)
            sp.dma_start(gffn_s, gffn.partition_broadcast(P)).then_inc(s_gffn, 16)

            def load(e, k, parity):
                if k < 8:
                    return sp.dma_start(gu_chunk(k, parity), wgu[e, k * P:(k + 1) * P, :]).then_inc(
                        s_even[k] if k < 4 and parity == 0 else s_slot[k], 16)
                return sp.dma_start(r3(slot(k), 2),
                                    wdn[e, (k - 8) * 256:(k - 7) * 256, :].rearrange(
                                        "(c p) n -> p c n", p=P)).then_inc(s_slot[k], 16)
            for k in (0, 1):
                load(0, k, 0)
            sp.wait_ge(s_W, 6 * NCT)
            for k in (4, 5):
                load(0, k, 0)
            sp.wait_ge(s_ops, 2)
            for k in range(6, NSLOT):
                load(0, k, 0)
            sp.wait_ge(s_yr, NCT)
            for k in (2, 3):
                load(0, k, 0)
            sp.wait_ge(s_op, 4)
            for k in range(4):
                load(1, k, 1)
            sp.wait_ge(s_lgT, 1)
            sp.dma_start(gfin_s, gfin.partition_broadcast(P)).then_inc(s_gfin, 16)

            def wait_free(k, n, parity):
                before, par = (n - 2, parity) if k < 4 else (n - 1, 1 - parity)
                if k == 11:
                    sp.wait_ge(m_y, before + 1)
                elif k < 8 and order[par].index(k) == 7:
                    sp.wait_ge(m_gu, before + 1)
                else:
                    done = k if k >= 8 else order[par].index(k) + 1
                    sp.wait_ge(m_used, before * (NSLOT - 2) + done)

            def reload(base, e, parity, chunks):
                for k in chunks:
                    wait_free(k, base + e, parity)
                    load(e, k, parity)

            first, second, down = range(4), range(4, 8), range(8, NSLOT)
            with sp.Fori(0, E // 2 - 2) as i:
                for parity in (1, 0):
                    e = 2 * i + 2 - parity
                    reload(0, e, parity, second)
                    reload(0, e + 1, 1 - parity, first)
                    reload(0, e, parity, down)
            reload(0, E - 3, 1, second)
            reload(0, E - 2, 0, first)
            reload(0, E - 3, 1, down)
            reload(0, E - 2, 0, range(4, NSLOT))
            reload(0, E - 1, 1, range(NSLOT))
            sp.wait_ge(s_np, 1)
            npass = sp.value_load(npass_i[0:1, 0:1], min_val=1, max_val=T // CAP)
            with sp.If(npass > 1):
                with sp.Fori(1, npass) as c:
                    with sp.Fori(0, E // 2) as i:
                        for parity in range(2):
                            reload(c * E, 2 * i + parity, parity, range(NSLOT))
            for t in range(TT):
                sp.wait_ge(f_o, t + 1)
                sp.dma_start(out.rearrange("(t p) d -> p t d", p=P)[:, t, :], hn[:, t, :]).then_inc(s_out, 16)
            sp.wait_ge(s_out, 16 * TT)

        @block.gpsimd
        def _(pool):
            pool.memset(rw[:, :, 0:1], 0.0).then_inc(s_pad, 1)
            for l in range(1, 8):
                mask = c_(C_LVL + 128 * (l - 1)).unsqueeze(1).to_broadcast([P, 4, P])
                for g in range(NCT):
                    m4 = slice(4 * g, 4 * g + 4)
                    if l == 1:
                        pool.wait_ge(s_Ae, 4 * g + 4)
                    elif l == 3:
                        pool.wait_ge(s_TE, g + 1)
                    elif l > 3:
                        pool.wait_ge(s_W, NCT * (l - 4) + g + 1)
                    pool.tensor_tensor(Cm[l % 2][:, m4, :], AT[:, m4, 0:P], mask, ALU.mult).then_inc(s_C, 1)

        @block.scalar
        def _(act):
            act.dma_start(relb_s[:, 0:NMOBA], relb).then_inc(s_ohot, 16)
            act.dma_start(ohot_s, onehot).then_inc(s_ohot, 16)
            act.dma_start(lora_s, wlora).then_inc(s_small, 16)
            act.dma_start(gup_s, gup).then_inc(s_small, 16)
            act.dma_start(wr_s[:, :], wr).then_inc(s_small, 16)
            act.dma_start(bgu_s[:, :], bgu).then_inc(s_small, 16)
            act.dma_start(bdn_s[:, :], bdown).then_inc(s_small, 16)
            act.wait_ge(s_par, 16)
            for k in range(KT):
                if k % 4 == 0:
                    act.wait_ge(s_x[k // 4], 16)
                act.activation(xg[:, k, :], hT[:, k, :], ACT.Copy, scale=pc(P_GMIX + k)).then_inc(s_xg, 1)
            for n in range(2):
                if n:
                    act.wait_ge(s_mem, 16)
                    act.activation(sq[1], hmT, ACT.Square).then_inc(s_sq, 1)
                act.wait_ge(s_ss, n + 1)
                act.activation(rstd[n], bank[7 - n][:, 0:256], ACT.Sqrt, scale=1.0 / D,
                               bias=c_(C_EPS, 1)).then_inc(s_rt, 1)

            def projected(u):
                act.wait_ge(s_proj, u + 1)
                ps = bank[u % 3]
                g = UNITS[u]
                if g == "mk":
                    act.activation(mk_s[:, :], ps[:, :], ACT.Copy).then_inc(s_pev, 1)
                elif g == "mv":
                    act.activation(mv_s[:, :], ps[:, :], ACT.Copy).then_inc(s_pev, 1)
                elif g < 5:
                    act.activation(rw[:, 2 * g:2 * g + 2, 1:257], r3(ps[:, :], 2), ACT.Copy).then_inc(s_pev, 1)
                elif g == 5:
                    act.activation(rw[:, 10, 1:257], ps[:, 0:256], ACT.Copy).then_inc(s_pev, 1)
                    act.activation(qk[:, 0, :], ps[:, 256:512], ACT.Copy).then_inc(s_pev, 1)
                elif g < 8:
                    act.activation(qk[:, 2 * g - 11:2 * g - 9, :], r3(ps[:, :], 2), ACT.Copy).then_inc(s_pev, 1)
                elif g == 8:
                    act.activation(qk[:, 5, :], ps[:, 0:256], ACT.Copy).then_inc(s_pev, 1)
                    act.activation(mq[:, 0, :], ps[:, 256:512], ACT.Copy).then_inc(s_pev, 1)
                elif g == 9:
                    act.activation(vn[:, :, 0:256], r3(ps[:, :], 2), ACT.Copy).then_inc(s_pev, 1)
                else:
                    act.activation(mq[:, 1, :], ps[:, 0:256], ACT.Copy).then_inc(s_pev, 1)
                    act.activation(vn[:, :, 256:384], r3(ps[:, 256:512], 2), ACT.Copy).then_inc(s_pev, 1)

            for u in range(2, 5):
                projected(u)
            act.wait_ge(s_mix, 1)
            act.activation(mx[0:64, 0, :], mx[0:64, 0, :], ACT.Tanh).then_inc(s_tanh, 1)
            act.activation(mx[:, 1, :], mx[:, 1, :], ACT.Sigmoid).then_inc(s_tanh, 1)
            for u in range(5, 8):
                projected(u)
            act.wait_ge(s_lora, 1)
            act.wait_ge(s_mix, 6)
            zw = [bank[3][:, 0:256], bank[3][:, 256:512], bank[4][:, 0:256]]
            za = [bank[5][:, 0:256], bank[5][:, 256:512], bank[6][:, 0:256]]
            for a in range(NCT):
                act.activation(sw[:, a, :], zw[a], ACT.Sigmoid, bias=pc(P_W0 + a)).then_inc(s_lsig, 1)
            for a in range(NCT):
                act.activation(sig_a[:, a, :], za[a], ACT.Sigmoid, bias=pc(P_A0 + a)).then_inc(s_lsig, 1)
            act.activation(gate[:, 0:2, :], r3(bank[7][:, :], 2), ACT.Copy).then_inc(s_lg, 1)
            act.activation(gate[:, 2, :], bank[4][:, 256:512], ACT.Copy).then_inc(s_lg, 1)
            projected(8)
            act.wait_ge(s_kkn, 1)
            act.activation(tmp2[:, 0:2, :], r3(bank[3][:, :], 2), ACT.Sqrt).then_inc(s_kkrt, 1)
            act.activation(tmp2[:, 2, :], bank[4][:, 0:256], ACT.Sqrt).then_inc(s_kkrt, 1)
            projected(9)
            act.wait_ge(s_cum, 1)
            for a in range(NCT):
                for c in range(2):
                    m = 2 * a + c
                    act.activation(epos[:, a, c, :], cum[:, a, c, :], ACT.Exp,
                                   bias=stat[:, m:m + 1], scale=-DECAY).then_inc(s_exp, 1)
                    act.activation(eneg[:, a, c * CH:(c + 1) * CH], cum[:, a, c, 1:129], ACT.Exp,
                                   bias=stat[:, 6 + m:7 + m], scale=DECAY).then_inc(s_exp, 1)
            for u in range(10, 13):
                projected(u)

            def token_major(n, dst):
                act.wait_ge(s_tp, n + 1)
                act.activation(dst, bank[(3, 4, 5, 4)[n]][:, 0:384], ACT.Copy).then_inc(s_tpe, 1)

            for n, dst in enumerate((Vn[:, 0, :], Vn[:, 1, :], Kn, Bn)):
                token_major(n, dst)

            def exponentials(p):
                for i in range(2):
                    j = 2 * p + i
                    w0 = job(j)[3]
                    act.wait_ge(s_Ssb, j + 1)
                    for q, (lo, hi) in enumerate(((0, w0), (w0, w0 + 256))):
                        act.activation(prob[i][:, lo:hi], prob[i][:, lo:hi], ACT.Exp,
                                       bias=stat[:, 32 + 16 * i + q:33 + 16 * i + q],
                                       accum_out=stat[:, 36 + 16 * i + q:37 + 16 * i + q]).then_inc(s_Pe, 1)

            def copy_w(l, g):
                n = NCT * (l - 2) + g
                act.wait_ge(s_W, n + 1)
                act.activation(Wm[:, 4 * g:4 * g + 4, :], r3(bank[n % 2][:, :], 4), ACT.Copy).then_inc(s_We, 1)

            for l in range(2, 8):
                p = l - 2
                copy_w(l, 0)
                copy_w(l, 1)
                if p < NPAIR:
                    exponentials(p)
                    for i in range(2):
                        j = 2 * p + i
                        w = job(j)[3] + 256
                        act.wait_ge(s_PT, j + 1)
                        act.activation(pT[i][:, 0:w], bank[6 + i][:, 0:w], ACT.Copy).then_inc(s_PTe, 1)
                copy_w(l, 2)
                if p < NPAIR:
                    act.wait_ge(s_O, p + 1)
                    act.activation(yT[:, job(2 * p)[4], :], bank[6][:, 0:256], ACT.Copy).then_inc(s_Oe, 1)
            act.wait_ge(s_ops, 2)
            act.activation(osb[:, 0:2, :], r3(bank[7][:, :], 2), ACT.Copy).then_inc(s_osb, 1)
            act.activation(osb[:, 2, :], bank[6][:, 0:256], ACT.Copy).then_inc(s_osb, 1)
            act.wait_ge(s_gc, 1)
            act.activation(tmp, osb, ACT.Square).then_inc(s_gvm, 1)
            act.wait_ge(s_gv, 1)
            act.activation(tmp2[:, 0:2, :], r3(bank[0][:, :], 2), ACT.Sqrt, bias=c_(C_EPS + 1, 1)).then_inc(s_grt, 1)
            act.activation(tmp2[:, 2, :], bank[1][:, 0:256], ACT.Sqrt, bias=c_(C_EPS + 1, 1)).then_inc(s_grt, 1)
            for n in range(4):
                t, h = n // 2, n % 2
                act.wait_ge(s_x2, n + 1)
                act.activation(sqx[:, 0:512] if h else sqx[:, 512:1024], x2[:, t, h * 512:h * 512 + 512], ACT.Square,
                               accum_out=stat[:, 64 + n:65 + n]).then_inc(s_sqx, 1)
                act.wait_ge(s_sqx, n + 1)
            act.wait_ge(s_m2, 1)
            act.activation(stat[:, 68:70], stat[:, 68:70], ACT.Sqrt, scale=1.0 / D, bias=c_(C_EPS, 1)).then_inc(s_r2, 1)
            for b in (1, 3):
                act.wait_ge(s_hT2, b + 1)
                act.activation(h2T[:, 2 * b:2 * b + 2, :], r3(bank[4 + b][:, :], 2), ACT.Copy).then_inc(s_hT2e, 1)
            act.wait_ge(s_lgT, 1)
            act.activation(lgT, bank[4][:, 0:256], ACT.Identity, bias=pc(P_BR)).then_inc(s_lgTe, 1)
            for t in range(TT):
                act.wait_ge(s_top, t + 1)
                act.activation(e4[:, 4 * t:4 * t + 4], v8[:, 8 * t:8 * t + 4], ACT.Exp,
                               bias=s4[:, t:t + 1], accum_out=s4[:, 2 + t:3 + t]).then_inc(s_tope, 1)

            def gathered(n):
                act.wait_ge(m_xg, n + 1)
                act.activation(xg_s, bank[6][:, :], ACT.Copy).then_inc(m_xgs, 1)

            def transposed(n):
                act.wait_ge(m_xt, n + 1)
                act.activation(XTs, bank[6][:, :], ACT.Copy).then_inc(m_xts, 1)

            gathered(0)
            transposed(0)
            act.wait_ge(s_np, 1)
            npass = act.value_load(npass_i[0:1, 0:1], min_val=1, max_val=T // CAP)
            with act.Fori(0, npass) as c:
                with act.Fori(0, E // 2) as i:
                    for parity in range(2):
                        n = c * E + 2 * i + parity
                        act.wait_ge(m_g, n + 1)
                        act.activation(sg, g1, ACT.Sigmoid, scale=ALPHA).then_inc(m_sig, 1)
                        gathered(n + 1)
                        if parity:
                            act.wait_ge(m_st, c * (E // 2) + i + 1)
                            act.activation(selT, bank[7][:, 0:256], ACT.Copy).then_inc(m_sts, 1)
                        transposed(n + 1)
                        act.wait_ge(m_ht, n + 1)
                        act.activation(hTs, bank[7][:, :], ACT.Copy).then_inc(m_hts, 1)
                        act.wait_ge(m_y, n + 1)
                        for h in range(2):
                            act.activation(y_s[parity * CAP:(parity + 1) * CAP, h * 512:(h + 1) * 512],
                                           bank[2][h * CAP:(h + 1) * CAP, :], ACT.Copy).then_inc(m_ys, 1)
            for t in range(TT):
                for h in range(2):
                    q = 2 * t + h
                    act.wait_ge(f_sq, q + 1)
                    act.activation(sqx[:, h * 512:(h + 1) * 512], x2[:, t, h * 512:(h + 1) * 512], ACT.Square,
                                   accum_out=stat[:, 80 + q:81 + q]).then_inc(f_ms, 1)
                    if t:
                        act.wait_ge(f_ms, q - 1)
                act.wait_ge(f_sum, t + 1)
                act.activation(stat[:, 84 + t:85 + t], stat[:, 84 + t:85 + t], ACT.Sqrt, scale=1.0 / D,
                               bias=c_(C_EPS, 1)).then_inc(f_rt, 1)

        @block.vector
        def _(dve):
            link = Chain(dve, s_dve)
            for h in range(2):
                dve.wait_ge(s_x[h], 16)
                hs = slice(4 * h, 4 * h + 4)
                link(dve.tensor_tensor(sq[0][:, hs, :], hT[:, hs, :], hT[:, hs, :], ALU.mult))
            dve.tensor_reduce(sums, sq[0].rearrange("p k t -> p t k"), AX, ALU.add).then_inc(s_sqh, 1)
            dve.wait_ge(s_rt, 1)
            link(dve.reciprocal(rstd[0], rstd[0]))
            dve.wait_ge(s_xg, KT)
            for k in range(KT):
                dve.tensor_tensor(hT[:, k, :], xg[:, k, :], rstd[0], ALU.mult).then_inc(s_h, 1)

            def divided(u):
                dve.wait_ge(s_proj, u + 1)
                dve.tensor_tensor(rw[:, 2 * u:2 * u + 2, 1:257], r3(bank[u][:, :], 2),
                                  rstd[0].unsqueeze(1).to_broadcast([P, 2, T]), ALU.mult).then_inc(s_div, 1)

            dve.wait_ge(s_sq, 1)
            dve.wait_ge(s_ss, 1)
            dve.tensor_reduce(sums, sq[1].rearrange("p k t -> p t k"), AX, ALU.add).then_inc(s_sqm, 1)
            divided(0)
            dve.wait_ge(s_rt, 2)
            link(dve.reciprocal(rstd[1], rstd[1]))
            for k in range(KT):
                dve.scalar_tensor_tensor(out=hmT[:, k, :], in0=hmT[:, k, :], scalar=pc(P_GMEM + k), in1=rstd[1],
                                         op0=ALU.mult, op1=ALU.mult).then_inc(s_h, 1)
            dve.wait_ge(s_bps, 1)
            dve.tensor_copy(brow_s[:, 0:256], bank[3][0:NMOBA, 0:256]).then_inc(s_brow, 1)
            dve.memset(brow_s[:, 256:512], NEG).then_inc(s_brow, 1)
            dve.wait_ge(s_h, 2 * KT)
            dve.wait_ge(s_pad, 1)

            def shift(u):
                lo, hi = 2 * u, min(2 * u + 2, 11)
                if u < 2:
                    dve.wait_ge(s_div, u + 1)
                else:
                    dve.wait_ge(s_pev, copies(UNITS.index(u)) + 1)
                link(dve.tensor_tensor(mx[:, lo:hi, :], rw[:, lo:hi, 0:256], rw[:, lo:hi, 1:257], ALU.subtract))
                for i in range(lo, hi):
                    ins = dve.scalar_tensor_tensor(out=mx[:, i, :], in0=mx[:, i, :], scalar=pc(P_MU + i),
                                                   in1=rw[:, i, 1:257], op0=ALU.mult, op1=ALU.add)
                    if i < hi - 1:
                        link(ins)
                    else:
                        ins.then_inc(s_mix, 1)

            divided(1)
            for u in range(3):
                shift(u)
            dve.wait_ge(s_mix, 3)
            dve.wait_ge(s_proj, UNITS.index("mv") + 1)
            for a in range(NCT):
                link(dve.tensor_scalar(kk_[:, a, :], kv[:, a, :], pc(P_KK + a), None, ALU.mult))
            dve.tensor_tensor(tmp, kk_, kk_, ALU.mult).then_inc(s_kksq, 1)
            for u in range(3, 6):
                shift(u)
            dve.wait_ge(s_mix, 6)
            link(dve.memset(cum[:, :, :, 0:1], 0.0))
            dve.wait_ge(s_lsig, 3)
            for a in range(NCT):
                for c in range(2):
                    link(dve.tensor_tensor_scan(cum[:, a, c, 1:129], c_(C_ONE), sw[:, a, c * CH:(c + 1) * CH],
                                                0.0, ALU.mult, ALU.add))
            cmid = raw[:, 768:768 + 6 * 129].rearrange("p (m n) -> p m n", m=6)[:, :, 64]
            link(dve.tensor_scalar(stat[:, 0:6], cmid, DECAY, None, ALU.mult))
            dve.tensor_scalar(stat[:, 6:12], cmid, -DECAY, None, ALU.mult).then_inc(s_cum, 1)
            dve.wait_ge(s_lsig, 6)
            dve.wait_ge(s_kkn, 1)
            for a in range(NCT):
                link(dve.tensor_scalar(tmp[:, a, :], sig_a[:, a, :], 1.0, pc(P_KA + a), ALU.subtract, ALU.mult))
            link(dve.scalar_tensor_tensor(out=kv, in0=tmp, scalar=1.0, in1=kv, op0=ALU.add, op1=ALU.mult))
            dve.wait_ge(s_kkrt, 2)
            link(dve.tensor_scalar(tmp2, tmp2, 1e-12, None, ALU.max))
            link(dve.reciprocal(tmp2, tmp2))
            link(dve.tensor_tensor(kk_, kk_, tmp2, ALU.mult))
            dve.wait_ge(s_flip, 1)
            for b in range(3):
                dve.tensor_copy(toep[:, b * 512:(b + 1) * 512], bank[5 + b][:, :]).then_inc(s_flipe, 1)
            for a in range(NCT):
                dve.scalar_tensor_tensor(out=tmp2[:, a, :], in0=kv[:, a, :], scalar=pc(P_RK + a), in1=rr[:, a, :],
                                         op0=ALU.mult, op1=ALU.mult).then_inc(s_rkp, 1)
            dve.wait_ge(s_exp, 12)
            link(dve.tensor_tensor(tmp, kk_, sig_a, ALU.mult))
            link(dve.tensor_tensor(bt, tmp, eneg, ALU.mult))
            link(dve.tensor_tensor(kt, kv, eneg, ALU.mult))
            for a in range(NCT):
                link(dve.tensor_tensor(RA[:, a, :, 1, :], r3(rr[:, a, :], 2), epos[:, a, :, 1:129], ALU.mult))
                link(dve.scalar_tensor_tensor(out=RA[:, a, :, 0, :], in0=r3(kk_[:, a, :], 2), scalar=-1.0,
                                              in1=epos[:, a, :, 0:128], op0=ALU.mult, op1=ALU.mult))
            dve.wait_ge(s_rks, 1)
            link(dve.tensor_tensor(bonus[:, 0:2, :], r3(bank[5][:, :], 2), vv[:, 0:2, :], ALU.mult))
            link(dve.tensor_tensor(bonus[:, 2, :], bank[6][:, 0:256], vv[:, 2, :], ALU.mult))
            link(dve.reciprocal(stat[:, 12:15], epos[:, :, 1, 0]))
            dve.tensor_tensor(stat[:, 12:15], stat[:, 12:15], epos[:, :, 0, 128], ALU.mult).then_inc(s_rwp, 1)

            def scores(p):
                for i in range(2):
                    j = 2 * p + i
                    w0 = job(j)[3]
                    w = w0 + 256
                    pr, ps = prob[i], bank[6 + i]
                    mxc = stat[:, 34 + 16 * i:36 + 16 * i]
                    dve.wait_ge(s_S, j + 1)
                    if j < NMOBA:
                        dve.scalar_tensor_tensor(out=pr[:, 0:128], in0=ps[:, 0:128], scalar=HD ** -0.5,
                                                 in1=toe[:, j, 128:256], op0=ALU.mult,
                                                 op1=ALU.add).then_inc(s_Sb, 1)
                        dve.scalar_tensor_tensor(out=pr[:, 128:384], in0=ps[:, 128:384], scalar=HD ** -0.5,
                                                 in1=toe[:, j, :], op0=ALU.mult, op1=ALU.add).then_inc(s_Sb, 1)
                    else:
                        dve.tensor_scalar(pr[:, 0:256], ps[:, 0:256], HD ** -0.5, None, ALU.mult).then_inc(s_Sb, 1)
                        dve.tensor_scalar(pr[:, 256:512], ps[:, 256:512], HD ** -0.5, None, ALU.mult).then_inc(s_Sb, 1)
                    dve.wait_ge(s_Sb, 2 * j + 1)
                    dve.tensor_reduce(mxc[:, 0:1], pr[:, 0:w0], AX, ALU.max).then_inc(s_Sm, 1)
                    dve.wait_ge(s_Sb, 2 * j + 2)
                    dve.tensor_reduce(mxc[:, 1:2], pr[:, w0:w], AX, ALU.max).then_inc(s_Sm, 1)
                    dve.wait_ge(s_Sm, 2 * j + 2)
                    dve.tensor_scalar(stat[:, 32 + 16 * i:34 + 16 * i], mxc, -1.0, None, ALU.mult).then_inc(s_Ssb, 1)

            def normalise(p):
                for i in range(2):
                    j = 2 * p + i
                    w0 = job(j)[3]
                    w = w0 + 256
                    rc = stat[:, 38 + 16 * i:40 + 16 * i]
                    dve.wait_ge(s_Pe, 2 * j + 2)
                    link(dve.reciprocal(rc, stat[:, 36 + 16 * i:38 + 16 * i]))
                    dve.tensor_scalar(prob[i][:, 0:w0], prob[i][:, 0:w0], rc[:, 0:1], None, ALU.mult).then_inc(s_Pn, 1)
                    dve.tensor_scalar(prob[i][:, w0:w], prob[i][:, w0:w], rc[:, 1:2], None, ALU.mult).then_inc(s_Pn, 1)

            dve.wait_ge(s_flipe, 3)
            scores(0)
            for m in range(NM):
                dve.wait_ge(s_A, m + 1)
                dve.tensor_tensor(AT[:, m, :].rearrange("p (a n) -> p a n", a=2),
                                  r3(bank[m % 4][:, :], 2),
                                  c_(C_MASK, 256).unsqueeze(1).to_broadcast([P, 2, 256]), ALU.mult).then_inc(s_Ae, 1)
            idb = ident.unsqueeze(1).to_broadcast([P, 4, P])
            for g in range(NCT):
                m4 = slice(4 * g, 4 * g + 4)
                dve.wait_ge(s_C, g + 1)
                dve.tensor_tensor(Em[:, m4, :], Cm[1][:, m4, :], idb, ALU.add).then_inc(s_E, 1)
                dve.wait_ge(s_T1, g + 1)
                dve.wait_ge(s_E, g + 1)
                dve.tensor_tensor(Tm[:, m4, :], r3(bank[g][:, :], 4), idb, ALU.add).then_inc(s_TE, 1)
            for l in range(2, 8):
                p = l - 2
                if p < NPAIR:
                    normalise(p)
                for g in range(NCT):
                    m4 = slice(4 * g, 4 * g + 4)
                    n = NCT * (l - 2) + g
                    dve.wait_ge(s_Y, n + 1)
                    dve.wait_ge(s_TE, n + 1)
                    y = 2 + 2 * (n % 2)
                    if l < 7:
                        link(dve.tensor_tensor(Tm[:, m4, :], r3(bank[y][:, :], 4), Tm[:, m4, :], ALU.add))
                    dve.tensor_tensor(Em[:, m4, :], r3(bank[y + 1][:, :], 4), Em[:, m4, :], ALU.add).then_inc(s_TE, 1)
                if p + 1 < NPAIR:
                    scores(p + 1)

            def own(bk, w):
                return r3(bank[bk][:, 0:NCT * w], NCT)

            Gv = G_s.rearrange("p (a h n) -> p a h n", a=NCT, h=2)
            Uv = U_s.rearrange("p (a h n) -> p a h n", a=NCT, h=2)
            for c in range(2):
                dve.wait_ge(s_sol, 3 * c + 1)
                for h in range(2):
                    src = own(h, P)[:, :, h * HD:(h + 1) * HD] if c == 0 else own(h, HD)
                    ins = dve.tensor_copy(Gv[:, :, h, :], src)
                    if h:
                        ins.then_inc(s_sole, 1)
                    else:
                        link(ins)
                dve.wait_ge(s_sol, 3 * c + 2)
                if c:
                    dve.wait_ge(s_ops, 1)
                link(dve.tensor_copy(Uv[:, :, 0, :], own(2, P)[:, :, 0:HD]))
                dve.tensor_copy(Uv[:, :, 1, :], own(3, P)[:, :, HD:P]).then_inc(s_sole, 1)
                if c == 0:
                    dve.wait_ge(s_sol, 3)
                    for a in range(NCT):
                        for h in range(2):
                            b = HD * h
                            ins = dve.tensor_scalar(X1[b:b + HD, a, :], bank[0][b:b + HD, a * P + b:a * P + b + HD],
                                                    stat[b:b + HD, 12 + a:13 + a], None, ALU.mult)
                            if a < NCT - 1 or h == 0:
                                link(ins)
                            else:
                                ins.then_inc(s_sole, 1)
            for a in range(NCT):
                link(dve.scalar_tensor_tensor(out=bonus[:, a, :], in0=bonus[:, a, :], scalar=pc(P_GNB + a),
                                              in1=gate[:, a, :], op0=ALU.add, op1=ALU.mult))
                link(dve.tensor_scalar(gate[:, a, :], gate[:, a, :], pc(P_GNG + a), None, ALU.mult))
            dve.wait_ge(s_gm, 1)
            dve.wait_ge(s_osb, 2)
            link(dve.tensor_tensor(osb[:, 0:2, :], osb[:, 0:2, :], r3(bank[0][:, :], 2), ALU.subtract))
            dve.tensor_tensor(osb[:, 2, :], osb[:, 2, :], bank[1][:, 0:256], ALU.subtract).then_inc(s_gc, 1)
            dve.wait_ge(s_grt, 2)
            for a in range(NCT):
                link(dve.reciprocal(tmp2[:, a, :], tmp2[:, a, :]))
                link(dve.tensor_tensor(osb[:, a, :], osb[:, a, :], tmp2[:, a, :], ALU.mult))
                link(dve.tensor_tensor(osb[:, a, :], osb[:, a, :], gate[:, a, :], ALU.mult))
                dve.tensor_tensor(yT[:, 3 + a, :], osb[:, a, :], bonus[:, a, :], ALU.add).then_inc(s_yr, 1)
            def pick_expert(e):
                col = cst[0:E, bass.ds(e + C_EHOT, 1)]
                dve.tensor_copy(pick, col.to_broadcast([E, CAP])).then_inc(m_pick, 1)

            pick_expert(0)
            dve.wait_ge(s_xn, 16)
            for n in range(4):
                t, h = n // 2, n % 2
                dve.wait_ge(s_op, n + 1)
                dve.tensor_tensor(x2[:, t, h * 512:h * 512 + 512], bank[OBANK[n]][:, :], xn[:, t, h * 512:h * 512 + 512],
                                  ALU.add).then_inc(s_x2, 1)
            dve.wait_ge(s_sqx, 4)
            dve.tensor_tensor(stat[:, 68:70], stat[:, 64:68:2], stat[:, 65:68:2], ALU.add).then_inc(s_m2, 1)
            dve.wait_ge(s_r2, 1)
            link(dve.reciprocal(stat[:, 68:70], stat[:, 68:70]))
            dve.wait_ge(s_gffn, 16)
            for n in range(4):
                h, t = n // 2, n % 2
                hs = slice(h * 512, (h + 1) * 512)
                dve.scalar_tensor_tensor(out=hn[:, t, hs], in0=x2[:, t, hs], scalar=stat[:, 68 + t:69 + t],
                                         in1=gffn_s[:, hs], op0=ALU.mult, op1=ALU.mult).then_inc(s_hn, 1)
            for b in (0, 2):
                dve.wait_ge(s_hT2, b + 1)
                dve.tensor_copy(h2T[:, 2 * b:2 * b + 2, :], r3(bank[4 + b][:, :], 2)).then_inc(s_hT2e, 1)
            iota_e = c_(C_IOTAE, E)
            link(dve.memset(MK, 0.0))
            link(dve.memset(MW, 0.0))
            dve.wait_ge(s_lgp, 1)
            link(dve.tensor_copy(lg, r3(bank[5][:, 0:64], 2)))
            both = range(TT)
            for t in both:
                dve.max(v8[:, 8 * t:8 * t + 8], lg[:, t, :]).then_inc(s_v8, 1)
            for t in both:
                dve.wait_ge(s_v8, t + 1)
                dve.tensor_scalar(s4[:, t:t + 1], v8[:, 8 * t:8 * t + 1], -1.0, None, ALU.mult).then_inc(s_top, 1)
                dve.max_index(i8[:, 8 * t:8 * t + 8], v8[:, 8 * t:8 * t + 8], lg[:, t, :]).then_inc(s_i8, 1)
            dve.wait_ge(s_i8, 2)
            link(dve.tensor_copy(i8f, i8))
            for k in range(TOPK):
                if k:
                    dve.wait_ge(s_mk, TT * k)
                for t in both:
                    dve.scalar_tensor_tensor(out=MK[:, t, :], in0=iota_e, scalar=i8f[:, 8 * t + k:8 * t + k + 1],
                                             in1=MK[:, t, :], op0=ALU.is_equal, op1=ALU.add).then_inc(s_mk, 1)
            dve.wait_ge(s_mk, TT * TOPK)
            dve.wait_ge(s_rank, 1)
            link(dve.scalar_tensor_tensor(out=RKs[:, :, 0:E], in0=r3(bank[2][:, 0:64], 2), scalar=NO_SLOT, in1=MK,
                                          op0=ALU.add, op1=ALU.mult))
            link(dve.tensor_scalar(RKs[:, :, 0:E], RKs[:, :, 0:E], -NO_SLOT, None, ALU.add))
            link(dve.tensor_scalar(RKs[:, :, E:E + 1], RKs[:, :, 0:1], -float(CAP), None, ALU.add))
            iota = c_(C_IOTA, CAP)

            def select(e):
                for t in range(TT):
                    ins = dve.tensor_scalar(sel[:, t, :], iota, RKs[:, t, :][:, bass.ds(e, 1)], None, ALU.is_equal)
                    ins.then_inc(m_sel, 1)

            select(0)
            dve.wait_ge(s_cnt, 1)
            link(dve.tensor_reduce(ctr[0:1, 0:1], bank[3][0:1, 0:E], AX, ALU.max))
            link(dve.tensor_scalar(ctr[0:1, 1:2], ctr[0:1, 0:1], CAP + 0.5, 1.0, ALU.is_gt, ALU.add))
            for k in range(2, T // CAP):
                link(dve.scalar_tensor_tensor(out=ctr[0:1, 1:2], in0=ctr[0:1, 0:1], scalar=k * CAP + 0.5,
                                              in1=ctr[0:1, 1:2], op0=ALU.is_gt, op1=ALU.add))
            dve.tensor_copy(npass_i[0:1, 0:1], ctr[0:1, 1:2]).then_inc(s_np, 1)
            dve.wait_ge(s_tope, 2)
            link(dve.reciprocal(s4[:, 2:4], s4[:, 2:4]))
            for t in both:
                link(dve.tensor_scalar(e4[:, 4 * t:4 * t + 4], e4[:, 4 * t:4 * t + 4], s4[:, 2 + t:3 + t], None, ALU.mult))
                for k in range(TOPK):
                    link(dve.tensor_scalar(ttmp, iota_e, i8f[:, 8 * t + k:8 * t + k + 1],
                                           e4[:, 4 * t + k:4 * t + k + 1], ALU.is_equal, ALU.mult))
                    ins = dve.tensor_tensor(MW[:, t, :], MW[:, t, :], ttmp, ALU.add)
                    if k < TOPK - 1 or t == 0:
                        link(ins)
                    else:
                        ins.then_inc(m_acc, 1)
            dve.wait_ge(m_acc, 1)
            dve.memset(y_s, 0.0).then_inc(m_ys, 1)
            dve.memset(selT, 0.0).then_inc(m_sts, 1)
            dve.wait_ge(m_ys, 1)
            dve.wait_ge(m_sts, 1)
            dve.wait_ge(s_np, 1)
            npass = dve.value_load(npass_i[0:1, 0:1], min_val=1, max_val=T // CAP)
            NB = 2
            with dve.Fori(0, npass) as c:
                with dve.Fori(0, E // 2) as i:
                    for parity in range(2):
                        e = 2 * i + parity
                        n = c * E + e
                        lk = Chain(dve, s_dvl, base=n * NB + c)
                        dve.wait_ge(m_xg, n + 1)
                        for t in range(TT):
                            dve.tensor_scalar(selw[:, t, parity, :], iota, RKs[:, t, :][:, bass.ds(e, 1)],
                                              MW[:, t, :][:, bass.ds(e, 1)], ALU.is_equal, ALU.mult).then_inc(m_selw, 1)
                        select(e + 1)
                        dve.wait_ge(m_gu, n + 1)
                        pair = [bank[b][:, :].rearrange("p (f g) -> p g f", g=2) for b in range(2)]
                        for b in range(2):
                            ins = dve.tensor_scalar(g1[:, b * 256:(b + 1) * 256], pair[b][:, 0, :], LIMIT, None, ALU.min)
                            if b:
                                ins.then_inc(m_g, 1)
                        for b in range(2):
                            ins = dve.tensor_scalar(u1[:, b * 256:(b + 1) * 256], pair[b][:, 1, :], LIMIT, -LIMIT,
                                                    ALU.min, ALU.max)
                            if b:
                                lk(ins)
                        pick_expert(e + 1)
                        dve.tensor_copy(pick_d, cst[0:E, bass.ds(e + C_EHOT, 1)].to_broadcast([E, CAP])).then_inc(m_pickd, 1)
                        dve.wait_ge(m_g, n + 1)
                        lk(dve.scalar_tensor_tensor(out=tu, in0=u1, scalar=1.0, in1=g1, op0=ALU.add, op1=ALU.mult))
                        dve.wait_ge(m_sig, n + 1)
                        dve.tensor_tensor(h_s, tu, sg, ALU.mult).then_inc(m_h, 1)
                        if parity == 0:
                            pair_no = c * (E // 2) + i
                            for q in range(4):
                                t, h = q // 2, q % 2
                                dve.wait_ge(m_sc, pair_no * 4 + (q + 1))
                                dve.tensor_tensor(x2[:, t, h * 512:h * 512 + 512], bank[2 + q][:, :],
                                                  x2[:, t, h * 512:h * 512 + 512], ALU.add).then_inc(m_acc, 1)
                            dve.wait_ge(m_acc, pair_no * 4 + 5)
                        assert lk.n == NB, lk.n
                lk = Chain(dve, s_dvl, base=(c + 1) * (E * NB) + c)
                lk(dve.tensor_scalar(RKs, RKs, -float(CAP), None, ALU.add))
            lf = Chain(dve, s_f)

            def join(q):
                t, h = q // 2, q % 2
                dve.wait_ge(f_sc, q + 1)
                dve.tensor_tensor(x2[:, t, h * 512:h * 512 + 512], bank[2 + q][:, :],
                                  x2[:, t, h * 512:h * 512 + 512], ALU.add).then_inc(f_sq, 1)

            def sum_halves(t):
                dve.wait_ge(f_ms, 2 * t + 2)
                dve.tensor_tensor(stat[:, 84 + t:85 + t], stat[:, 80 + 2 * t:81 + 2 * t],
                                  stat[:, 81 + 2 * t:82 + 2 * t], ALU.add).then_inc(f_sum, 1)

            def normalised(t):
                dve.wait_ge(f_rt, t + 1)
                lf(dve.reciprocal(stat[:, 84 + t:85 + t], stat[:, 84 + t:85 + t]))
                dve.scalar_tensor_tensor(out=hn[:, t, :], in0=x2[:, t, :], scalar=stat[:, 84 + t:85 + t],
                                         in1=gfin_s, op0=ALU.mult, op1=ALU.mult).then_inc(f_o, 1)

            dve.wait_ge(s_gfin, 16)
            for q in range(3):
                join(q)
            dve.wait_ge(f_sq, 2)
            sum_halves(0)
            join(3)
            normalised(0)
            dve.wait_ge(f_sq, 4)
            sum_halves(1)
            normalised(1)

        @block.tensor
        def _(pe):
            mm = pe.matmul
            def norm_sum(n, ready):
                pe.wait_ge(ready, 1)
                mm(bank[7 - n][:, 0:256], ones, sums, start=True, stop=True).then_inc(s_ss, 1)

            def unit_start(u):
                if u in (3, 4):
                    pe.wait_ge(s_div, u - 2)
                elif u > 4:
                    pe.wait_ge(s_pev, copies(u - 2))

            def channels(out_ap, w, h, first=False):
                for k in range(KT):
                    if first:
                        pe.wait_ge(s_xg, k + 1)
                        pe.wait_ge(s_win0[k // 4], 16)
                    i = mm(out_ap, w[:, k, :], h[:, k, :], start=k == 0, stop=k == KT - 1)
                return i

            def tokens(ps, col, ncol, w, h, lo):
                for t in range(TT):
                    for k in range(KT):
                        i = mm(ps[:, col + t * ncol:col + (t + 1) * ncol], h[:, k, t * P:(t + 1) * P],
                               w[:, k, lo:lo + ncol], start=k == 0, stop=k == KT - 1)
                return i

            three = lambda b: [bank[b][:, 0:256], bank[b][:, 256:512], bank[b + 1][:, 0:256]]
            for u, g in enumerate(UNITS):
                unit_start(u)
                ps = bank[u % 3]
                if g == "mk":
                    pe.wait_ge(s_wmem, 16)
                    pe.wait_ge(s_h, 2 * KT)
                    for a in range(2):
                        i = channels(ps[:, a * 256:(a + 1) * 256], wmem_s[:, :, a * P:(a + 1) * P], hmT)
                    i.then_inc(s_proj, 1)
                    continue
                if g == "mv":
                    tokens(ps, 0, 256, wmem_s, hmT, 256).then_inc(s_proj, 1)
                    continue
                if g:
                    pe.wait_ge(s_win[g], 16)
                if g == 9:
                    i = tokens(ps, 0, 256, win_s[g], hT, 0)
                else:
                    h_in = xg if g < 2 else hT
                    channels(ps[:, 0:256], win_s[g][:, :, 0:P], h_in, first=g == 0)
                    if g == 0:
                        pe.wait_ge(s_par, 16)
                        norm_sum(0, s_sqh)
                        pe.wait_ge(s_ohot, 32)
                        mm(bank[3][0:NMOBA, 0:512], relb_s[:, 0:NMOBA], ohot_s, start=True, stop=True).then_inc(s_bps, 1)
                    if g == 1:
                        norm_sum(1, s_sqm)
                    if g == 10:
                        i = tokens(ps, 256, 128, win_s[g], hT, 128)
                    else:
                        i = channels(ps[:, 256:512], win_s[g][:, :, P:2 * P], h_in)
                i.then_inc(s_proj, 1)
                if g == 3:
                    pe.wait_ge(s_tanh, 2)
                    pe.wait_ge(s_small, 5 * 16)
                    pe.wait_ge(s_brow, 1)
                    pe.wait_ge(s_rt, 2)
                    zw = [bank[3][:, 0:256], bank[3][:, 256:512], bank[4][:, 0:256]]
                    za = [bank[5][:, 0:256], bank[5][:, 256:512], bank[6][:, 0:256]]
                    zg = [bank[7][:, 0:256], bank[7][:, 256:512], bank[4][:, 256:512]]
                    for a in range(NCT):
                        cs = slice(a * P, (a + 1) * P)
                        mm(zw[a], lora_s[0:64, cs], mx[0:64, 0, :], start=True, stop=True)
                        mm(za[a], lora_s[64:128, cs], mx[64:128, 0, :], start=True, stop=True)
                    for a in range(NCT):
                        i = mm(zg[a], gup_s[:, a * P:(a + 1) * P], mx[:, 1, :], start=True, stop=True)
                    i.then_inc(s_lora, 1)
                if g == 6:
                    pe.wait_ge(s_cst, 16)
                    pe.wait_ge(s_kksq, 1)
                    pe.wait_ge(s_lsig, 6)
                    pe.wait_ge(s_lg, 2)
                    for a in range(NCT):
                        i = mm(three(3)[a], blk, tmp[:, a, :], start=True, stop=True)
                    i.then_inc(s_kkn, 1)
                if g == 7:
                    pe.wait_ge(s_toep, 16)
                    for b in range(3):
                        i = mm(bank[5 + b][:, :], c_(C_ANTI), toep[:, b * 512:(b + 1) * 512], start=True, stop=True)
                    i.then_inc(s_flip, 1)
                if g == 9:
                    pe.wait_ge(s_flipe, 3)
                    pe.wait_ge(s_rkp, 3)
                    for a in range(NCT):
                        i = mm(three(5)[a], blk, tmp2[:, a, :], start=True, stop=True)
                    i.then_inc(s_rks, 1)

            def token_major(n):
                for a in range(NCT):
                    src = (vv[:, a, 0:128], vv[:, a, 128:256], kt[:, a, 0:128], bt[:, a, 0:128])[n]
                    i = pe.transpose(bank[(3, 4, 5, 4)[n]][:, a * P:(a + 1) * P], src, ident)
                i.then_inc(s_tp, 1)

            def attend_scores(p):
                for part_ in range(2):
                    for i in range(2):
                        q_, k_, _, w0 = job(2 * p + i)[0:4]
                        if part_ == 0:
                            mm(bank[6 + i][:, 0:w0], q_[:, 0:128], k_[:, 0:w0], start=True, stop=True)
                        else:
                            mm(bank[6 + i][:, w0:w0 + 256], q_[:, 128:256], k_, start=True, stop=True).then_inc(s_S, 1)

            def attend_transpose(p):
                for i in range(2):
                    w0 = job(2 * p + i)[3]
                    pr, pb = prob[i], bank[6 + i]
                    pe.wait_ge(s_Pn, 4 * p + 2 * i + 2)
                    pe.transpose(pb[:, 0:128], pr[:, 0:128], ident)
                    if w0 == 256:
                        pe.transpose(pb[:, 256:384], pr[:, 128:256], ident)
                    pe.transpose(pb[:, 128:256], pr[:, w0:w0 + 128], ident)
                    pe.transpose(pb[:, w0 + 128:w0 + 256], pr[:, w0 + 128:w0 + 256], ident).then_inc(s_PT, 1)

            def attend_output(p):
                pe.wait_ge(s_PTe, 2 * p + 2)
                heads = [job(2 * p + i) for i in range(2)]
                w0 = heads[0][3]
                lo = 256 - w0
                o = [bank[6][b:b + HD, 0:256] for b in (0, HD)]
                if lo:
                    for i in range(2):
                        mm(o[i][:, 0:lo], heads[i][5](0), pT[i][:, 0:lo], start=True, stop=True)
                for i in range(2):
                    mm(o[i][:, lo:256], heads[i][5](0), pT[i][:, lo:256], start=True, stop=False)
                for i in range(2):
                    r = mm(o[i][:, lo:256], heads[i][5](1), pT[i][:, 256:256 + w0], start=False, stop=True)
                r.then_inc(s_O, 1)

            pe.wait_ge(s_kkrt, 2)
            token_major(0)
            token_major(1)
            pe.wait_ge(s_pev, copies(len(UNITS)))
            pe.wait_ge(s_rwp, 1)
            attend_scores(0)
            token_major(2)
            pe.wait_ge(s_tpe, 2)
            token_major(3)
            for m2 in range(NM // 2):
                a, c = m2 // 2, m2 % 2
                if m2 == 1:
                    pe.wait_ge(s_tpe, 1)
                if m2 >= 2:
                    pe.wait_ge(s_Ae, 2 * m2 - 2)
                for half, z in enumerate((bt, kt)):
                    for h in range(2):
                        b = HD * h
                        rhs = RA[b:b + HD, a, c, :, :].rearrange("p r n -> p (r n)")
                        i = mm(bank[(2 * m2 + h) % 4][:, half * 256:half * 256 + 256],
                               z[b:b + HD, a, c * CH:(c + 1) * CH], rhs, start=True, stop=True)
                        if half:
                            i.then_inc(s_A, 1)
            pe.wait_ge(s_Ae, NM)
            for g in range(NCT):
                pe.wait_ge(s_C, g + 1)
                for q in range(4):
                    i = pe.transpose(bank[g][:, q * P:(q + 1) * P], Cm[1][:, 4 * g + q, :], ident)
                i.then_inc(s_T1, 1)
            pe.wait_ge(s_tpe, 4)

            def w_step(l, g):
                n = NCT * (l - 2) + g
                pe.wait_ge(s_C, NCT * (l - 1) + g + 1)
                pe.wait_ge(s_TE, n + 1)
                if l == 2:
                    pe.wait_ge(s_TE, NCT)
                if n >= 2:
                    pe.wait_ge(s_We, n - 1)
                for q in range(4):
                    i = mm(bank[n % 2][:, q * P:(q + 1) * P], Cm[l % 2][:, 4 * g + q, :], Tm[:, 4 * g + q, :],
                           start=True, stop=True)
                i.then_inc(s_W, 1)

            def y_step(l, g):
                n = NCT * (l - 2) + g
                y = 2 + 2 * (n % 2)
                pe.wait_ge(s_We, n + 1)
                if n >= 2:
                    pe.wait_ge(s_TE, NCT + n - 1)
                for q in range(4):
                    m = 4 * g + q
                    if l < 7:
                        mm(bank[y][:, q * P:(q + 1) * P], Em[:, m, :], Wm[:, m, :], start=True, stop=True)
                    i = mm(bank[y + 1][:, q * P:(q + 1) * P], Wm[:, m, :], Em[:, m, :], start=True, stop=True)
                i.then_inc(s_Y, 1)

            for l in range(2, 8):
                p = l - 2
                w_step(l, 0)
                w_step(l, 1)
                y_step(l, 0)
                if p < NPAIR:
                    attend_transpose(p)
                w_step(l, 2)
                y_step(l, 1)
                if p < NPAIR:
                    attend_output(p)
                y_step(l, 2)
                if p + 1 < NPAIR:
                    pe.wait_ge(s_Oe, p + 1)
                    attend_scores(p + 1)
            pe.wait_ge(s_TE, NCT * 7)
            pe.wait_ge(s_Oe, NPAIR)

            def project_out(n, tiles):
                t, h = n // 2, n % 2
                for k in tiles:
                    i = mm(bank[OBANK[n]][:, :], yT[:, k, t * P:(t + 1) * P], wout_s[:, k, h * 512:(h + 1) * 512],
                           start=k == 0, stop=k == 5)
                return i

            pe.wait_ge(s_wout, 16)

            pairs = [(a, h) for a in range(NCT) for h in range(2)]
            for a, h in pairs:
                i = mm(bank[h][:, a * P:(a + 1) * P], AT[:, a * 4 + h, 256:384], Vn[:, 0, a * P:(a + 1) * P],
                       start=True, stop=True)
            i.then_inc(s_sol, 1)

            def solve(c):
                pe.wait_ge(s_sole, 3 * c + 1)
                for a, h in pairs:
                    i = mm(bank[2 + h][:, a * P:(a + 1) * P], Em[:, a * 4 + c * 2 + h, :], G_s[:, a * P:(a + 1) * P],
                           start=True, stop=True)
                i.then_inc(s_sol, 1)

            def out_part(c, a, h, which):
                m, b = a * 4 + c * 2 + h, HD * h
                o = bank[7 - a // 2][b:b + HD, (a % 2) * 256 + c * CH:(a % 2) * 256 + (c + 1) * CH]
                vs = slice(a * P + b, a * P + b + HD)
                if which == 0:
                    return mm(o, U_s[:, vs], AT[:, m, 128:256], start=False, stop=True)
                if which == 1:
                    return mm(o, Vn[:, c, vs], AT[:, m, 384:512], start=True, stop=False)
                return mm(o, X1[b:b + HD, a, :], RA[b:b + HD, a, 1, 1, :], start=False, stop=False)

            project_out(0, (0,))
            solve(0)
            project_out(0, (1,))
            pe.wait_ge(s_sole, 2)
            for a in range(NCT):
                cs = slice(a * P, (a + 1) * P)
                mm(bank[0][:, cs], Bn[:, cs], U_s[:, cs], start=True, stop=False)
                i = mm(bank[0][:, cs], Kn[:, cs], Vn[:, 0, cs], start=False, stop=True)
            i.then_inc(s_sol, 1)
            for a, h in pairs:
                out_part(0, a, h, 1)
                i = out_part(0, a, h, 0)
            i.then_inc(s_ops, 1)
            project_out(0, (2,))
            pe.wait_ge(s_sole, 3)
            for a, h in pairs:
                b = HD * h
                o = bank[h][:, a * HD:(a + 1) * HD]
                mm(o, AT[:, a * 4 + 2 + h, 256:384], Vn[:, 1, a * P + b:a * P + b + HD], start=True, stop=False)
                i = mm(o, RA[b:b + HD, a, 1, 0, :], X1[b:b + HD, a, :], start=False, stop=True)
            i.then_inc(s_sol, 1)
            project_out(0, (6,))
            solve(1)
            project_out(0, (7,))
            project_out(1, (0,))
            pe.wait_ge(s_sole, 5)
            for a, h in pairs:
                out_part(1, a, h, 1)
                out_part(1, a, h, 2)
                i = out_part(1, a, h, 0)
            i.then_inc(s_ops, 1)

            early = (0, 1, 2, 6, 7)
            project_out(1, (1,))
            pe.wait_ge(s_osb, 2)
            for a in range(NCT):
                i = mm(three(0)[a], c_(C_BLK64), osb[:, a, :], start=True, stop=True)
            i.then_inc(s_gm, 1)
            project_out(1, (2, 6, 7))
            pe.wait_ge(s_gvm, 1)
            for a in range(NCT):
                i = mm(three(0)[a], c_(C_BLK64), tmp[:, a, :], start=True, stop=True)
            i.then_inc(s_gv, 1)
            project_out(2, early)
            project_out(3, early)
            for n in range(4):
                for a in range(NCT):
                    if n == 0:
                        pe.wait_ge(s_yr, a + 1)
                    i = project_out(n, (3 + a,))
                i.then_inc(s_op, 1)
            def gate_up(lhs, w, first, last):
                for b in range(2):
                    for h in range(2):
                        i = mm(bank[b][h * CAP:(h + 1) * CAP, :], lhs,
                               w[:, h * 1024 + b * 512:h * 1024 + (b + 1) * 512], start=first, stop=last)
                return i

            def gate_up_bias(n):
                pe.wait_ge(m_pick, n + 1)
                gate_up(pick, bgu_s[:, :], True, False)

            pe.wait_ge(s_grt, 2)
            gate_up_bias(0)
            for b in range(4):
                if b % 2 == 0:
                    pe.wait_ge(s_hn, b + 2)
                pe.wait_ge(s_x2, 4)
                for k in range(2):
                    for t in range(TT):
                        i = pe.transpose(bank[4 + b][:, k * 256 + t * P:k * 256 + (t + 1) * P],
                                         hn[:, t, (2 * b + k) * P:(2 * b + k + 1) * P], ident)
                i.then_inc(s_hT2, 1)
            pe.wait_ge(s_hT2e, 4)
            for r in range(2):
                for q in range(4):
                    k = 4 * r + q
                    i = mm(bank[4][q * E:(q + 1) * E, 0:256], wr_s[:, k * E:(k + 1) * E], h2T[:, k, :],
                           start=r == 0, stop=r == 1)
            i.then_inc(s_lgT, 1)
            pe.wait_ge(s_lgTe, 1)
            for t in range(TT):
                i = mm(bank[5][:, t * E:(t + 1) * E], lgT[:, t * P:(t + 1) * P], c_(C_STK, E), start=True, stop=True)
            i.then_inc(s_lgp, 1)
            pe.wait_ge(s_mk, TT * TOPK)
            strict = c_(C_MASK)
            mm(bank[2][:, 0:E], strict, MK[:, 0, :], start=True, stop=True)
            mm(bank[2][:, E:2 * E], strict, MK[:, 1, :], start=True, stop=False)
            mm(bank[2][:, E:2 * E], ones, MK[:, 0, :], start=False, stop=True).then_inc(s_rank, 1)
            mm(bank[3][0:1, 0:E], ones[:, 0:1], MK[:, 0, :], start=True, stop=False)
            mm(bank[3][0:1, 0:E], ones[:, 0:1], MK[:, 1, :], start=False, stop=True).then_inc(s_cnt, 1)

            def gather(n):
                pe.wait_ge(m_sel, n * 2 + 2)
                for t in range(TT):
                    for h in range(2):
                        i = mm(bank[6][h * CAP:(h + 1) * CAP, :], sel[:, t, :], hn[:, t, h * 512:(h + 1) * 512],
                               start=t == 0, stop=t == 1)
                i.then_inc(m_xg, 1)

            def turn(n):
                pe.wait_ge(m_xgs, n + 1)
                for b in range(4):
                    i = pe.transpose(bank[6][:, b * P:(b + 1) * P], xg_s[:, b * P:(b + 1) * P], ident)
                i.then_inc(m_xt, 1)

            def scatter(done):
                for q in range(4):
                    t, h = q // 2, q % 2
                    mm(bank[2 + q][:, :], selT[:, t * P:(t + 1) * P], y_s[:, h * 512:(h + 1) * 512],
                       start=True, stop=True).then_inc(done, 1)

            gather(0)
            turn(0)
            pe.wait_ge(s_np, 1)
            npass = pe.value_load(npass_i[0:1, 0:1], min_val=1, max_val=T // CAP)
            def expert(n, pair_no, parity):
                pe.wait_ge(m_xts, n + 1)
                for n_k, k in enumerate(order[parity]):
                    if k < 4:
                        pe.wait_ge((s_slot if parity else s_even)[k], pair_no * 16 + 16)
                    else:
                        pe.wait_ge(s_slot[k], n * 16 + 16)
                    gate_up(kcol(XTs, k), gu_chunk(k, parity), False, n_k == KT - 1).then_inc(
                        m_gu if n_k == KT - 1 else m_used, 1)
                if parity == 0:
                    pe.wait_ge(m_ys, n * 2 + 1)
                    pe.wait_ge(m_sts, pair_no + 1)
                    pe.wait_ge(m_acc, pair_no * 4 + 1)
                    scatter(m_sc)
                else:
                    pe.wait_ge(m_selw, n * 2 + 2)
                    for t in range(TT):
                        i = pe.transpose(bank[7][:, t * P:(t + 1) * P],
                                         selw[:, t, :, :].rearrange("p e s -> p (e s)"), ident)
                    i.then_inc(m_st, 1)
                gather(n + 1)
                turn(n + 1)
                if parity:
                    pe.wait_ge(m_sts, pair_no + 2)
                pe.wait_ge(m_h, n + 1)
                for b in range(4):
                    i = pe.transpose(bank[7][:, b * P:(b + 1) * P], h_s[:, b * P:(b + 1) * P], ident)
                i.then_inc(m_ht, 1)
                pe.wait_ge(m_hts, n + 1)
                if parity == 0:
                    pe.wait_ge(m_acc, pair_no * 4 + 2)
                else:
                    pe.wait_ge(m_ys, n * 2 + 1)
                pe.wait_ge(m_pickd, n + 1)
                for h in range(2):
                    mm(bank[2][h * CAP:(h + 1) * CAP, :], pick_d, bdn_s[:, h * 512:(h + 1) * 512],
                       start=True, stop=False)
                for k in range(KT):
                    if k % 2 == 0:
                        pe.wait_ge(s_slot[8 + k // 2], n * 16 + 16)
                    w = r3(slot(8 + k // 2), 2)[:, k % 2, :]
                    for h in range(2):
                        i = mm(bank[2][h * CAP:(h + 1) * CAP, :], kcol(hTs, k), w[:, h * 512:(h + 1) * 512],
                               start=False, stop=k == KT - 1)
                    if k % 2:
                        i.then_inc(m_y if k == KT - 1 else m_used, 1)
                gate_up_bias(n + 1)

            with pe.Fori(0, npass) as c:
                with pe.Fori(0, E // 2) as i:
                    for parity in range(2):
                        expert(c * E + 2 * i + parity, c * (E // 2) + i, parity)
            pe.wait_ge(m_acc, npass * (2 * E) + 1)
            pe.wait_ge(m_ys, npass * (2 * E) + 1)
            pe.wait_ge(m_sts, npass * (E // 2) + 1)
            scatter(f_sc)


def _bucket_onehot():
    import math
    import numpy as np
    n = np.maximum(255 - np.arange(256), 0)
    nf = np.maximum(n, 1).astype(np.float32)
    large = 16 + (np.log(nf / np.float32(16)) / np.float32(math.log(8.0)) * np.float32(16)).astype(np.int32)
    b = np.where(n < 16, n, np.minimum(large, 31))
    oh = np.zeros((32, 512), np.float32)
    oh[b, np.arange(256)] = 1.0
    return oh


def _constants(parameters):
    import numpy as np
    c = np.zeros((P, C_END), np.float32)
    s, t = np.meshgrid(np.arange(P), np.arange(P), indexing="ij")
    c[:, C_ID:C_ID + P] = s == t
    c[:, C_PAR:C_PAR + P_END] = parameters
    c[:, C_MASK:C_MASK + P] = s < t
    c[:, C_MASK + P:C_MASK + 2 * P] = s <= t
    for l in range(1, 8):
        b = 2 ** l
        c[:, C_LVL + P * (l - 1):C_LVL + P * l] = (s // b == t // b) & (s % b < b // 2) & (t % b >= b // 2)
    c[:, C_BLK:C_BLK + P] = s // HD == t // HD
    c[:, C_ONE:C_ONE + P] = 1.0
    c[:, C_BLK64:C_BLK64 + P] = (s // HD == t // HD) / HD
    c[:, C_ANTI:C_ANTI + P] = s + t == P - 1
    c[:, C_EHOT:C_EHOT + E + 1] = np.arange(P)[:, None] == np.arange(E + 1)[None, :] % E
    c[:, C_EPS], c[:, C_EPS + 1] = EPS, GN_EPS
    c[:, C_STK:C_STK + E] = np.arange(P)[:, None] % E == np.arange(E)[None, :]
    c[:, C_IOTA:C_IOTA + CAP] = np.arange(CAP)
    c[:, C_IOTAE:C_IOTAE + E] = np.arange(E)
    return c


def kernel(**inputs):
    import numpy as np
    import concourse.bacc as bacc
    from concourse import mybir as mb
    from concourse.bass_utils import run_bass_kernel_spmd

    A = {k: np.asarray(v) for k, v in inputs.items()}
    order = [18, 19, 12, 13, 14, 9, 10, 11, 15, 16, 17, 0, 1, 2, 3, 4, 5, 20, 6, 7, 21, 8]
    w = A["w_in"][0].reshape(KT, P, 22, P)[:, :, order, :]
    col = lambda v: v.reshape(-1, P).T
    mu = A["rwkv_mu"][0].reshape(11, P)[[9, 10, 3, 4, 5, 0, 1, 2, 6, 7, 8]].T
    tr = lambda v: v.reshape(T, KT, P).transpose(2, 1, 0)
    arrays = {
        "xT": tr(A["x"][0]), "x": A["x"][0], "memT": tr(A["mem"][0]),
        "win": w.reshape(KT, P, NG, 256).transpose(2, 1, 0, 3),
        "wmem": A["w_mem_kv"][0].reshape(KT, P, 512).transpose(1, 0, 2),
        "wout": A["w_out"][0],
        "consts": _constants(np.concatenate([col(A["g_mix"][0]), col(A["g_mem"][0]), mu] + [
            col(A[n][0]) for n in ("rwkv_w0", "rwkv_a0", "rwkv_k_k", "rwkv_k_a", "rwkv_r_k",
                                   "rwkv_gn_g", "rwkv_gn_b")] + [
            np.concatenate([A["b_router"][0], np.zeros(P - E, np.float32)])[:, None]], axis=1)),
        "wlora": np.concatenate([A["rwkv_w_up"][0], A["rwkv_a_up"][0]], axis=0),
        "gup": A["rwkv_g_up"][0], "relb": A["rel_bias"], "onehot": _bucket_onehot(),
        "wr": A["w_router"][0].reshape(KT, P, E).transpose(1, 0, 2).reshape(P, KT * E),
        "bgu": A["b_gate_up"][0],
        "bdown": A["b_down"][0], "gffn": A["g_ffn"][0], "gfin": A["g_final"],
        "wgu": A["w_gate_up"][0], "wdn": A["w_down"][0],
    }
    arrays = {k: np.ascontiguousarray(v) for k, v in arrays.items()}
    nc = bacc.Bacc("TRN2", target_bir_lowering=False, num_devices=1)
    args = [nc.dram_tensor(k, v.shape, mb.dt.from_np(v.dtype), kind="ExternalInput").ap()
            for k, v in arrays.items()]
    out = nc.dram_tensor("out", (T, D), mb.dt.float32, kind="ExternalOutput").ap()
    layer_kernel(nc, *args, out)
    r = run_bass_kernel_spmd(nc, [arrays], core_ids=[0])
    return r.results[0]["out"].reshape(1, T, D)
```
